# Optimizing a Trainium2 kernel written in Bass

```python
import jax, jax.numpy as jnp
from jax import lax
import numpy as np

D_MODEL = 1024
BATCH = 1
SEQ = 256
DEPTH = 2
DEC_BATCH = 8
DEC_SEQ = 1
PAST_LEN = 2048
PAGE_SIZE = 128

MIX_WIDTH = D_MODEL
CONV_WIDTH = MIX_WIDTH // 2
POOL_WIDTH = MIX_WIDTH - CONV_WIDTH
CONV_HEADS = 8
CONV_K = 3
POOL_WINDOWS = (2, 4, 8, 16)
N_POOL_GROUPS = len(POOL_WINDOWS)
POOL_GROUP = POOL_WIDTH // N_POOL_GROUPS
POOL_HIST = max(POOL_WINDOWS) - 1
IN_COLS = 3 * CONV_WIDTH + POOL_WIDTH
D_FF = ((8 * D_MODEL // 3) + 127) // 128 * 128
N_EXPERTS = 8
TOP_K = 2
D_FF_EXPERT = (7 * D_MODEL) // 2
N_DENSE = (DEPTH + 1) // 2
N_MOE = DEPTH // 2
EPS = 1e-6
ADA_SCALE = 0.5

kernel_name = "hybrid_conv_pool_adaln_moe_decode_step"

def rms_norm(x, g):
    xf = x.astype(jnp.float32)
    y = xf * lax.rsqrt(jnp.mean(xf * xf, axis=-1, keepdims=True) + EPS)
    return (y * g.astype(jnp.float32)).astype(x.dtype)

def swiglu(h, wg, wu, wd):
    a = jnp.einsum('bld,df->blf', h, wg)
    b = jnp.einsum('bld,df->blf', h, wu)
    return jnp.einsum('blf,fd->bld', jax.nn.silu(a) * b, wd)

def short_conv_mixer(b_gate, c_gate, hv, conv_buf, conv_w):
    v = c_gate * hv
    z = jnp.concatenate([conv_buf.astype(v.dtype), v], axis=1)
    y = lax.conv_general_dilated(
        z, conv_w[:, None, :].astype(v.dtype), window_strides=(1,), padding='VALID',
        dimension_numbers=('NWC', 'WIO', 'NWC'), feature_group_count=CONV_WIDTH)
    return b_gate * y, z[:, -(CONV_K - 1):]

def pool_mixer(u, pool_buf, start, pool_w, pool_scale):
    L = u.shape[1]
    z = jnp.concatenate([pool_buf.astype(u.dtype), u], axis=1)
    s = jnp.cumsum(z.astype(jnp.float32), axis=1)
    s = jnp.pad(s, ((0, 0), (1, 0), (0, 0)))
    pos = start + jnp.arange(L, dtype=jnp.int32)
    uf = u.astype(jnp.float32)
    outs = []
    for g, w in enumerate(POOL_WINDOWS):
        sl = slice(g * POOL_GROUP, (g + 1) * POOL_GROUP)
        win = s[:, POOL_HIST + 1:POOL_HIST + 1 + L, sl] - s[:, POOL_HIST + 1 - w:POOL_HIST + 1 - w + L, sl]
        cnt = jnp.minimum(pos + 1, w).astype(jnp.float32)[None, :, None]
        d = (win / cnt - uf[..., sl]).astype(u.dtype)
        outs.append(jnp.einsum('blc,cd->bld', d, pool_w[g]))
    y = jnp.concatenate(outs, axis=-1) * pool_scale
    return y, z[:, -POOL_HIST:]

def moe_swiglu(h, router_w, wg, wu, wd):
    logits = jnp.einsum('bld,de->ble', h, router_w).astype(jnp.float32)
    top_v, top_i = lax.top_k(logits, TOP_K)
    probs = jax.nn.softmax(top_v, axis=-1)
    gates = jnp.sum(probs[..., None] * jax.nn.one_hot(top_i, N_EXPERTS, dtype=jnp.float32), axis=-2)
    gates = gates.astype(h.dtype)
    out = jnp.zeros_like(h)
    for e in range(N_EXPERTS):
        out = out + gates[..., e:e + 1] * swiglu(h, wg[e], wu[e], wd[e])
    return out

def run_trunk(x, c, conv_state, pool_state, start,
              w_ada, b_ada, g_mix, g_ffn, w_in, conv_w, pool_w, pool_scale,
              g_conv_out, g_pool_out, w_out, dense_w_gate, dense_w_up, dense_w_down,
              router_w, moe_w_gate, moe_w_up, moe_w_down, g_final):
    Bn = x.shape[0]
    new_conv, new_pool = [], []
    for i in range(DEPTH):
        if conv_state is None:
            cbuf = jnp.zeros((Bn, CONV_K - 1, CONV_WIDTH), x.dtype)
            pbuf = jnp.zeros((Bn, POOL_HIST, POOL_WIDTH), x.dtype)
        else:
            cbuf, pbuf = conv_state[i], pool_state[i]
        mod = (jax.nn.silu(c) @ w_ada[i] + b_ada[i])[:, None, :]
        sh1, sc1, gt1, sh2, sc2, gt2 = jnp.split(mod, 6, axis=-1)
        h = rms_norm(x, g_mix[i]) * (1 + sc1) + sh1
        p = jnp.einsum('bld,dn->bln', h, w_in[i])
        b_g = p[..., :CONV_WIDTH]
        c_g = p[..., CONV_WIDTH:2 * CONV_WIDTH]
        hv = p[..., 2 * CONV_WIDTH:3 * CONV_WIDTH]
        u = p[..., 3 * CONV_WIDTH:]
        ya, cb_new = short_conv_mixer(b_g, c_g, hv, cbuf, conv_w[i])
        yb, pb_new = pool_mixer(u, pbuf, start, pool_w[i], pool_scale[i])
        m = jnp.concatenate([rms_norm(ya, g_conv_out[i]), rms_norm(yb, g_pool_out[i])], axis=-1)
        x = x + gt1 * jnp.einsum('blm,md->bld', m, w_out[i])
        h = rms_norm(x, g_ffn[i]) * (1 + sc2) + sh2
        j = i // 2
        if i % 2 == 0:
            f = swiglu(h, dense_w_gate[j], dense_w_up[j], dense_w_down[j])
        else:
            f = moe_swiglu(h, router_w[j], moe_w_gate[j], moe_w_up[j], moe_w_down[j])
        x = x + gt2 * f
        new_conv.append(cb_new)
        new_pool.append(pb_new)
    y = rms_norm(x, g_final)
    return y, jnp.stack(new_conv, axis=0), jnp.stack(new_pool, axis=0)

def setup_inputs(seed: int = 0) -> dict:
    key = jax.random.key(seed)
    ks = jax.random.split(key, 28)
    f32 = jnp.float32
    nrm = lambda k, shape, s: jax.random.normal(k, shape, f32) * s
    D = D_MODEL
    return {
        "x_prompt": nrm(ks[0], (BATCH, SEQ, D), 1.0),
        "x_sample": nrm(ks[1], (DEC_BATCH, DEC_SEQ, D), 1.0),
        "c_prompt": nrm(ks[2], (BATCH, D), 1.0),
        "c_sample": nrm(ks[3], (DEC_BATCH, D), 1.0),
        "state_conv": nrm(ks[4], (DEPTH, DEC_BATCH, CONV_K - 1, CONV_WIDTH), 1.0),
        "state_pool": nrm(ks[5], (DEPTH, DEC_BATCH, POOL_HIST, POOL_WIDTH), 1.0),
        "w_ada": nrm(ks[6], (DEPTH, D, 6 * D), ADA_SCALE * D ** -0.5),
        "b_ada": nrm(ks[7], (DEPTH, 6 * D), 0.02),
        "g_mix": 1.0 + nrm(ks[8], (DEPTH, D), 0.05),
        "g_ffn": 1.0 + nrm(ks[9], (DEPTH, D), 0.05),
        "w_in": nrm(ks[10], (DEPTH, D, IN_COLS), D ** -0.5),
        "conv_w": nrm(ks[11], (DEPTH, CONV_K, CONV_WIDTH), CONV_K ** -0.5),
        "pool_w": nrm(ks[12], (DEPTH, N_POOL_GROUPS, POOL_GROUP, POOL_GROUP), POOL_GROUP ** -0.5),
        "pool_scale": 1.0 + nrm(ks[13], (DEPTH, POOL_WIDTH), 0.1),
        "g_conv_out": 1.0 + nrm(ks[14], (DEPTH, CONV_WIDTH), 0.05),
        "g_pool_out": 1.0 + nrm(ks[15], (DEPTH, POOL_WIDTH), 0.05),
        "w_out": nrm(ks[16], (DEPTH, MIX_WIDTH, D), MIX_WIDTH ** -0.5),
        "dense_w_gate": nrm(ks[17], (N_DENSE, D, D_FF), D ** -0.5),
        "dense_w_up": nrm(ks[18], (N_DENSE, D, D_FF), D ** -0.5),
        "dense_w_down": nrm(ks[19], (N_DENSE, D_FF, D), D_FF ** -0.5),
        "router_w": nrm(ks[20], (N_MOE, D, N_EXPERTS), D ** -0.5),
        "moe_w_gate": nrm(ks[21], (N_MOE, N_EXPERTS, D, D_FF_EXPERT), D ** -0.5),
        "moe_w_up": nrm(ks[22], (N_MOE, N_EXPERTS, D, D_FF_EXPERT), D ** -0.5),
        "moe_w_down": nrm(ks[23], (N_MOE, N_EXPERTS, D_FF_EXPERT, D), D_FF_EXPERT ** -0.5),
        "g_final": 1.0 + nrm(ks[24], (D,), 0.05),
    }

def reference(x_prompt, x_sample, c_prompt, c_sample, state_conv, state_pool,
              w_ada, b_ada, g_mix, g_ffn, w_in, conv_w, pool_w, pool_scale,
              g_conv_out, g_pool_out, w_out, dense_w_gate, dense_w_up, dense_w_down,
              router_w, moe_w_gate, moe_w_up, moe_w_down, g_final):
    params = (w_ada, b_ada, g_mix, g_ffn, w_in, conv_w, pool_w, pool_scale,
              g_conv_out, g_pool_out, w_out, dense_w_gate, dense_w_up, dense_w_down,
              router_w, moe_w_gate, moe_w_up, moe_w_down, g_final)
    y_prompt, conv_p, pool_p = run_trunk(x_prompt, c_prompt, None, None, 0, *params)
    y_sample, conv_s, pool_s = run_trunk(x_sample, c_sample, state_conv, state_pool, PAST_LEN, *params)
    return (y_prompt, y_sample, conv_p, pool_p, conv_s, pool_s)


_drawn_inputs = setup_inputs


def setup_inputs(seed=0):
    import zlib

    import numpy as np

    out = dict(_drawn_inputs(seed))
    spreads = {}
    factors = {'g_pool_out': 2.725}
    for name, (base, spread) in spreads.items():
        noise = np.random.default_rng([zlib.crc32(name.encode()), seed]).standard_normal(out[name].shape)
        drawn = base * np.exp(spread * noise) if base else spread * noise
        out[name] = __import__('jax').numpy.asarray(drawn.astype(out[name].dtype))
    for name, factor in factors.items():
        out[name] = (out[name] * factor).astype(out[name].dtype)
    return out
```

```python
from contextlib import ExitStack

import concourse.bass as bass
from concourse import mybir

F32 = mybir.dt.float32
F32R = mybir.dt.float32r
I32 = mybir.dt.int32
ALU = mybir.AluOpType
ACT = mybir.ActivationFunctionType
AX_X = mybir.AxisListType.X

P = 128
EPS = 1e-6
RAW_SLOTS = 6
SPLIT_SLOTS = 3
CHUNK = 2048
BANK = 512
HIST = 15
WINDOWS = (2, 4, 8, 16)
ADA_PARTS = 6
SH1, SC1, GT1, SH2, SC2, GT2 = range(ADA_PARTS)


def hybrid_trunk(nc, a, o):
    depth, d_model, _ = a["w_ada"].shape
    seq = a["x_prompt"].shape[1]
    dec = a["x_sample"].shape[0]
    T = seq + dec
    S = dec + 1
    KC = d_model // P
    GB = a["pool_w"].shape[1]
    d_ff = a["dense_w_gate"].shape[2]
    FC = d_ff // P
    n_exp = a["moe_w_gate"].shape[1]
    d_ffe = a["moe_w_gate"].shape[3]
    GROUPS = d_ffe // BANK
    GC = BANK // P
    TT = -(-T // P)
    LAST = T - (TT - 1) * P
    HALVES = d_model // BANK
    ZU = HIST + seq + dec * (HIST + 1)
    ZV = 2 + seq + dec * 3
    SU = HIST + seq
    SV = 2 + seq
    EXTRA = 4
    assert depth == 2 and GB == 4 and KC == 8 and d_model == 2 * BANK and d_ffe % BANK == 0
    assert (TT - 1) * n_exp >= EXTRA and 2 * T < 5 * (P + 1)

    ADA_CHUNKS = depth * ADA_PARTS * KC // 2
    dense = []

    def cols_256(kind, l, w, rows, j, first=True, last=True, k0=0):
        src = w.rearrange("(k p) n -> p k n", p=P)[:, k0:k0 + rows, 256 * j:256 * j + 256]
        return dict(kind=kind, layer=l, nk=rows, k0=k0, j=j, src=src, first=first, last=last, width=256)

    for l in range(depth):
        dense += [cols_256("in", l, a["w_in"][l], KC, j) for j in range(4 * GB // 2)]
        dense.append(dict(kind="pool", layer=l, nk=GB, k0=0, j=0, first=True, last=True, width=P,
                          src=a["pool_w"][l].rearrange("g c d -> c g d")))
        dense += [cols_256("out", l, a["w_out"][l], KC, j) for j in range(KC // 2)]
        if l % 2 == 0:
            for j in range(FC // 2):
                dense.append(cols_256("gate", l, a["dense_w_gate"][l // 2], KC, j))
                dense.append(cols_256("up", l, a["dense_w_up"][l // 2], KC, j))
            for j in range(KC // 2):
                for k0 in range(0, FC, KC):
                    dense.append(cols_256("down", l, a["dense_w_down"][l // 2], min(KC, FC - k0), j,
                                          k0 == 0, k0 + KC >= FC, k0))
    D0 = ADA_CHUNKS
    M0 = D0 + len(dense)
    PER_EXPERT = 6 * GROUPS
    M1 = M0 + n_exp * PER_EXPERT

    blocks, taken = [], {"act": 0, "dve": 0}
    for i, ch in enumerate(dense):
        ch["n"] = D0 + i
        ch["blocks"] = []
        if ch["kind"] == "down" and not ch["first"]:
            ch["blocks"] = dense[i - 1]["blocks"]
        else:
            for b in range(GB if ch["kind"] == "pool" else 2):
                col = 2 * ch["j"] + b
                eng = "dve"
                if ch["kind"] == "in" and not 2 * GB <= col < 3 * GB or ch["kind"] in ("gate", "pool"):
                    eng = "act"
                taken[eng] += 1
                ch["blocks"].append(len(blocks))
                blocks.append(dict(eng=eng, count=taken[eng], col=col if ch["kind"] != "pool" else b))
    n_norms = 2 * depth + 1

    ctx = ExitStack()
    with ctx:
        def sb(name, shape, dt=F32):
            return ctx.enter_context(nc.sbuf_tensor(name, shape, dt))

        def sem(name):
            return ctx.enter_context(nc.semaphore(name))

        raw = sb("raw", [P, RAW_SLOTS, CHUNK])
        w_hi = sb("w_hi", [P, SPLIT_SLOTS, CHUNK], F32R)
        w_lo = sb("w_lo", [P, SPLIT_SLOTS, CHUNK], F32R)
        xT = sb("xT", [P, KC, T])
        h_hi = sb("h_hi", [P, KC, T], F32R)
        h_lo = sb("h_lo", [P, KC, T], F32R)
        parts = sb("parts", [P, 2 * FC * T], F32R)
        work = sb("work", [P, 8192])
        modT = sb("modT", [P, depth, ADA_PARTS * KC, S])
        par = sb("par", [P, 184])
        ident = sb("ident", [P, P])
        ones = sb("ones", [P, P])
        tri = sb("tri", [P, P])
        slot_no = sb("slot_no", [P, P])
        silu_c = sb("silu_c", [P, KC, 2 * S], F32R)
        last_rows = sb("last_rows", [P, GB, HIST + dec + 2 + 2 * dec])
        ROWS = HIST + dec + 2 + 2 * dec

        hid_hi = parts[:, 0:FC * T].rearrange("p (k t) -> p k t", t=T)
        hid_lo = parts[:, FC * T:2 * FC * T].rearrange("p (k t) -> p k t", t=T)

        at = 0

        def part(n):
            nonlocal at
            at += n
            assert at <= 2 * FC * T
            return parts[:, at - n:at]

        tok_hi = part(TT * d_model).rearrange("p (j d) -> p j d", j=TT)
        tok_lo = part(TT * d_model).rearrange("p (j d) -> p j d", j=TT)
        sel = part(TT * P).rearrange("p (j s) -> p j s", j=TT)
        selT = part(T)
        eh_hi = part(GC * P).rearrange("p (k s) -> p k s", k=GC)
        eh_lo = part(GC * P).rearrange("p (k s) -> p k s", k=GC)
        xs_hi = h_hi[:, :, 0:P]
        xs_lo = h_lo[:, :, 0:P]
        y_hi = h_hi[:, :, P:2 * P]
        y_lo = h_lo[:, :, P:2 * P]

        x_rows = work[:, 0:3 * d_model].rearrange("p (j d) -> p j d", j=3)
        c_rows = work[:, 3 * d_model:4 * d_model]
        par_rows = work[:, 4 * d_model:4 * d_model + 2 * P].rearrange("p (j d) -> p j d", j=2)
        zu = work[:, 0:GB * ZU].rearrange("p (b z) -> p b z", b=GB)
        at_v = GB * ZU
        zv = work[:, at_v:at_v + GB * ZV].rearrange("p (b z) -> p b z", b=GB)
        at_b = at_v + GB * ZV
        b_gate = work[:, at_b:at_b + GB * T].rearrange("p (b t) -> p b t", b=GB)
        at_c = at_b + GB * T
        c_gate = work[:, at_c:at_c + GB * T].rearrange("p (b t) -> p b t", b=GB)
        at_s = at_c + GB * T
        sum_a = work[:, at_s:at_s + GB * ZU].rearrange("p (b z) -> p b z", b=GB)
        at_t = at_s + GB * ZU
        sum_b = work[:, at_t:at_t + 3 * ZU].rearrange("p (b z) -> p b z", b=3)
        at_w = at_t + 3 * ZU
        scr = work[:, at_w:at_w + 2 * (ZV - 2)].rearrange("p (b z) -> p b z", b=2)
        assert at_w + 2 * (ZV - 2) <= 8192
        diff = c_gate
        y_pool = work[:, at_s:at_s + GB * T].rearrange("p (b t) -> p b t", b=GB)
        msq = work[:, at_t:at_t + 2 * T].rearrange("p (b t) -> p b t", b=2)
        pool_rows = work[:, at_s:at_s + BANK]
        conv_rows = work[:, at_t:at_t + BANK]
        new_rows = work[:, at_s + GB * T:at_s + GB * T + BANK]
        sq = work[:, 0:KC * T].rearrange("p (c t) -> p c t", c=KC)
        hn = work[:, KC * T:2 * KC * T].rearrange("p (c t) -> p c t", c=KC)
        rstd = work[:, at_w:at_w + T]
        var = work[:, at_w + T:at_w + 2 * T]
        silu_g = work[:, 0:2 * 2 * T].rearrange("p (b t) -> p b t", b=4)
        hid_f = work[:, 4 * T:4 * T + 2 * T].rearrange("p (b t) -> p b t", b=2)
        acc = work[:, 0:KC * T].rearrange("p (c t) -> p c t", c=KC)
        e_silu = work[:, 2112:2112 + BANK]
        e_hid = work[:, 2624:2624 + BANK]
        y_f = work[:, 3136:3136 + d_model]
        assert KC * T <= 2112
        r0 = 2 * KC * T
        E = n_exp
        logit = work[:, r0:r0 + TT * E].rearrange("p (j e) -> p j e", j=TT)
        r0 += TT * E
        cmp1 = work[:, r0:r0 + TT * E * E].rearrange("p (j e f) -> p j e f", j=TT, e=E)
        r0 += TT * E * E
        cmp2 = work[:, r0:r0 + TT * E * E].rearrange("p (j e f) -> p j e f", j=TT, e=E)
        r0 += TT * E * E
        rank = work[:, r0:r0 + TT * E].rearrange("p (j e) -> p j e", j=TT)
        r0 += TT * E
        chosen = work[:, r0:r0 + TT * E].rearrange("p (j e) -> p j e", j=TT)
        r0 += TT * E
        lmax = work[:, r0:r0 + TT]
        lsum = work[:, r0 + TT:r0 + 2 * TT]
        r0 += 2 * TT
        earlier = work[:, r0:r0 + E * E].rearrange("p (e f) -> p e f", e=E)
        r0 += E * E
        real = work[:, r0:r0 + TT]
        r0 += TT
        gate = work[:, r0:r0 + E * TT].rearrange("p (e j) -> p e j", e=E)
        r0 += TT * E
        place = work[:, r0:r0 + E * TT].rearrange("p (e j) -> p e j", e=E)
        r0 += TT * E
        place_e = work[:, r0:r0 + TT]
        gate_e = work[:, r0 + TT:r0 + 2 * TT]
        gate_slot = work[:, r0 + 2 * TT:r0 + 2 * TT + 1]
        r0 += 2 * TT + 1
        NX = (TT - 1) * E
        more = work[:, r0:r0 + NX].rearrange("p (j e) -> p j e", e=E)
        more_row = work[:, r0:r0 + NX]
        more_no = work[:, r0 + NX:r0 + 2 * NX]
        tmp_row = work[:, r0 + 2 * NX:r0 + 3 * NX]
        code_e = work[:, r0 + 3 * NX:r0 + 4 * NX]
        code_s = work[:, r0 + 4 * NX:r0 + 5 * NX]
        r0 += 5 * NX
        hit = work[:, r0:r0 + EXTRA * NX].rearrange("p (i k) -> p i k", i=EXTRA)
        hit2 = work[:, r0 + EXTRA * NX:r0 + 2 * EXTRA * NX].rearrange("p (i k) -> p i k", i=EXTRA)
        r0 += 2 * EXTRA * NX
        extra_shift = work[:, r0:r0 + EXTRA]
        extra_f = work[:, r0 + EXTRA:r0 + 2 * EXTRA + 1]
        r0 += 2 * EXTRA + 1
        assert r0 <= at_w, (r0, at_w)
        fix = sb("fix", [P, GB, HIST + 1])
        extra_i = sb("extra_i", [P, EXTRA + 1], I32)
        iota_i = work[:, 4 * d_model + 2 * P:4 * d_model + 3 * P].bitcast(I32)
        router = sb("router", [P, KC, E])
        y_rows = work[:, 2 * KC * T:2 * KC * T + TT * d_model].rearrange("p (j d) -> p j d", j=TT)

        ps = ctx.enter_context(nc.psum_tensor("ps", [P, 8, BANK], F32))

        G_MIX, G_FFN, G_FIN, CONV, PSC, GCO, GPO, BADA = 96, 112, 128, 136, 160, 168, 176, 0

        def pcol(i, n=1):
            return par[:, i:i + n]

        raw_in = [sem(f"raw_in{i}") for i in range(RAW_SLOTS)]
        hi_done = sem("hi_done")
        lo_done = sem("lo_done")
        used = sem("used")
        rows_in = sem("rows_in")
        states_in = [sem(f"states_in{l}") for l in range(depth)]
        router_in = sem("router_in")
        consts = sem("consts")
        pool_step = sem("pool_step")
        dve_step = sem("dve_step")
        act_step = sem("act_step")
        c_silu = sem("c_silu")
        turned = sem("turned")
        c_split = sem("c_split")
        par_done = sem("par_done")
        x_done = sem("x_done")
        turned_out = sem("turned_out")
        ada_out = sem("ada_out")
        squares = sem("squares")
        sums = sem("sums")
        inv_var = sem("inv_var")
        rstd_done = sem("rstd_done")
        normed = sem("normed")
        h_hi_done = sem("h_hi_done")
        h_lo_done = sem("h_lo_done")
        act_took = sem("act_took")
        dve_took = sem("dve_took")
        ffn_hi = sem("ffn_hi")
        ffn_lo = sem("ffn_lo")
        state_turned = sem("state_turned")
        state_put = sem("state_put")
        diff_done = sem("diff_done")
        diff_hi = sem("diff_hi")
        diff_lo = sem("diff_lo")
        mix_y = sem("mix_y")
        mix_sq = sem("mix_sq")
        mix_inv = sem("mix_inv")
        mix_rstd = sem("mix_rstd")
        m_f = sem("m_f")
        m_hi = sem("m_hi")
        m_lo = sem("m_lo")
        tails = sem("tails")
        tails_turned = sem("tails_turned")
        tails_out = sem("tails_out")
        out_dma = sem("out_dma")
        shift_dma = sem("shift_dma")
        sq_used = sem("sq_used")
        logits_ps = sem("logits_ps")
        chosen_done = sem("chosen_done")
        cum_ps = sem("cum_ps")
        route_exp = sem("route_exp")
        route_max = sem("route_max")
        extra_done = sem("extra_done")
        tok_turned = sem("tok_turned")
        tok_copied = sem("tok_copied")
        tok_zero = sem("tok_zero")
        acc_zero = sem("acc_zero")
        sel_made = sem("sel_made")
        place_made = sem("place_made")
        gather_ps = sem("gather_ps")
        gathered = sem("gathered")
        e_silu_done = sem("e_silu_done")
        e_hid_done = sem("e_hid_done")
        e_turned = sem("e_turned")
        e_hi_done = sem("e_hi_done")
        e_lo_done = sem("e_lo_done")
        y_scaled = sem("y_scaled")
        y_hi_done = sem("y_hi_done")
        y_lo_done = sem("y_lo_done")
        selT_ps = sem("selT_ps")
        selT_done = sem("selT_done")
        comb_ps = sem("comb_ps")
        combined = sem("combined")
        fin_f = sem("fin_f")
        fin_ps = sem("fin_ps")
        fin_out = sem("fin_out")
        y_dma = sem("y_dma")

        block = ctx.enter_context(nc.Block())

        def rs(n):
            return n % RAW_SLOTS

        def ss(n):
            return n % SPLIT_SLOTS

        def dense_end(kind, l):
            return max(ch["n"] for ch in dense if ch["kind"] == kind and ch["layer"] == l)

        def count_of(kind, l, col):
            return next(blocks[b]["count"] for ch in dense if ch["kind"] == kind and ch["layer"] == l
                        for b in ch["blocks"] if blocks[b]["col"] == col)

        def misc_plan():
            return {("hid", GROUPS - 1): 6, ("hid", 0): 7, "comb": (6, 7), "selT": 6,
                    **{("hid", g): 7 if g % 2 else 6 for g in range(1, GROUPS - 1)}}

        def group_end(e, g, first):
            return (M0 + 3 if first and g == 0 else M0 - 2 + PER_EXPERT * e + 6 * g + 3) + 1

        def expert_end(e):
            return M0 - 2 + PER_EXPERT * (e + 1) + 6

        def expert_chunks(first):
            for pos in range(PER_EXPERT):
                g, q = divmod(pos, 6)
                if q >= 4 and g == 0 and first:
                    continue
                yield pos, ("gu" if q < 4 else "down"), g

        def chunk_no(e, pos, first):
            if first and pos < 4:
                return M0 + pos
            return M0 - 2 + PER_EXPERT * e + pos

        def slot_of(pos, first):
            return (M0 + pos) % 6 if first and pos < 4 else (M0 - 2 + pos) % 6

        NORM_H = 2

        @block.sync
        def _(sp):
            def load(n, slot, dst, src, free=True):
                if free:
                    sp.wait_ge(lo_done, n - RAW_SLOTS + 1)
                sp.dma_start(dst, src).then_inc(raw_in[slot], 16)

            ada = a["w_ada"].rearrange("l (k p) n -> l p k n", p=P)
            per_layer = ADA_CHUNKS // depth
            for n in range(RAW_SLOTS):
                load(n, n, raw[:, n, :].rearrange("p (k m) -> p k m", k=KC),
                     ada[0, :, :, 256 * n:256 * n + 256], free=False)
            for l in range(depth):
                lo = 1 if l == 0 else 0
                with sp.Fori(lo, per_layer // RAW_SLOTS) as i:
                    for j in range(RAW_SLOTS):
                        load(per_layer * l + RAW_SLOTS * i + j, j,
                             raw[:, j, :].rearrange("p (k m) -> p k m", k=KC),
                             ada[l, :, :, bass.ds(RAW_SLOTS * 256 * i + 256 * j, 256)])
            for ch in dense:
                n, w = ch["n"], ch["width"]
                load(n, rs(n), raw[:, rs(n), 0:ch["nk"] * w].rearrange("p (k m) -> p k m", m=w), ch["src"])

            wg = a["moe_w_gate"][0].rearrange("e (k p) n -> e p k n", p=P)
            wu = a["moe_w_up"][0].rearrange("e (k p) n -> e p k n", p=P)
            wd = a["moe_w_down"][0].rearrange("e (k p) n -> e p k n", p=P)

            def gate_up(n, slot, e, g, q):
                w = (wg if q < 2 else wu)[e, :, 4 * (q % 2):4 * (q % 2) + 4, BANK * g:BANK * (g + 1)]
                load(n, slot, raw[:, slot, :].rearrange("p (k m) -> p k m", k=4), w)

            def down(n, slot, e, g, q):
                w = wd[e, :, GC * g + 2 * q:GC * g + 2 * q + 2, :]
                load(n, slot, raw[:, slot, :].rearrange("p (k m) -> p k m", k=2), w)

            def expert(e, first):
                for pos, kind, g in expert_chunks(first):
                    n, s, q = chunk_no(e, pos, first), slot_of(pos, first), pos % 6
                    if kind == "gu":
                        gate_up(n, s, e, g, q)
                    elif g == 0:
                        down(n, s, e - 1, GROUPS - 1, q - 4)
                    else:
                        down(n, s, e, g - 1, q - 4)

            expert(0, True)
            with sp.Fori(1, n_exp) as e:
                expert(e, False)
            for q in range(2):
                down(M1 - 2 + q, (M1 - 2 + q) % 6, n_exp - 1, GROUPS - 1, q)

            sp.wait_ge(extra_done, 1)
            many = sp.value_load(extra_i[0:1, EXTRA:EXTRA + 1], min_val=0, max_val=EXTRA)
            with sp.If(many > 0):
                with sp.Fori(0, many) as i:
                    e = sp.value_load(extra_i[0:1, bass.ds(i, 1)], min_val=0, max_val=n_exp - 1)
                    for pos in range(PER_EXPERT):
                        g, q = divmod(pos, 6)
                        n, s = M1 + PER_EXPERT * i + pos, (M1 + pos) % 6
                        if q < 4:
                            gate_up(n, s, e, g, q)
                        else:
                            down(n, s, e, g, q - 4)

        @block.gpsimd
        def _(pool):
            steps = [0]

            def link(ins):
                steps[0] += 1
                ins.then_inc(pool_step, 1)
                pool.wait_ge(pool_step, steps[0])

            link(pool.memset(ident[:, :], 0.0))
            link(pool.affine_select(out=ident[:, :], in_=ident[:, :], compare_op=ALU.not_equal, fill=1.0, base=0,
                                    pattern=[[-1, P]], channel_multiplier=1))
            pool.memset(ones[:, :], 1.0).then_inc(consts, 1)
            link(pool.memset(tri[:, :], 0.0))
            link(pool.affine_select(out=tri[:, :], in_=tri[:, :], compare_op=ALU.is_ge, fill=1.0, base=0,
                                    pattern=[[-1, P]], channel_multiplier=1))
            link(pool.iota(iota_i, pattern=[[1, P]], base=0, channel_multiplier=0))
            link(pool.tensor_copy(slot_no[:, :], iota_i))
            for g, w in enumerate(WINDOWS):
                link(pool.tensor_scalar(fix[:, g, :], slot_no[:, 0:HIST + 1], 1.0, float(w), ALU.add, ALU.min))
            pool.engine_nop().then_inc(consts, 1)
            pool.dma_start(router[:, :, :], a["router_w"][0].rearrange("(k p) e -> p k e", p=P)).then_inc(router_in, 16)

            for l in range(depth):
                pool.dma_start(o["pool_sample"][l, :, 0:HIST - 1, :], a["state_pool"][l, :, 1:HIST, :])\
                    .then_inc(shift_dma, 16)
            for l in range(depth):
                pool.wait_ge(act_took, count_of("in", l, 4 * GB - 1))
                pool.wait_ge(dve_took, count_of("in", l, 3 * GB - 1))
                pool.wait_ge(state_put, 2 * (l + 1))
                if l:
                    pool.wait_ge(tails_turned, l)
                pool.tensor_copy(last_rows[:, :, 0:HIST], zu[:, :, seq:seq + HIST]).then_inc(tails, 1)
                us = zu[:, :, SU:].rearrange("p b (s r) -> p b s r", r=HIST + 1)
                pool.tensor_copy(last_rows[:, :, HIST:HIST + dec], us[:, :, :, HIST]).then_inc(tails, 1)
                o1 = HIST + dec
                pool.tensor_copy(last_rows[:, :, o1:o1 + 2], zv[:, :, seq:seq + 2]).then_inc(tails, 1)
                vs = zv[:, :, SV:].rearrange("p b (s r) -> p b s r", r=3)
                pool.tensor_copy(last_rows[:, :, o1 + 2:o1 + 2 + 2 * dec].rearrange("p b (s r) -> p b s r", r=2),
                                 vs[:, :, :, 1:3]).then_inc(tails, 1)

            pool.wait_ge(h_lo_done, NORM_H * 4)
            link(pool.memset(earlier, 0.0))
            link(pool.affine_select(out=earlier, in_=earlier, compare_op=ALU.is_ge, fill=1.0, base=0,
                                    pattern=[[-1, E], [1, E]], channel_multiplier=0))
            link(pool.memset(real, 1.0))
            link(pool.affine_select(out=real[:, TT - 1:TT], in_=real[:, TT - 1:TT], compare_op=ALU.is_gt, fill=0.0,
                                    base=LAST, pattern=[[0, 1]], channel_multiplier=-1))
            link(pool.memset(logit, 0.0))
            link(pool.memset(tok_hi[:, TT - 1, :].bitcast(F32), 0.0))
            link(pool.memset(tok_lo[:, TT - 1, :].bitcast(F32), 0.0))
            pool.iota(code_e.bitcast(I32).rearrange("p (j e) -> p j e", e=E), pattern=[[0, TT - 1], [1, E]], base=0,
                      channel_multiplier=0).then_inc(pool_step, 1)
            pool.iota(code_s.bitcast(I32).rearrange("p (j e) -> p j e", e=E), pattern=[[P, TT - 1], [0, E]], base=P,
                      channel_multiplier=0).then_inc(pool_step, 1)
            steps[0] += 2
            pool.wait_ge(pool_step, steps[0])
            link(pool.tensor_copy(tmp_row, code_e.bitcast(I32)))
            link(pool.tensor_copy(code_e, tmp_row))
            link(pool.tensor_copy(tmp_row, code_s.bitcast(I32)))
            link(pool.tensor_copy(code_s, tmp_row))
            pool.memset(acc, 0.0).then_inc(tok_zero, 1)
            pool.wait_ge(shift_dma, 16 * depth)

        @block.scalar
        def _(act):
            steps = [0]

            def link(ins):
                steps[0] += 1
                ins.then_inc(act_step, 1)
                act.wait_ge(act_step, steps[0])

            act.dma_start(c_rows[0:1, :], a["c_prompt"]).then_inc(rows_in, 16)
            act.dma_start(c_rows[1:S, :], a["c_sample"]).then_inc(rows_in, 16)
            act.dma_start(par_rows[0:depth * ADA_PARTS * KC, 0, :],
                          a["b_ada"].rearrange("l (j p) -> (l j) p", p=P)).then_inc(rows_in, 16)
            small = [("g_mix", "l (j p) -> (l j) p"), ("g_ffn", "l (j p) -> (l j) p"), ("g_final", "(j p) -> j p"),
                     ("conv_w", "l k (j p) -> (l k j) p"), ("pool_scale", "l (j p) -> (l j) p"),
                     ("g_conv_out", "l (j p) -> (l j) p"), ("g_pool_out", "l (j p) -> (l j) p")]
            r = 0
            for name, pattern in small:
                v = a[name].rearrange(pattern, p=P)
                act.dma_start(par_rows[r:r + v.shape[0], 1, :], v).then_inc(rows_in, 16)
                r += v.shape[0]
            PAR_ROWS = r
            act.dma_start(x_rows[:, 0:seq // P, :], a["x_prompt"][0].rearrange("(j p) d -> p j d", p=P))\
                .then_inc(rows_in, 16)
            act.dma_start(x_rows[0:dec, seq // P, :], a["x_sample"].rearrange("b s d -> (b s) d"))\
                .then_inc(rows_in, 16)

            def load_states(l):
                act.dma_start(pool_rows[0:dec * HIST, :], a["state_pool"][l].rearrange("b r c -> (b r) c"))\
                    .then_inc(states_in[l], 16)
                act.dma_start(conv_rows[0:dec * 2, :], a["state_conv"][l].rearrange("b r c -> (b r) c"))\
                    .then_inc(states_in[l], 16)

            load_states(0)
            ROW_DMAS = 3 + len(small) + 2
            act.wait_ge(rows_in, 16 * ROW_DMAS)
            act.activation(c_rows[0:S, :], c_rows[0:S, :], ACT.Silu).then_inc(c_silu, 1)

            def hi(n, slot, width=CHUNK, free=True):
                if free:
                    act.wait_ge(used, n - SPLIT_SLOTS + 1)
                act.activation(w_hi[:, slot % SPLIT_SLOTS, 0:width], raw[:, slot, 0:width], ACT.Copy)\
                    .then_inc(hi_done, 1)

            def landed(slot, turn):
                act.wait_ge(raw_in[slot], 16 * (turn + 1))

            act.wait_ge(turned, 1)
            c_ps = ps[:, 4, 0:KC * S].rearrange("p (k s) -> p k s", k=KC)
            act.activation(silu_c[:, :, 0:S], c_ps, ACT.Copy).then_inc(c_split, 1)
            act.wait_ge(turned, 3)
            act.activation(par[:, 0:96], ps[:, 5, 0:96], ACT.Copy).then_inc(par_done, 1)
            act.activation(par[:, 96:96 + PAR_ROWS], ps[:, 5, 96:96 + PAR_ROWS], ACT.Copy).then_inc(par_done, 1)

            for n in range(RAW_SLOTS):
                landed(n, 0)
                hi(n, n, free=n >= SPLIT_SLOTS)
            with act.Fori(1, ADA_CHUNKS // RAW_SLOTS) as i:
                for j in range(RAW_SLOTS):
                    landed(j, i)
                    hi(RAW_SLOTS * i + j, j)

            def norm_scalar(k):
                act.wait_ge(x_done, k + 1)
                act.activation(sq, xT[:, :, :], ACT.Square).then_inc(squares, 1)
                act.wait_ge(inv_var, k + 1)
                act.activation(rstd, var, ACT.Sqrt).then_inc(rstd_done, 1)
                if k == n_norms - 1:
                    return
                for half in range(NORM_H):
                    c0, c1 = half * KC // NORM_H, (half + 1) * KC // NORM_H
                    act.wait_ge(normed, NORM_H * k + half + 1)
                    act.activation(h_hi[:, c0:c1, :], hn[:, c0:c1, :], ACT.Copy).then_inc(h_hi_done, 1)

            def take(ch):
                act.wait_ge(used, ch["n"] + 1)
                for b in ch["blocks"]:
                    blk, col = blocks[b], blocks[b]["col"]
                    src = ps[:, b % 4, 0:T]
                    if blk["eng"] != "act":
                        continue
                    if ch["kind"] == "in" and col < GB:
                        act.activation(b_gate[:, col, :], src, ACT.Copy).then_inc(act_took, 1)
                    elif ch["kind"] == "in" and col < 2 * GB:
                        act.activation(c_gate[:, col - GB, :], src, ACT.Copy).then_inc(act_took, 1)
                    elif ch["kind"] == "in":
                        u = col - 3 * GB
                        us = zu[:, u, SU:].rearrange("p (s r) -> p s r", r=HIST + 1)
                        link(act.activation(us[:, :, HIST], src[:, seq:T], ACT.Copy))
                        act.activation(zu[:, u, HIST:SU], src[:, 0:seq], ACT.Copy).then_inc(act_took, 1)
                    elif ch["kind"] == "gate":
                        if ch["j"] >= 2:
                            act.wait_ge(dve_took, count_of("up", ch["layer"], col - 4))
                        act.activation(silu_g[:, 2 * (ch["j"] % 2) + col % 2, :], src, ACT.Silu)\
                            .then_inc(act_took, 1)
                    elif ch["kind"] == "pool":
                        act.activation(y_pool[:, col, :], src, ACT.Copy,
                                       scale=pcol(PSC + GB * ch["layer"] + col)).then_inc(act_took, 1)
                if ch["kind"] == "up":
                    for b in range(2):
                        f = 2 * ch["j"] + b
                        act.wait_ge(dve_took, count_of("up", ch["layer"], f))
                        act.activation(hid_hi[:, f, :], hid_f[:, b, :], ACT.Copy).then_inc(ffn_hi, 1)

            def mixer_scalar(l):
                act.wait_ge(diff_done, l + 1)
                act.activation(h_hi[:, 0:GB, :], diff, ACT.Copy).then_inc(diff_hi, 1)

            def mix_norm_scalar(l):
                act.wait_ge(mix_y, l + 1)
                for b in range(2 * GB):
                    k = 2 * GB * l + b
                    if b >= 2:
                        act.wait_ge(sq_used, k - 1)
                    src = b_gate[:, b, :] if b < GB else y_pool[:, b - GB, :]
                    act.activation(scr[:, b % 2, 0:T], src, ACT.Square).then_inc(mix_sq, 1)
                act.wait_ge(mix_inv, l + 1)
                act.activation(msq, msq, ACT.Sqrt).then_inc(mix_rstd, 1)
                for half in range(2):
                    act.wait_ge(m_f, 2 * l + half + 1)
                    for b in range(GB):
                        src = (b_gate if half == 0 else y_pool)[:, b, :]
                        ins = act.activation(h_hi[:, half * GB + b, :], src, ACT.Copy,
                                             scale=pcol((GCO if half == 0 else GPO) + GB * l + b))
                    ins.then_inc(m_hi, 1)

            def tails_scalar(l):
                act.wait_ge(tails_turned, l + 1)
                if l:
                    act.wait_ge(out_dma, 64 * l)
                act.activation(new_rows[0:ROWS, :], ps[0:ROWS, 6, :], ACT.Copy).then_inc(tails_out, 1)
                act.wait_ge(tails_out, l + 1)
                o1 = HIST + dec
                act.dma_start(o["pool_prompt"][l, 0], new_rows[0:HIST, :]).then_inc(out_dma, 16)
                act.dma_start(o["pool_sample"][l, :, HIST - 1, :], new_rows[HIST:o1, :]).then_inc(out_dma, 16)
                act.dma_start(o["conv_prompt"][l, 0], new_rows[o1:o1 + 2, :]).then_inc(out_dma, 16)
                act.dma_start(o["conv_sample"][l].rearrange("b r c -> (b r) c"), new_rows[o1 + 2:ROWS, :])\
                    .then_inc(out_dma, 16)

            norm_scalar(0)

            def after(ch):
                if ch["n"] == dense_end("in", ch["layer"]):
                    mixer_scalar(ch["layer"])
                if ch["n"] == dense_end("pool", ch["layer"]):
                    mix_norm_scalar(ch["layer"])
                    tails_scalar(ch["layer"])
                    if ch["layer"] == 0:
                        act.wait_ge(m_lo, 2)
                        act.wait_ge(mix_rstd, 1)
                        load_states(1)
                if ch["n"] == dense_end("out", ch["layer"]):
                    norm_scalar(2 * ch["layer"] + 1)
                if ch["kind"] == "down" and ch["n"] == dense_end("down", ch["layer"]):
                    norm_scalar(2 * ch["layer"] + 2)

            for ch in dense:
                landed(rs(ch["n"]), ch["n"] // RAW_SLOTS)
                hi(ch["n"], rs(ch["n"]), ch["nk"] * ch["width"])
                back = ch["n"] - D0 - SPLIT_SLOTS
                if back >= 0:
                    take(dense[back])
                    after(dense[back])
            for k in range(SPLIT_SLOTS):
                landed((M0 + k) % 6, (M0 + k) // 6)
                hi(M0 + k, (M0 + k) % 6)
                take(dense[len(dense) - SPLIT_SLOTS + k])
                after(dense[len(dense) - SPLIT_SLOTS + k])

            act.wait_ge(route_max, 1)
            act.wait_ge(chosen_done, 1)
            act.activation(rank, logit, ACT.Exp).then_inc(route_exp, 1)

            for s in range(4 * TT):
                j, part_no, half = s // 4, s // 2 % 2, s % 2
                rows = LAST if j == TT - 1 else P
                act.wait_ge(tok_turned, s + 1)
                if s == 0:
                    act.wait_ge(tok_zero, 1)
                dst = (tok_hi if part_no == 0 else tok_lo)[0:rows, j, half * BANK:(half + 1) * BANK]
                act.activation(dst, ps[0:rows, 4 + s % 4, :], ACT.Copy).then_inc(tok_copied, 1)

            def take_gather(e):
                for s in range(4):
                    act.wait_ge(gather_ps, 4 * e + s + 1)
                    dst = (xs_hi if s < 2 else xs_lo)[:, 4 * (s % 2):4 * (s % 2) + 4, :]
                    act.activation(dst, ps[:, 6 + s % 2, :].rearrange("p (c s) -> p c s", c=4), ACT.Copy)\
                        .then_inc(gathered, 1)

            def silu(q, bank, ready):
                act.wait_ge(used, ready)
                act.wait_ge(e_hid_done, q)
                act.activation(e_silu, ps[:, bank, :], ACT.Silu).then_inc(e_silu_done, 1)

            def split_hidden(q, bank):
                act.wait_ge(e_turned, q + 1)
                act.activation(eh_hi, ps[:, bank, :].rearrange("p (k s) -> p k s", k=GC), ACT.Copy)\
                    .then_inc(e_hi_done, 1)

            def scale_y(e, ready):
                act.wait_ge(used, ready)
                for half in range(HALVES):
                    act.activation(y_f[:, half * BANK:(half + 1) * BANK], ps[:, 4 + half, :], ACT.Copy,
                                   scale=gate_slot).then_inc(y_scaled, 1)
                act.wait_ge(y_scaled, HALVES * (e + 1))
                act.activation(y_hi, y_f.rearrange("p (c d) -> p c d", c=KC), ACT.Copy).then_inc(y_hi_done, 1)

            def take_selT(e, bank):
                act.wait_ge(selT_ps, e + 1)
                act.activation(selT, ps[:, bank, 0:T], ACT.Copy).then_inc(selT_done, 1)
                act.activation(gate_slot, ps[:, bank, T:T + 1], ACT.Copy).then_inc(selT_done, 1)

            plan = misc_plan()

            def expert(e, first, split_before=0):
                for pos, kind, g in expert_chunks(first):
                    n, s = chunk_no(e, pos, first), slot_of(pos, first)
                    if not (first and pos < split_before):
                        landed(s, n // 6 if isinstance(n, int) else (M0 - 2 + pos) // 6 + GROUPS * e)
                        hi(n, s)
                    if pos % 6 == 0 and (pos or not first):
                        silu(GROUPS * e + g - 1, (g - 1) % GROUPS % 2 * 2, group_end(e, g - 1, first))
                    if pos == 0 and not first:
                        take_gather(e)
                    if pos % 6 == 3 and (pos > 3 or not first):
                        split_hidden(GROUPS * e + g - 1, plan["hid", (g - 1) % GROUPS])
                    if pos == 8 and not first:
                        scale_y(e - 1, expert_end(e - 1))
                    if pos == 13:
                        take_selT(e, plan["selT"])

            take_gather(0)
            expert(0, True, SPLIT_SLOTS)
            with act.Fori(1, n_exp) as e:
                expert(e, False)
            for q in range(2):
                n = M1 - 2 + q
                landed(n % 6, n // 6)
                hi(n, n % 6)
                if q == 0:
                    silu(n_exp * GROUPS - 1, (GROUPS - 1) % 2 * 2, group_end(n_exp, -1, False))
            split_hidden(n_exp * GROUPS - 1, plan["hid", GROUPS - 1])
            scale_y(n_exp - 1, M1)

            act.wait_ge(extra_done, 1)
            many = act.value_load(extra_i[0:1, EXTRA:EXTRA + 1], min_val=0, max_val=EXTRA)
            with act.If(many > 0):
                with act.Fori(0, many) as i:
                    take_selT(n_exp + i, 7)
                    take_gather(n_exp + i)
                    for pos in range(PER_EXPERT):
                        g, q = divmod(pos, 6)
                        landed((M1 + pos) % 6, (M1 + pos) // 6 + GROUPS * i)
                        hi(M1 + PER_EXPERT * i + pos, (M1 + pos) % 6)
                        if q == 5:
                            silu(GROUPS * (n_exp + i) + g, 0, M1 + PER_EXPERT * i + 6 * g + 4)
                            split_hidden(GROUPS * (n_exp + i) + g, 6)
                    scale_y(n_exp + i, M1 + PER_EXPERT * (i + 1))

            norm_scalar(n_norms - 1)
            act.wait_ge(out_dma, 64 * depth)
            for s in range(2 * TT):
                j, half = divmod(s, 2)
                rows = LAST if j == TT - 1 else P
                act.wait_ge(fin_ps, s + 1)
                act.activation(y_rows[0:rows, j, half * BANK:(half + 1) * BANK], ps[0:rows, s, :], ACT.Copy)\
                    .then_inc(fin_out, 1)
            for j in range(TT):
                act.wait_ge(fin_out, 2 * (j + 1))
                if j < TT - 1:
                    act.dma_start(o["y_prompt"][0, j * P:(j + 1) * P, :], y_rows[:, j, :]).then_inc(y_dma, 16)
                else:
                    act.dma_start(o["y_sample"].rearrange("b s d -> (b s) d"), y_rows[0:LAST, j, :])\
                        .then_inc(y_dma, 16)
            act.wait_ge(y_dma, 16 * TT)

        @block.vector
        def _(dve):
            steps = [0]

            def link(ins):
                steps[0] += 1
                ins.then_inc(dve_step, 1)
                dve.wait_ge(dve_step, steps[0])

            dve.wait_ge(consts, 2)
            link(dve.reciprocal(fix[:, :, :], fix[:, :, :]))
            for g, w in enumerate(WINDOWS):
                link(dve.tensor_scalar(fix[:, g, :], fix[:, g, :], float(w), None, ALU.mult))

            def lo(n, slot, width=CHUNK):
                dve.wait_ge(hi_done, n + 1)
                dve.tensor_tensor(w_lo[:, slot % SPLIT_SLOTS, 0:width], raw[:, slot, 0:width],
                                  w_hi[:, slot % SPLIT_SLOTS, 0:width].bitcast(F32), ALU.subtract)\
                    .then_inc(lo_done, 1)

            dve.wait_ge(c_split, 1)
            c_ps = ps[:, 4, 0:KC * S].rearrange("p (k s) -> p k s", k=KC)
            dve.tensor_tensor(silu_c[:, :, S:2 * S], c_ps, silu_c[:, :, 0:S].bitcast(F32), ALU.subtract)\
                .then_inc(c_split, 1)
            for c in range(KC):
                dve.wait_ge(turned, 4 + c)
                dve.tensor_copy(xT[:, c, :], ps[:, (0, 1, 2, 3)[c % 4], 0:T]).then_inc(turned_out, 1)
            dve.wait_ge(turned_out, KC)
            dve.wait_ge(par_done, 2)

            def take_ada(i, half, count):
                dve.wait_ge(used, count)
                nb = 2 * RAW_SLOTS
                v = ps[:, half, 0:nb * 2 * S].rearrange("p (b s) -> p b s", b=nb)
                m = modT[:, :, :, :].rearrange("p l j s -> p (l j) s")
                dst = m[:, bass.ds(2 * nb * i + nb * half, nb), :]
                bias = par[:, bass.ds(2 * nb * i + nb * half, nb)]
                bias = bias.unsqueeze(2).to_broadcast([P, nb, S])
                dve.tensor_tensor(dst, v[:, :, 0:S], bias, ALU.add).then_inc(ada_out, 1)
                dve.wait_ge(ada_out, 3 + 2 * (2 * i + half) + 1)
                dve.tensor_tensor(dst, dst, v[:, :, S:2 * S], ALU.add).then_inc(ada_out, 1)

            for _ in range(3):
                dve.engine_nop().then_inc(ada_out, 1)
            with dve.Fori(0, ADA_CHUNKS // (2 * RAW_SLOTS)) as i:
                for j in range(2 * RAW_SLOTS):
                    lo(2 * RAW_SLOTS * i + j, j % RAW_SLOTS)
                    if j % RAW_SLOTS == RAW_SLOTS - 1:
                        take_ada(i, j // RAW_SLOTS, 2 * RAW_SLOTS * i + j + 1)
            dve.wait_ge(ada_out, 3 + 2 * ADA_CHUNKS // RAW_SLOTS)

            def mod(l, what):
                return modT[:, l, what * KC:(what + 1) * KC, :]

            for l in range(depth):
                for what, g in ((SC1, G_MIX), (SC2, G_FFN)):
                    gv = pcol(g + KC * l, KC).unsqueeze(2).to_broadcast([P, KC, S])
                    link(dve.scalar_tensor_tensor(out=mod(l, what), in0=mod(l, what), scalar=1.0, in1=gv,
                                                  op0=ALU.add, op1=ALU.mult))
            dve.engine_nop().then_inc(x_done, 1)

            def norm_vector(k):
                l, first = divmod(k, 2)
                dve.wait_ge(sums, k + 1)
                link(dve.tensor_scalar(var, ps[:, 4, 0:T], 1.0 / d_model, EPS, ALU.mult, ALU.add))
                dve.reciprocal(var, var).then_inc(inv_var, 1)
                dve.wait_ge(rstd_done, k + 1)
                rb = rstd.unsqueeze(1).to_broadcast([P, KC, T])
                link(dve.tensor_tensor(hn, xT[:, :, :], rb, ALU.mult))
                if k == n_norms - 1:
                    for c in range(KC):
                        dve.tensor_scalar(hn[:, c, :], hn[:, c, :], pcol(G_FIN + c), None, ALU.mult)\
                            .then_inc(fin_f, 1)
                    return
                sc, sh = (mod(l, SC1), mod(l, SH1)) if first == 0 else (mod(l, SC2), mod(l, SH2))
                hs = hn[:, :, seq:T]
                link(dve.tensor_tensor(hs, hs, sc[:, :, 1:S], ALU.mult))
                link(dve.tensor_tensor(hs, hs, sh[:, :, 1:S], ALU.add))
                for half in range(NORM_H):
                    for c in range(half * KC // NORM_H, (half + 1) * KC // NORM_H):
                        ins = dve.tensor_scalar(hn[:, c, 0:seq], hn[:, c, 0:seq], sc[:, c, 0:1], sh[:, c, 0:1],
                                                ALU.mult, ALU.add)
                        if c % (KC // NORM_H) != KC // NORM_H - 1:
                            ins.then_inc(dve_step, 1)
                            steps[0] += 1
                    dve.wait_ge(dve_step, steps[0])
                    ins.then_inc(normed, 1)
                for half in range(NORM_H):
                    c0, c1 = half * KC // NORM_H, (half + 1) * KC // NORM_H
                    dve.wait_ge(h_hi_done, NORM_H * k + half + 1)
                    dve.tensor_tensor(h_lo[:, c0:c1, :], hn[:, c0:c1, :], h_hi[:, c0:c1, :].bitcast(F32),
                                      ALU.subtract).then_inc(h_lo_done, 1)

            def add_gated(l, gt, c, src_p, src_s, done):
                link(dve.tensor_tensor(scr[:, 0, 0:dec], src_s, mod(l, gt)[:, c, 1:S], ALU.mult))
                link(dve.tensor_tensor(xT[:, c, seq:T], xT[:, c, seq:T], scr[:, 0, 0:dec], ALU.add))
                ins = dve.scalar_tensor_tensor(out=xT[:, c, 0:seq], in0=src_p, scalar=mod(l, gt)[:, c, 0:1],
                                               in1=xT[:, c, 0:seq], op0=ALU.mult, op1=ALU.add)
                if done is not None:
                    ins.then_inc(done, 1)
                return ins

            def take(ch):
                dve.wait_ge(used, ch["n"] + 1)
                l = ch["layer"]
                for b in ch["blocks"]:
                    blk, col = blocks[b], blocks[b]["col"]
                    src = ps[:, b % 4, 0:T]
                    if blk["eng"] != "dve":
                        continue
                    if ch["kind"] == "in":
                        v = col - 2 * GB
                        dve.wait_ge(act_took, count_of("in", l, GB + v))
                        vs = zv[:, v, SV:].rearrange("p (s r) -> p s r", r=3)
                        link(dve.tensor_tensor(vs[:, :, 2], src[:, seq:T], c_gate[:, v, seq:T], ALU.mult))
                        dve.tensor_tensor(zv[:, v, 2:SV], src[:, 0:seq], c_gate[:, v, 0:seq], ALU.mult)\
                            .then_inc(dve_took, 1)
                    elif ch["kind"] == "out":
                        add_gated(l, GT1, col, src[:, 0:seq], src[:, seq:T], dve_took)
                    elif ch["kind"] == "down" and ch["last"]:
                        add_gated(l, GT2, col, src[:, 0:seq], src[:, seq:T], dve_took)
                    elif ch["kind"] == "up":
                        f = col
                        dve.wait_ge(act_took, count_of("gate", l, f))
                        if f >= 2:
                            dve.wait_ge(ffn_lo, f - 1)
                        dve.tensor_tensor(hid_f[:, col % 2, :], src, silu_g[:, 2 * (ch["j"] % 2) + col % 2, :],
                                          ALU.mult).then_inc(dve_took, 1)
                if ch["kind"] == "up":
                    for b in range(2):
                        f = 2 * ch["j"] + b
                        dve.wait_ge(ffn_hi, f + 1)
                        dve.tensor_tensor(hid_lo[:, f, :], hid_f[:, b, :], hid_hi[:, f, :].bitcast(F32),
                                          ALU.subtract).then_inc(ffn_lo, 1)

            def put_states(l):
                link(dve.memset(zu[:, :, 0:HIST], 0.0))
                link(dve.memset(zv[:, :, 0:2], 0.0))
                dve.wait_ge(state_turned, 2 * (l + 1))
                us = zu[:, :, SU:].rearrange("p b (s r) -> p b s r", r=HIST + 1)
                ups = ps[:, 6, 0:GB * dec * HIST].rearrange("p (b s r) -> p b s r", b=GB, s=dec)
                vs = zv[:, :, SV:].rearrange("p b (s r) -> p b s r", r=3)
                vps = ps[:, 7, 0:GB * dec * 2].rearrange("p (b s r) -> p b s r", b=GB, s=dec)
                for b in range(GB):
                    link(dve.tensor_copy(us[:, b, :, 0:HIST], ups[:, b]))
                    link(dve.tensor_copy(vs[:, b, :, 0:2], vps[:, b]))
                dve.engine_nop().then_inc(state_put, 1)
                dve.engine_nop().then_inc(state_put, 1)

            def mixer_vector(l):
                dve.wait_ge(act_took, count_of("in", l, 4 * GB - 1))
                if l:
                    dve.wait_ge(out_dma, 64 * l)
                n1 = ZU - 1
                link(dve.tensor_tensor(sum_a[:, :, 0:n1], zu[:, :, 0:n1], zu[:, :, 1:ZU], ALU.add))
                n2 = n1 - 2
                link(dve.tensor_tensor(sum_b[:, :, 0:n2], sum_a[:, 1:, 0:n2], sum_a[:, 1:, 2:n2 + 2], ALU.add))
                n3 = n2 - 4
                link(dve.tensor_tensor(sum_a[:, 2:, 0:n3], sum_b[:, 1:, 0:n3], sum_b[:, 1:, 4:n3 + 4], ALU.add))
                n4 = n3 - 8
                link(dve.tensor_tensor(sum_b[:, 2, 0:n4], sum_a[:, 3, 0:n4], sum_a[:, 3, 8:n4 + 8], ALU.add))
                wins = [sum_a[:, 0, :], sum_b[:, 0, :], sum_a[:, 2, :], sum_b[:, 2, :]]
                for g, w in enumerate(WINDOWS):
                    s0 = HIST + 1 - w
                    head = wins[g][:, s0:s0 + HIST + 1]
                    link(dve.tensor_tensor(head, head, fix[:, g, :], ALU.mult))
                    link(dve.scalar_tensor_tensor(out=diff[:, g, 0:seq], in0=wins[g][:, s0:s0 + seq], scalar=1.0 / w,
                                                  in1=zu[:, g, HIST:SU], op0=ALU.mult, op1=ALU.subtract))
                    ends = zu[:, g, SU:].rearrange("p (s r) -> p s r", r=HIST + 1)[:, :, HIST]
                    at_ = SU + HIST + 1 - w
                    wv = wins[g][:, at_:at_ + (HIST + 1) * (dec - 1) + 1:HIST + 1]
                    ins = dve.scalar_tensor_tensor(out=diff[:, g, seq:T], in0=wv, scalar=1.0 / w, in1=ends,
                                                   op0=ALU.mult, op1=ALU.subtract)
                    if g < GB - 1:
                        link(ins)
                ins.then_inc(diff_done, 1)
                dve.wait_ge(diff_hi, l + 1)
                dve.tensor_tensor(h_lo[:, 0:GB, :], diff, h_hi[:, 0:GB, :].bitcast(F32), ALU.subtract)\
                    .then_inc(diff_lo, 1)
                n = ZV - 2
                for b in range(GB):
                    w = [pcol(CONV + (3 * l + k) * GB + b) for k in range(3)]
                    link(dve.tensor_scalar(scr[:, 0, :], zv[:, b, 0:n], w[0], None, ALU.mult))
                    link(dve.scalar_tensor_tensor(out=scr[:, 1, :], in0=zv[:, b, 1:n + 1], scalar=w[1],
                                                  in1=scr[:, 0, :], op0=ALU.mult, op1=ALU.add))
                    link(dve.scalar_tensor_tensor(out=scr[:, 0, :], in0=zv[:, b, 2:n + 2], scalar=w[2],
                                                  in1=scr[:, 1, :], op0=ALU.mult, op1=ALU.add))
                    link(dve.tensor_tensor(b_gate[:, b, 0:seq], b_gate[:, b, 0:seq], scr[:, 0, 0:seq], ALU.mult))
                    last = dve.tensor_tensor(b_gate[:, b, seq:T], b_gate[:, b, seq:T],
                                             scr[:, 0, SV:SV + 3 * (dec - 1) + 1:3], ALU.mult)
                    link(last)

            def mix_norm_vector(l):
                dve.engine_nop().then_inc(mix_y, 1)
                dve.wait_ge(sq_used, 2 * GB * (l + 1))
                sums_ps = ps[:, 4:6, 0:T]
                link(dve.tensor_scalar(msq, sums_ps, 1.0 / (GB * P), EPS, ALU.mult, ALU.add))
                dve.reciprocal(msq, msq).then_inc(mix_inv, 1)
                dve.wait_ge(mix_rstd, l + 1)
                for half, y in ((0, b_gate), (1, y_pool)):
                    rb = msq[:, half, :].unsqueeze(1).to_broadcast([P, GB, T])
                    dve.tensor_tensor(y, y, rb, ALU.mult).then_inc(m_f, 1)
                for half, y in ((0, b_gate), (1, y_pool)):
                    dve.wait_ge(m_hi, 2 * l + half + 1)
                    for b in range(GB):
                        ins = dve.scalar_tensor_tensor(
                            out=h_lo[:, half * GB + b, :], in0=y[:, b, :],
                            scalar=pcol((GCO if half == 0 else GPO) + GB * l + b),
                            in1=h_hi[:, half * GB + b, :].bitcast(F32), op0=ALU.mult, op1=ALU.subtract)
                    ins.then_inc(m_lo, 1)

            norm_vector(0)
            put_states(0)

            def after(ch):
                l = ch["layer"]
                if ch["n"] == dense_end("in", l):
                    mixer_vector(l)
                if ch["n"] == dense_end("pool", l):
                    dve.wait_ge(act_took, blocks[ch["blocks"][-1]]["count"])
                    mix_norm_vector(l)
                if ch["n"] == dense_end("out", l):
                    dve.wait_ge(dve_took, blocks[ch["blocks"][-1]]["count"])
                    if l == 0:
                        dve.wait_ge(tails, 4)
                    else:
                        dve.wait_ge(tails, 8)
                    dve.engine_nop().then_inc(x_done, 1)
                    norm_vector(2 * l + 1)
                if ch["kind"] == "down" and ch["n"] == dense_end("down", l):
                    dve.wait_ge(dve_took, blocks[ch["blocks"][-1]]["count"])
                    dve.engine_nop().then_inc(x_done, 1)
                    norm_vector(2 * l + 2)
                    dve.wait_ge(h_lo_done, NORM_H * (2 * l + 3))
                    put_states(l + 1)

            for ch in dense:
                lo(ch["n"], rs(ch["n"]), ch["nk"] * ch["width"])
                back = ch["n"] - D0 - SPLIT_SLOTS
                if back >= 0:
                    take(dense[back])
                    after(dense[back])
            for k in range(SPLIT_SLOTS):
                lo(M0 + k, (M0 + k) % 6)
                take(dense[len(dense) - SPLIT_SLOTS + k])
                after(dense[len(dense) - SPLIT_SLOTS + k])

            dve.wait_ge(tok_zero, 1)
            dve.wait_ge(logits_ps, 1)
            for j in range(TT):
                rows = LAST if j == TT - 1 else P
                link(dve.tensor_copy(logit[0:rows, j, :], ps[0:rows, 4, E * j:E * (j + 1)]))
            shape = [P, TT, E, E]
            mine = logit.unsqueeze(3).to_broadcast(shape)
            other = logit.unsqueeze(2).to_broadcast(shape)
            link(dve.tensor_tensor(cmp1, other, mine, ALU.is_gt))
            link(dve.tensor_tensor(cmp2, other, mine, ALU.is_equal))
            link(dve.tensor_tensor(cmp2, cmp2, earlier.unsqueeze(1).to_broadcast(shape), ALU.mult))
            link(dve.tensor_tensor(cmp1, cmp1, cmp2, ALU.add))
            link(dve.tensor_reduce(rank, cmp1, axis=AX_X, op=ALU.add))
            link(dve.tensor_scalar(chosen, rank, 2.0, None, ALU.is_lt))
            dve.tensor_tensor(chosen, chosen, real.unsqueeze(2).to_broadcast([P, TT, E]), ALU.mult)\
                .then_inc(chosen_done, 1)
            link(dve.tensor_reduce(lmax, logit, axis=AX_X, op=ALU.max))
            dve.tensor_tensor(logit, logit, lmax.unsqueeze(2).to_broadcast([P, TT, E]), ALU.subtract)\
                .then_inc(route_max, 1)
            dve.wait_ge(chosen_done, 1)
            dve.wait_ge(route_exp, 1)
            link(dve.tensor_tensor(logit, rank, chosen, ALU.mult))
            link(dve.tensor_reduce(lsum, logit, axis=AX_X, op=ALU.add))
            link(dve.tensor_scalar(lsum, lsum, 1e-30, None, ALU.max))
            link(dve.reciprocal(lsum, lsum))
            link(dve.tensor_tensor(gate.rearrange("p e j -> p j e"), logit,
                                   lsum.unsqueeze(2).to_broadcast([P, TT, E]), ALU.mult))
            dve.wait_ge(cum_ps, 1)
            before = ps[:, 5, 0:TT * E].rearrange("p (j e) -> p j e", j=TT)
            link(dve.tensor_scalar(rank, before, 1000.0, None, ALU.add))
            link(dve.tensor_tensor(rank, rank, chosen, ALU.mult))
            link(dve.tensor_scalar(place.rearrange("p e j -> p j e"), rank, -1000.0, None, ALU.add))
            count = ps[:, 5, TT * E:(TT + 1) * E]
            for j in range(TT - 1):
                link(dve.tensor_scalar(more[:, j, :], count, float(P * (j + 1)), None, ALU.is_gt))
            cur, nxt, d = more_row, more_no, 1
            link(dve.tensor_copy(tmp_row, more_row))
            cur = tmp_row
            while d < NX:
                link(dve.tensor_copy(nxt[:, 0:d], cur[:, 0:d]))
                link(dve.tensor_tensor(nxt[:, d:NX], cur[:, d:NX], cur[:, 0:NX - d], ALU.add))
                cur, nxt = nxt, cur
                d *= 2
            want = slot_no[:, 1:EXTRA + 1].unsqueeze(2).to_broadcast([P, EXTRA, NX])
            link(dve.tensor_tensor(hit, cur.unsqueeze(1).to_broadcast([P, EXTRA, NX]), want, ALU.is_equal))
            link(dve.tensor_tensor(hit, hit, more_row.unsqueeze(1).to_broadcast([P, EXTRA, NX]), ALU.mult))
            link(dve.tensor_tensor(hit2, hit, code_s.unsqueeze(1).to_broadcast([P, EXTRA, NX]), ALU.mult))
            link(dve.tensor_reduce(extra_shift, hit2, axis=AX_X, op=ALU.add))
            link(dve.tensor_tensor(hit2, hit, code_e.unsqueeze(1).to_broadcast([P, EXTRA, NX]), ALU.mult))
            link(dve.tensor_reduce(extra_f[:, 0:EXTRA], hit2, axis=AX_X, op=ALU.add))
            link(dve.tensor_copy(extra_f[:, EXTRA:EXTRA + 1], cur[:, NX - 1:NX]))
            dve.tensor_copy(extra_i[:, :], extra_f).then_inc(extra_done, 1)

            def make_sel(k, e):
                dve.wait_ge(selT_done, 2 * k)
                dve.wait_ge(gather_ps, 4 * k)
                dve.tensor_copy(place_e, place[:, e, :] if isinstance(e, int) else
                                place[:, bass.ds(e, 1), :].rearrange("p e j -> p (e j)")).then_inc(place_made, 1)
                dve.tensor_copy(gate_e, gate[:, e, :] if isinstance(e, int) else
                                gate[:, bass.ds(e, 1), :].rearrange("p e j -> p (e j)")).then_inc(place_made, 1)

            def fill_sel(k, places):
                dve.wait_ge(place_made, places)
                for j in range(TT):
                    dve.tensor_scalar(sel[:, j, :], slot_no[:, :], place_e[:, j:j + 1], None, ALU.is_equal)\
                        .then_inc(sel_made, 1)

            def hidden(q, bank):
                dve.wait_ge(e_silu_done, q + 1)
                dve.wait_ge(e_turned, q)
                dve.tensor_tensor(e_hid, ps[:, bank + 1, :], e_silu, ALU.mult).then_inc(e_hid_done, 1)

            def split_hidden(q, bank):
                dve.wait_ge(e_hi_done, q + 1)
                dve.tensor_tensor(eh_lo, ps[:, bank, :].rearrange("p (k s) -> p k s", k=GC),
                                  eh_hi.bitcast(F32), ALU.subtract).then_inc(e_lo_done, 1)

            def split_y(e):
                dve.wait_ge(y_hi_done, e + 1)
                dve.tensor_tensor(y_lo, y_f.rearrange("p (c d) -> p c d", c=KC), y_hi.bitcast(F32), ALU.subtract)\
                    .then_inc(y_lo_done, 1)

            def combine(e, banks):
                for c in range(KC):
                    dve.wait_ge(comb_ps, KC * e + c + 1)
                    dve.tensor_tensor(acc[:, c, :], acc[:, c, :], ps[:, banks[c % 2], 0:T], ALU.add)\
                        .then_inc(combined, 1)
                dve.wait_ge(combined, KC * (e + 1))

            plan = misc_plan()

            def expert(e, first, last, split_before=0):
                for pos, kind, g in expert_chunks(first):
                    n, s = chunk_no(e, pos, first), slot_of(pos, first)
                    if not (first and pos < split_before):
                        lo(n, s)
                    if pos % 6 == 0 and (pos or not first):
                        hidden(GROUPS * e + g - 1, (g - 1) % GROUPS % 2 * 2)
                    if pos % 6 == 3 and (pos > 3 or not first):
                        split_hidden(GROUPS * e + g - 1, plan["hid", (g - 1) % GROUPS])
                    if pos == 8 and not first:
                        split_y(e - 1)
                    if pos == 12 and not first:
                        combine(e - 1, plan["comb"])
                    if pos == 18 and not last:
                        make_sel(e + 1, e + 1)
                        fill_sel(e + 1, 2 * (e + 2))

            make_sel0 = [dve.tensor_copy(place_e, place[:, 0, :]), dve.tensor_copy(gate_e, gate[:, 0, :])]
            for ins in make_sel0:
                ins.then_inc(place_made, 1)
            fill_sel(0, 2)
            expert(0, True, False, SPLIT_SLOTS)
            with dve.Fori(1, n_exp - 1) as e:
                expert(e, False, False)
            expert(n_exp - 1, False, True)
            for q in range(2):
                n = M1 - 2 + q
                lo(n, n % 6)
                if q == 0:
                    hidden(n_exp * GROUPS - 1, (GROUPS - 1) % 2 * 2)
            split_hidden(n_exp * GROUPS - 1, plan["hid", GROUPS - 1])
            split_y(n_exp - 1)
            combine(n_exp - 1, (6, 7))

            dve.wait_ge(extra_done, 1)
            many = dve.value_load(extra_i[0:1, EXTRA:EXTRA + 1], min_val=0, max_val=EXTRA)
            with dve.If(many > 0):
                with dve.Fori(0, many) as i:
                    e = dve.value_load(extra_i[0:1, bass.ds(i, 1)], min_val=0, max_val=n_exp - 1)
                    k = n_exp + i
                    make_sel(k, e)
                    dve.wait_ge(place_made, 2 * n_exp + 3 * i + 2)
                    dve.tensor_scalar(place_e, place_e, extra_shift[:, bass.ds(i, 1)], None, ALU.subtract)\
                        .then_inc(place_made, 1)
                    fill_sel(k, 2 * n_exp + 3 * i + 3)
                    for pos in range(PER_EXPERT):
                        g, q = divmod(pos, 6)
                        lo(M1 + PER_EXPERT * i + pos, (M1 + pos) % 6)
                        if q == 5:
                            hidden(GROUPS * k + g, 0)
                            split_hidden(GROUPS * k + g, 6)
                    split_y(k)
                    combine(k, (6, 7))

            dve.wait_ge(combined, KC * n_exp)
            for c in range(KC):
                last = add_gated(1, GT2, c, acc[:, c, 0:seq], acc[:, c, seq:T], None)
                link(last)
            dve.engine_nop().then_inc(x_done, 1)
            norm_vector(n_norms - 1)

        @block.tensor
        def _(pe):
            pe.wait_ge(consts, 2)
            pe.wait_ge(c_silu, 1)
            for k in range(KC):
                ins = pe.transpose(ps[:, 4, k * S:(k + 1) * S], c_rows[0:S, k * P:(k + 1) * P], ident[0:S, 0:S])
            ins.then_inc(turned, 1)
            n0 = depth * ADA_PARTS * KC
            pe.transpose(ps[:, 5, 0:n0], par_rows[0:n0, 0, :], ident[0:n0, 0:n0]).then_inc(turned, 1)
            pe.transpose(ps[:, 5, n0:184], par_rows[0:184 - n0, 1, :], ident[0:184 - n0, 0:184 - n0])\
                .then_inc(turned, 1)
            for c in range(KC):
                if c >= 4:
                    pe.wait_ge(turned_out, c - 3)
                for j in range(TT):
                    rows = LAST if j == TT - 1 else P
                    ins = pe.transpose(ps[:, c % 4, j * P:j * P + rows], x_rows[0:rows, j, c * P:(c + 1) * P],
                                       ident[0:rows, 0:rows])
                ins.then_inc(turned, 1)
            def turn_states(l):
                pe.wait_ge(states_in[l], 32)
                if l:
                    pe.wait_ge(tails_out, l)
                for b in range(GB):
                    n = dec * HIST
                    ins = pe.transpose(ps[:, 6, b * n:(b + 1) * n], pool_rows[0:n, b * P:(b + 1) * P],
                                       ident[0:n, 0:n])
                ins.then_inc(state_turned, 1)
                for b in range(GB):
                    n = dec * 2
                    ins = pe.transpose(ps[:, 7, b * n:(b + 1) * n], conv_rows[0:n, b * P:(b + 1) * P],
                                       ident[0:n, 0:n])
                ins.then_inc(state_turned, 1)

            turn_states(0)
            pe.wait_ge(c_split, 2)
            pe.wait_ge(turned_out, KC)

            with pe.Fori(0, ADA_CHUNKS // (2 * RAW_SLOTS)) as i:
                for j in range(2 * RAW_SLOTS):
                    s, bank = j % SPLIT_SLOTS, j // RAW_SLOTS
                    pe.wait_ge(lo_done, 2 * RAW_SLOTS * i + j + 1)
                    if j % RAW_SLOTS == 0:
                        pe.wait_ge(ada_out, 1 + 4 * i + 2 * bank)
                    for b in range(2):
                        blk = 2 * (j % RAW_SLOTS) + b
                        out = ps[:, bank, blk * 2 * S:(blk + 1) * 2 * S]
                        for k in range(KC):
                            w = slice(256 * k + P * b, 256 * k + P * (b + 1))
                            pe.matmul(out, w_hi[:, s, w], silu_c[:, k, :], start=(k == 0), stop=False)
                            ins = pe.matmul(out, w_lo[:, s, w], silu_c[:, k, :], start=False, stop=(k == KC - 1))
                    ins.then_inc(used, 1)
            pe.wait_ge(ada_out, 3 + 2 * ADA_CHUNKS // RAW_SLOTS)

            def norm_sums(k):
                pe.wait_ge(squares, k + 1)
                if k:
                    pe.wait_ge(inv_var, k)
                for c in range(KC):
                    ins = pe.matmul(ps[:, 4, 0:T], ones[:, :], sq[:, c, :], start=(c == 0), stop=(c == KC - 1))
                ins.then_inc(sums, 1)

            def bank_free(b):
                if b >= 4:
                    old = blocks[b - 4]
                    pe.wait_ge(act_took if old["eng"] == "act" else dve_took, old["count"])

            norm_sums(0)
            for ch in dense:
                n, s, l, kind = ch["n"], ch["n"] % SPLIT_SLOTS, ch["layer"], ch["kind"]
                x_hi, x_lo = (hid_hi, hid_lo) if kind == "down" else (h_hi, h_lo)
                pe.wait_ge(lo_done, n + 1)
                if kind == "in" and ch["j"] == 0:
                    pe.wait_ge(h_lo_done, NORM_H * (2 * l + 1))
                if kind == "gate" and ch["j"] == 0:
                    pe.wait_ge(h_lo_done, NORM_H * (2 * l + 2))
                if kind == "pool":
                    pe.wait_ge(diff_lo, l + 1)
                if kind == "out" and ch["j"] == 0:
                    for b in range(2 * GB):
                        pe.wait_ge(mix_sq, 2 * GB * l + b + 1)
                        pe.matmul(ps[:, 4 + b // GB, 0:T], ones[:, :], scr[:, b % 2, 0:T], start=(b % GB == 0),
                                  stop=(b % GB == GB - 1)).then_inc(sq_used, 1)
                    pe.wait_ge(tails, 4 * (l + 1))
                    for b in range(GB):
                        ins = pe.transpose(ps[0:ROWS, 6, b * P:(b + 1) * P], last_rows[:, b, :], ident[:, :])
                    ins.then_inc(tails_turned, 1)
                    pe.wait_ge(m_lo, 2 * (l + 1))
                if kind == "down":
                    pe.wait_ge(ffn_lo, min(FC, ch["k0"] + ch["nk"]))
                for b, blk in enumerate(ch["blocks"]):
                    if ch["first"]:
                        bank_free(blk)
                    out = ps[:, blk % 4, 0:T]
                    if kind == "pool":
                        w = slice(P * b, P * (b + 1))
                        pe.matmul(out, w_hi[:, s, w], h_hi[:, b, :], start=True, stop=False)
                        pe.matmul(out, w_hi[:, s, w], h_lo[:, b, :], start=False, stop=False)
                        ins = pe.matmul(out, w_lo[:, s, w], h_hi[:, b, :], start=False, stop=True)
                        continue
                    for k in range(ch["nk"]):
                        w = slice(256 * k + P * b, 256 * k + P * (b + 1))
                        kk = ch["k0"] + k
                        pe.matmul(out, w_hi[:, s, w], x_hi[:, kk, :], start=(kk == 0), stop=False)
                        pe.matmul(out, w_hi[:, s, w], x_lo[:, kk, :], start=False, stop=False)
                        ins = pe.matmul(out, w_lo[:, s, w], x_hi[:, kk, :], start=False,
                                        stop=ch["last"] and k == ch["nk"] - 1)
                ins.then_inc(used, 1)
                if n == dense_end("out", l):
                    norm_sums(2 * l + 1)
                if kind == "down" and n == dense_end("down", l):
                    norm_sums(2 * l + 2)
                    turn_states(l + 1)

            pe.wait_ge(router_in, 16)
            pe.wait_ge(h_lo_done, NORM_H * 4)
            pe.wait_ge(inv_var, 4)
            for j in range(TT):
                rows = LAST if j == TT - 1 else P
                for k in range(KC):
                    ins = pe.matmul(ps[0:rows, 4, E * j:E * (j + 1)], hn[:, k, j * P:j * P + rows], router[:, k, :],
                                    start=(k == 0), stop=(k == KC - 1))
            ins.then_inc(logits_ps, 1)
            pe.wait_ge(chosen_done, 1)
            for j in range(TT + 1):
                out = ps[:, 5, E * j:E * (j + 1)]
                for i in range(min(j + 1, TT)):
                    ins = pe.matmul(out, tri[:, :] if i == j else ones[:, :], chosen[:, i, :], start=(i == 0),
                                    stop=(i == min(j, TT - 1)))
            ins.then_inc(cum_ps, 1)
            pe.wait_ge(extra_done, 1)
            for s in range(4 * TT):
                j, part_no, half = s // 4, s // 2 % 2, s % 2
                rows = LAST if j == TT - 1 else P
                if s >= 4:
                    pe.wait_ge(tok_copied, s - 3)
                src = (h_hi if part_no == 0 else h_lo)
                for c in range(4):
                    ins = pe.transpose(ps[0:rows, 4 + s % 4, c * P:(c + 1) * P],
                                       src[:, 4 * half + c, j * P:j * P + rows].bitcast(F32), ident[:, :])
                ins.then_inc(tok_turned, 1)
            pe.wait_ge(tok_copied, 4 * TT)

            free = {6: None, 7: None}

            def bank(b):
                if free[b] is not None:
                    pe.wait_ge(*free[b])

            def gather(k):
                pe.wait_ge(sel_made, TT * (k + 1))
                for s in range(4):
                    b = 6 + s % 2
                    bank(b)
                    src = tok_hi if s < 2 else tok_lo
                    for c in range(4):
                        cc = 4 * (s % 2) + c
                        for j in range(TT):
                            ins = pe.matmul(ps[:, b, c * P:(c + 1) * P], src[:, j, cc * P:(cc + 1) * P], sel[:, j, :],
                                            start=(j == 0), stop=(j == TT - 1))
                    ins.then_inc(gather_ps, 1)
                    free[b] = (gathered, 4 * k + s + 1)

            def turn_sel(k, b):
                bank(b)
                for j in range(TT):
                    rows = LAST if j == TT - 1 else P
                    pe.transpose(ps[:, b, j * P:j * P + rows], sel[0:rows, j, :].bitcast(F32), ident[0:rows, 0:rows])
                for j in range(TT):
                    ins = pe.matmul(ps[:, b, T:T + 1], sel[:, j, :].bitcast(F32), gate_e[:, j:j + 1], start=(j == 0),
                                    stop=(j == TT - 1))
                ins.then_inc(selT_ps, 1)
                free[b] = (selT_done, 2 * (k + 1))

            def gate_up(n, s, c, b, groups_read):
                pe.wait_ge(lo_done, n + 1)
                if c == 0 and groups_read is not None:
                    pe.wait_ge(e_hid_done, groups_read)
                out = ps[:, b + c // 2, :]
                for k in range(4):
                    kk = 4 * (c % 2) + k
                    wv = slice(BANK * k, BANK * (k + 1))
                    pe.matmul(out, xs_hi[:, kk, :], w_hi[:, s, wv], start=(kk == 0), stop=False)
                    pe.matmul(out, xs_hi[:, kk, :], w_lo[:, s, wv], start=False, stop=False)
                    ins = pe.matmul(out, xs_lo[:, kk, :], w_hi[:, s, wv], start=False, stop=(kk == KC - 1))
                ins.then_inc(used, 1)

            def turn_hidden(q, b):
                pe.wait_ge(e_hid_done, q + 1)
                bank(b)
                for k in range(GC):
                    ins = pe.transpose(ps[:, b, k * P:(k + 1) * P], e_hid[:, k * P:(k + 1) * P], ident[:, :])
                ins.then_inc(e_turned, 1)
                free[b] = (e_lo_done, q + 1)

            def down(n, s, q, e, g, c):
                pe.wait_ge(lo_done, n + 1)
                if c == 0:
                    pe.wait_ge(e_lo_done, q + 1)
                    if g == 0:
                        pe.wait_ge(y_scaled, HALVES * e)
                for k in range(2):
                    kk = 2 * c + k
                    first, last = g == 0 and kk == 0, g == GROUPS - 1 and kk == GC - 1
                    for half in range(HALVES):
                        out = ps[:, 4 + half, :]
                        wv = slice(d_model * k + half * BANK, d_model * k + (half + 1) * BANK)
                        pe.matmul(out, eh_hi[:, kk, :], w_hi[:, s, wv], start=first, stop=False)
                        pe.matmul(out, eh_hi[:, kk, :], w_lo[:, s, wv], start=False, stop=False)
                        ins = pe.matmul(out, eh_lo[:, kk, :], w_hi[:, s, wv], start=False, stop=last)
                ins.then_inc(used, 1)

            def combine(e, banks):
                pe.wait_ge(y_lo_done, e + 1)
                for c in range(KC):
                    b = banks[c % 2]
                    bank(b)
                    out = ps[:, b, 0:T]
                    pe.matmul(out, y_hi[:, c, :], selT, start=True, stop=False)
                    pe.matmul(out, y_lo[:, c, :], selT, start=False, stop=True).then_inc(comb_ps, 1)
                    free[b] = (combined, KC * e + c + 1)

            plan = misc_plan()

            def expert(e, first, last):
                for b in (6, 7):
                    free[b] = (gathered, 4 * e + b - 3)
                for pos, kind, g in expert_chunks(first):
                    n, s = chunk_no(e, pos, first), slot_of(pos, first) % SPLIT_SLOTS
                    q = pos % 6
                    if q == 1 and (g or not first):
                        turn_hidden(GROUPS * e + g - 1, plan["hid", (g - 1) % GROUPS])
                    if kind == "gu":
                        if pos == 0:
                            pe.wait_ge(gathered, 4 * (e + 1))
                        read = GROUPS * e + g - (1 if g else 0)
                        gate_up(n, s, q, g % 2 * 2, None if first and g < 2 else read)
                    elif g == 0:
                        down(n, s, GROUPS * e - 1, e - 1, GROUPS - 1, q - 4)
                    else:
                        down(n, s, GROUPS * e + g - 1, e, g - 1, q - 4)
                    if pos == 9:
                        if not first:
                            combine(e - 1, plan["comb"])
                        turn_sel(e, plan["selT"])
                    if pos == 6 * (GROUPS - 1) + 4 and not last:
                        gather(e + 1)

            free[6] = free[7] = (tok_copied, 4 * TT)
            gather(0)
            expert(0, True, False)
            with pe.Fori(1, n_exp - 1) as e:
                expert(e, False, False)
            expert(n_exp - 1, False, True)
            q = n_exp * GROUPS - 1
            turn_hidden(q, plan["hid", GROUPS - 1])
            for c in range(2):
                n = M1 - 2 + c
                down(n, n % SPLIT_SLOTS, q, n_exp - 1, GROUPS - 1, c)
            combine(n_exp - 1, (6, 7))

            many = pe.value_load(extra_i[0:1, EXTRA:EXTRA + 1], min_val=0, max_val=EXTRA)
            with pe.If(many > 0):
                with pe.Fori(0, many) as i:
                    k = n_exp + i
                    pe.wait_ge(combined, KC * k)
                    free[6] = free[7] = None
                    pe.wait_ge(sel_made, TT * (k + 1))
                    turn_sel(k, 7)
                    gather(k)
                    pe.wait_ge(gathered, 4 * (k + 1))
                    for g in range(GROUPS):
                        q = GROUPS * k + g
                        for c in range(4):
                            n = M1 + PER_EXPERT * i + 6 * g + c
                            gate_up(n, (M1 + 6 * g + c) % SPLIT_SLOTS, c, 0, q)
                        free[6] = None
                        if g:
                            pe.wait_ge(e_lo_done, q)
                        turn_hidden(q, 6)
                        for c in range(2):
                            n = M1 + PER_EXPERT * i + 6 * g + 4 + c
                            down(n, (M1 + 6 * g + 4 + c) % SPLIT_SLOTS, q, k, g, c)
                    free[6] = free[7] = None
                    combine(k, (6, 7))

            norm_sums(n_norms - 1)
            pe.wait_ge(fin_f, KC)
            for s in range(2 * TT):
                j, half = divmod(s, 2)
                rows = LAST if j == TT - 1 else P
                for c in range(4):
                    ins = pe.transpose(ps[0:rows, s, c * P:(c + 1) * P], hn[:, 4 * half + c, j * P:j * P + rows],
                                       ident[:, :])
                ins.then_inc(fin_ps, 1)



_INS = ["x_prompt", "x_sample", "c_prompt", "c_sample", "state_conv", "state_pool", "w_ada", "b_ada", "g_mix",
        "g_ffn", "w_in", "conv_w", "pool_w", "pool_scale", "g_conv_out", "g_pool_out", "w_out", "dense_w_gate",
        "dense_w_up", "dense_w_down", "router_w", "moe_w_gate", "moe_w_up", "moe_w_down", "g_final"]


def kernel(**inputs):
    import numpy as _np
    import concourse.bacc as _bacc
    from concourse import mybir as _mybir
    from concourse.bass_utils import run_bass_kernel_spmd as _run

    nc = _bacc.Bacc("TRN2", target_bir_lowering=False, num_devices=1)
    arrays, a, o = {}, {}, {}
    for name in _INS:
        v = _np.ascontiguousarray(inputs[name])
        arrays[f"in_{name}_dram"] = v
        a[name] = nc.dram_tensor(f"in_{name}_dram", v.shape, _mybir.dt.from_np(v.dtype), kind="ExternalInput").ap()
    outs = {
        "y_prompt": inputs["x_prompt"].shape, "y_sample": inputs["x_sample"].shape,
        "conv_prompt": (inputs["state_conv"].shape[0], inputs["x_prompt"].shape[0]) + inputs["state_conv"].shape[2:],
        "pool_prompt": (inputs["state_pool"].shape[0], inputs["x_prompt"].shape[0]) + inputs["state_pool"].shape[2:],
        "conv_sample": inputs["state_conv"].shape, "pool_sample": inputs["state_pool"].shape,
    }
    for name, shape in outs.items():
        o[name] = nc.dram_tensor(f"out_{name}_dram", tuple(shape), _mybir.dt.float32, kind="ExternalOutput").ap()
    hybrid_trunk(nc, a, o)
    r = _run(nc, [arrays], core_ids=[0])
    return tuple(r.results[0][f"out_{name}_dram"] for name in outs)
```

```python
from contextlib import ExitStack

import concourse.bass as bass
from concourse import mybir

F32 = mybir.dt.float32
F32R = mybir.dt.float32r
I32 = mybir.dt.int32
ALU = mybir.AluOpType
ACT = mybir.ActivationFunctionType
AX_X = mybir.AxisListType.X

P = 128
EPS = 1e-6
RAW_SLOTS = 6
SPLIT_SLOTS = 3
CHUNK = 2048
BANK = 512
HIST = 15
WINDOWS = (2, 4, 8, 16)
ADA_PARTS = 6
SH1, SC1, GT1, SH2, SC2, GT2 = range(ADA_PARTS)


def hybrid_trunk(nc, a, o):
    depth, d_model, _ = a["w_ada"].shape
    seq = a["x_prompt"].shape[1]
    dec = a["x_sample"].shape[0]
    T = seq + dec
    S = dec + 1
    KC = d_model // P
    GB = a["pool_w"].shape[1]
    d_ff = a["dense_w_gate"].shape[2]
    FC = d_ff // P
    n_exp = a["moe_w_gate"].shape[1]
    d_ffe = a["moe_w_gate"].shape[3]
    GROUPS = d_ffe // BANK
    GC = BANK // P
    TT = -(-T // P)
    LAST = T - (TT - 1) * P
    HALVES = d_model // BANK
    ZU = HIST + seq + dec * (HIST + 1)
    ZV = 2 + seq + dec * 3
    SU = HIST + seq
    SV = 2 + seq
    EXTRA = 4
    assert depth == 2 and GB == 4 and KC == 8 and d_model == 2 * BANK and d_ffe % BANK == 0
    assert (TT - 1) * n_exp >= EXTRA and 2 * T < 5 * (P + 1)

    stream = []

    def cols_256(kind, l, w, rows, j, first=True, last=True, k0=0):
        src = w.rearrange("(k p) n -> p k n", p=P)[:, k0:k0 + rows, 256 * j:256 * j + 256]
        return dict(kind=kind, layer=l, nk=rows, k0=k0, j=j, src=src, first=first, last=last, width=256)

    ADA_Q = KC // 2

    def ada(l, *what):
        return [cols_256("ada", l, a["w_ada"][l], KC, ADA_Q * part + q) for part in what for q in range(ADA_Q)]

    def in_phase(l):
        half = GB // 2
        js = [3 * half + j for j in range(half)] + [half + j for j in range(2 * half)] + list(range(half))
        cs = [cols_256("in", l, a["w_in"][l], KC, j) for j in js]
        cs.insert(3 * half, dict(kind="pool", layer=l, nk=GB, k0=0, j=0, first=True, last=True, width=P,
                                 src=a["pool_w"][l].rearrange("g c d -> c g d")))
        return cs

    def out_phase(l):
        return [cols_256("out", l, a["w_out"][l], KC, j) for j in range(KC // 2)]

    def ffn_phase(l):
        cs = []
        for j in range(FC // 2):
            cs.append(cols_256("gate", l, a["dense_w_gate"][l // 2], KC, j))
            cs.append(cols_256("up", l, a["dense_w_up"][l // 2], KC, j))
        for j in range(KC // 2):
            for k0 in range(0, FC, KC):
                cs.append(cols_256("down", l, a["dense_w_down"][l // 2], min(KC, FC - k0), j,
                                   k0 == 0, k0 + KC >= FC, k0))
        return cs

    phases = [in_phase(0), out_phase(0), ffn_phase(0), in_phase(1), out_phase(1)]
    fillers = [ada(0, SH1, SC1), ada(0, GT1, SH2), ada(0, SC2, GT2), ada(1, SH1, SC1, GT1), ada(1, SH2),
               ada(1, SC2, GT2)]
    for fill, phase in zip(fillers, phases + [[]]):
        stream += fill + phase
    split = [ch for ch in stream if ch["kind"] != "ada"]
    for n, ch in enumerate(stream):
        ch["n"] = n
    for m, ch in enumerate(split):
        ch["m"] = m
    for k, ch in enumerate([ch for ch in stream if ch["kind"] == "ada"]):
        ch["a"] = k
    N_ADA = len(stream) - len(split)
    M0 = len(split)
    PER_EXPERT = 6 * GROUPS
    M1 = M0 + n_exp * PER_EXPERT
    assert N_ADA % RAW_SLOTS == 0

    blocks, taken = [], {"act": 0, "dve": 0}
    for i, ch in enumerate(split):
        if ch["kind"] == "down" and not ch["first"]:
            ch["blocks"] = split[i - 1]["blocks"]
            continue
        ch["blocks"] = []
        for b in range(GB if ch["kind"] == "pool" else 2):
            col = b if ch["kind"] == "pool" else 2 * ch["j"] + b
            eng = "dve"
            if ch["kind"] in ("gate", "pool") or ch["kind"] == "in" and (col >= 3 * GB or GB <= col < 2 * GB):
                eng = "act"
            taken[eng] += 1
            ch["blocks"].append(len(blocks))
            blocks.append(dict(eng=eng, count=taken[eng], col=col))
    n_norms = 2 * depth + 1

    ctx = ExitStack()
    with ctx:
        def sb(name, shape, dt=F32):
            return ctx.enter_context(nc.sbuf_tensor(name, shape, dt))

        def sem(name):
            return ctx.enter_context(nc.semaphore(name))

        raw = sb("raw", [P, RAW_SLOTS, CHUNK])
        w_hi = sb("w_hi", [P, SPLIT_SLOTS, CHUNK], F32R)
        w_lo = sb("w_lo", [P, SPLIT_SLOTS, CHUNK], F32R)
        xT = sb("xT", [P, KC, T])
        h_hi = sb("h_hi", [P, KC, T], F32R)
        h_lo = sb("h_lo", [P, KC, T], F32R)
        parts = sb("parts", [P, 2 * FC * T], F32R)
        work = sb("work", [P, 8192])
        modT = sb("modT", [P, depth, ADA_PARTS * KC, S])
        par = sb("par", [P, 184])
        ident = sb("ident", [P, P])
        ones = sb("ones", [P, P])
        slot_no = sb("slot_no", [P, P])
        silu_c = sb("silu_c", [P, KC, S])
        last_rows = sb("last_rows", [P, GB, HIST + dec + 2 + 2 * dec])
        ROWS = HIST + dec + 2 + 2 * dec

        hid_hi = parts[:, 0:FC * T].rearrange("p (k t) -> p k t", t=T)
        hid_lo = parts[:, FC * T:2 * FC * T].rearrange("p (k t) -> p k t", t=T)

        at = 0

        def part(n):
            nonlocal at
            at += n
            assert at <= 2 * FC * T
            return parts[:, at - n:at]

        tok_hi = part(TT * d_model).rearrange("p (j d) -> p j d", j=TT)
        tok_lo = part(TT * d_model).rearrange("p (j d) -> p j d", j=TT)
        sel = part(TT * 2 * P).rearrange("p (j s) -> p j s", j=TT)
        selT = part(T)
        eh_hi = part(GC * P).rearrange("p (k s) -> p k s", k=GC)
        eh_lo = part(GC * P).rearrange("p (k s) -> p k s", k=GC)
        y_hi = part(d_model).rearrange("p (c d) -> p c d", c=KC)
        y_lo = part(d_model).rearrange("p (c d) -> p c d", c=KC)
        xs_hi = h_hi[:, :, 0:2 * P]
        xs_lo = h_lo[:, :, 0:2 * P]

        x_rows = work[:, 0:3 * d_model].rearrange("p (j d) -> p j d", j=3)
        c_rows = work[:, 3 * d_model:4 * d_model]
        par_rows = work[:, 4 * d_model:4 * d_model + 2 * P].rearrange("p (j d) -> p j d", j=2)
        zu = work[:, 0:GB * ZU].rearrange("p (b z) -> p b z", b=GB)
        at_v = GB * ZU
        zv = work[:, at_v:at_v + GB * ZV].rearrange("p (b z) -> p b z", b=GB)
        at_b = at_v + GB * ZV
        b_gate = work[:, at_b:at_b + GB * T].rearrange("p (b t) -> p b t", b=GB)
        at_c = at_b + GB * T
        c_gate = work[:, at_c:at_c + GB * T].rearrange("p (b t) -> p b t", b=GB)
        at_s = at_c + GB * T
        conv = b_gate
        diff = parts[:, 0:2 * GB * T].rearrange("p (h b t) -> p h b t", h=2, b=GB)
        sum_a = work[:, at_s:at_s + GB * ZU].rearrange("p (b z) -> p b z", b=GB)
        at_t = at_s + GB * ZU
        sum_b = work[:, at_t:at_t + 3 * ZU].rearrange("p (b z) -> p b z", b=3)
        at_w = at_t + 3 * ZU
        scr = work[:, at_w:at_w + 2 * (ZV - 2)].rearrange("p (b z) -> p b z", b=2)
        assert at_w + 2 * (ZV - 2) <= 8192
        y_pool = work[:, at_s:at_s + GB * T].rearrange("p (b t) -> p b t", b=GB)
        msq = work[:, at_t:at_t + 2 * T].rearrange("p (b t) -> p b t", b=2)
        mix_squares = work[:, at_t + 2 * T:at_t + 4 * T].rearrange("p (b t) -> p b t", b=2)
        assert at_t + 4 * T <= at_w
        pool_rows = work[:, at_s:at_s + BANK]
        conv_rows = work[:, at_t:at_t + BANK]
        new_rows = work[:, at_s + GB * T:at_s + GB * T + BANK]
        sq = work[:, 0:KC * T].rearrange("p (c t) -> p c t", c=KC)
        hn = work[:, KC * T:2 * KC * T].rearrange("p (c t) -> p c t", c=KC)
        rstd = work[:, at_w:at_w + T]
        var = work[:, at_w + T:at_w + 2 * T]
        silu_g = work[:, 0:2 * 2 * T].rearrange("p (b t) -> p b t", b=4)
        hid_f = work[:, 4 * T:4 * T + 2 * T].rearrange("p (b t) -> p b t", b=2)
        acc = work[:, 0:KC * T].rearrange("p (c t) -> p c t", c=KC)
        e_silu = work[:, 2112:2112 + BANK]
        e_hid = work[:, 2624:2624 + BANK]
        y_f = work[:, 3136:3136 + d_model]
        assert KC * T <= 2112
        r0 = 2 * KC * T
        E = n_exp
        logit = work[:, r0:r0 + TT * E].rearrange("p (j e) -> p j e", j=TT)
        r0 += TT * E
        cmp1 = work[:, r0:r0 + TT * E * E].rearrange("p (j e f) -> p j e f", j=TT, e=E)
        r0 += TT * E * E
        cmp2 = work[:, r0:r0 + TT * E * E].rearrange("p (j e f) -> p j e f", j=TT, e=E)
        r0 += TT * E * E
        rank = work[:, r0:r0 + TT * E].rearrange("p (j e) -> p j e", j=TT)
        r0 += TT * E
        chosen = work[:, r0:r0 + TT * E].rearrange("p (j e) -> p j e", j=TT)
        r0 += TT * E
        lmax = work[:, r0:r0 + TT]
        lsum = work[:, r0 + TT:r0 + 2 * TT]
        r0 += 2 * TT
        earlier = work[:, r0:r0 + E * E].rearrange("p (e f) -> p e f", e=E)
        r0 += E * E
        real = work[:, r0:r0 + TT]
        r0 += TT
        gate = work[:, r0:r0 + E * TT].rearrange("p (e j) -> p e j", e=E)
        r0 += TT * E
        place = work[:, r0:r0 + E * TT].rearrange("p (e j) -> p e j", e=E)
        r0 += TT * E
        place_e = work[:, r0:r0 + 2 * TT].rearrange("p (e j) -> p e j", e=2)
        gate_e = work[:, r0 + 2 * TT:r0 + 4 * TT].rearrange("p (e j) -> p e j", e=2)
        gate_slot = work[:, r0 + 4 * TT:r0 + 4 * TT + 1]
        r0 += 4 * TT + 1
        tri = work[:, 6800:6800 + P]
        logitT = work[0:E, 7000:7000 + T]
        assert r0 <= 6800 and 7000 + T <= at_w
        NX = (TT - 1) * E
        more = work[:, r0:r0 + NX].rearrange("p (j e) -> p j e", e=E)
        more_row = work[:, r0:r0 + NX]
        more_no = work[:, r0 + NX:r0 + 2 * NX]
        tmp_row = work[:, r0 + 2 * NX:r0 + 3 * NX]
        code_e = work[:, r0 + 3 * NX:r0 + 4 * NX]
        code_s = work[:, r0 + 4 * NX:r0 + 5 * NX]
        r0 += 5 * NX
        hit = work[:, r0:r0 + EXTRA * NX].rearrange("p (i k) -> p i k", i=EXTRA)
        hit2 = work[:, r0 + EXTRA * NX:r0 + 2 * EXTRA * NX].rearrange("p (i k) -> p i k", i=EXTRA)
        r0 += 2 * EXTRA * NX
        extra_shift = work[:, r0:r0 + EXTRA]
        extra_f = work[:, r0 + EXTRA:r0 + 2 * EXTRA + 1]
        r0 += 2 * EXTRA + 1
        assert r0 <= at_w, (r0, at_w)
        m_hi_t = parts[:, 2 * GB * T:2 * GB * T + KC * T].rearrange("p (k t) -> p k t", t=T)
        m_lo_t = parts[:, 2 * GB * T + KC * T:2 * GB * T + 2 * KC * T].rearrange("p (k t) -> p k t", t=T)
        fix = sb("fix", [P, GB, HIST + 1])
        extra_i = sb("extra_i", [P, EXTRA + 1], I32)
        ada_rows = sb("ada_rows", [S, BANK])
        iota_i = work[:, 4 * d_model + 2 * P:4 * d_model + 3 * P].bitcast(I32)
        router = sb("router", [P, KC, E])
        y_rows = work[:, 2 * KC * T:2 * KC * T + TT * d_model].rearrange("p (j d) -> p j d", j=TT)

        ps = ctx.enter_context(nc.psum_tensor("ps", [P, 8, BANK], F32))

        PAR_ROWS = 88
        G_MIX, G_FFN, G_FIN, CONV, PSC, GCO, GPO, BADA = 96, 112, 128, 136, 160, 168, 176, 0

        def pcol(i, n=1):
            return par[:, i:i + n]

        raw_in = [sem(f"raw_in{i}") for i in range(RAW_SLOTS)]
        hi_done = sem("hi_done")
        lo_done = sem("lo_done")
        used = sem("used")
        c_in = sem("c_in")
        x_in = sem("x_in")
        par_in = sem("par_in")
        states_in = [sem(f"states_in{l}") for l in range(depth)]
        router_in = sem("router_in")
        consts = sem("consts")
        pool_step = sem("pool_step")
        dve_step = sem("dve_step")
        act_step = sem("act_step")
        c_silu = sem("c_silu")
        turned = sem("turned")
        c_done = sem("c_done")
        ada_used = sem("ada_used")
        ada_copied = sem("ada_copied")
        ada_turned = sem("ada_turned")
        ada_out = sem("ada_out")
        par_done = sem("par_done")
        x_done = sem("x_done")
        x_last = sem("x_last")
        turned_out = sem("turned_out")
        squares = sem("squares")
        sums = sem("sums")
        inv_var = sem("inv_var")
        rstd_done = sem("rstd_done")
        normed = sem("normed")
        h_hi_done = sem("h_hi_done")
        h_lo_done = sem("h_lo_done")
        act_took = sem("act_took")
        dve_took = sem("dve_took")
        ffn_hi = sem("ffn_hi")
        ffn_lo = sem("ffn_lo")
        state_turned = sem("state_turned")
        state_put = sem("state_put")
        diff_done = sem("diff_done")
        diff_hi = sem("diff_hi")
        diff_lo = sem("diff_lo")
        mix_sq = sem("mix_sq")
        mix_inv = sem("mix_inv")
        mix_rstd = sem("mix_rstd")
        m_f = sem("m_f")
        m_hi = sem("m_hi")
        m_lo = sem("m_lo")
        tails = sem("tails")
        tails_turned = sem("tails_turned")
        tails_out = sem("tails_out")
        out_dma = sem("out_dma")
        shift_dma = sem("shift_dma")
        sq_used = sem("sq_used")
        logits_ps = sem("logits_ps")
        logits_row = sem("logits_row")
        logits_turned = sem("logits_turned")
        chosen_done = sem("chosen_done")
        cum_ps = sem("cum_ps")
        route_exp = sem("route_exp")
        route_max = sem("route_max")
        extra_done = sem("extra_done")
        tok_turned = sem("tok_turned")
        tok_copied = sem("tok_copied")
        tok_zero = sem("tok_zero")
        acc_zero = sem("acc_zero")
        sel_made = sem("sel_made")
        place_made = sem("place_made")
        gather_ps = sem("gather_ps")
        gathered = sem("gathered")
        e_silu_done = sem("e_silu_done")
        e_hid_done = sem("e_hid_done")
        e_turned = sem("e_turned")
        e_hi_done = sem("e_hi_done")
        e_lo_done = sem("e_lo_done")
        y_scaled = sem("y_scaled")
        y_hi_done = sem("y_hi_done")
        y_lo_done = sem("y_lo_done")
        selT_ps = sem("selT_ps")
        selT_done = sem("selT_done")
        comb_ps = sem("comb_ps")
        combined = sem("combined")
        fin_f = sem("fin_f")
        fin_ps = sem("fin_ps")
        fin_out = sem("fin_out")
        y_dma = sem("y_dma")

        block = ctx.enter_context(nc.Block())

        def slot_reader(ch):
            return (ada_used, ch["a"] + 1) if ch["kind"] == "ada" else (lo_done, ch["m"] + 1)

        def part_end(ch):
            return ch["j"] // ADA_Q if ch["j"] % ADA_Q == ADA_Q - 1 else None

        def count_of(kind, l, col):
            return next(blocks[b]["count"] for ch in split if ch["kind"] == kind and ch["layer"] == l
                        for b in ch["blocks"] if blocks[b]["col"] == col)

        def misc_plan():
            return {("hid", GROUPS - 1): 6, ("hid", 0): 7, "comb": (6, 7), "selT": 6,
                    **{("hid", g): 7 if g % 2 else 6 for g in range(1, GROUPS - 1)}}

        def group_end(e, g, first):
            return (M0 + 3 if first and g == 0 else M0 - 2 + PER_EXPERT * e + 6 * g + 3) + 1

        def expert_end(e):
            return M0 - 2 + PER_EXPERT * (e + 1) + 6

        def expert_chunks(first):
            for pos in range(PER_EXPERT):
                g, q = divmod(pos, 6)
                if q >= 4 and g == 0 and first:
                    continue
                yield pos, ("gu" if q < 4 else "down"), g

        def chunk_no(e, pos, first):
            if first and pos < 4:
                return M0 + pos
            return M0 - 2 + PER_EXPERT * e + pos

        def slot_of(pos, first):
            return (M0 + pos) % 6 if first and pos < 4 else (M0 - 2 + pos) % 6

        NORM_H = 2

        @block.sync
        def _(sp):
            sp.dma_start(c_rows[0:1, :], a["c_prompt"]).then_inc(c_in, 16)
            sp.dma_start(c_rows[1:S, :], a["c_sample"]).then_inc(c_in, 16)
            sp.dma_start(x_rows[:, 0:seq // P, :], a["x_prompt"][0].rearrange("(j p) d -> p j d", p=P))\
                .then_inc(x_in, 16)
            sp.dma_start(x_rows[0:dec, seq // P, :], a["x_sample"].rearrange("b s d -> (b s) d")).then_inc(x_in, 16)

            def load(m, slot, dst, src):
                if isinstance(m, int) and m < M0 + RAW_SLOTS:
                    sp.wait_ge(*slot_reader(stream[len(stream) - RAW_SLOTS + m - M0]))
                else:
                    sp.wait_ge(lo_done, m - RAW_SLOTS + 1)
                sp.dma_start(dst, src).then_inc(raw_in[slot], 16)

            for n, ch in enumerate(stream):
                if n >= RAW_SLOTS:
                    sp.wait_ge(*slot_reader(stream[n - RAW_SLOTS]))
                w = ch["width"]
                sp.dma_start(raw[:, n % RAW_SLOTS, 0:ch["nk"] * w].rearrange("p (k m) -> p k m", m=w), ch["src"])\
                    .then_inc(raw_in[n % RAW_SLOTS], 16)

            wg = a["moe_w_gate"][0].rearrange("e (k p) n -> e p k n", p=P)
            wu = a["moe_w_up"][0].rearrange("e (k p) n -> e p k n", p=P)
            wd = a["moe_w_down"][0].rearrange("e (k p) n -> e p k n", p=P)

            def gate_up(n, slot, e, g, q):
                w = (wg if q < 2 else wu)[e, :, 4 * (q % 2):4 * (q % 2) + 4, BANK * g:BANK * (g + 1)]
                load(n, slot, raw[:, slot, :].rearrange("p (k m) -> p k m", k=4), w)

            def down(n, slot, e, g, q):
                w = wd[e, :, GC * g + 2 * q:GC * g + 2 * q + 2, :]
                load(n, slot, raw[:, slot, :].rearrange("p (k m) -> p k m", k=2), w)

            def expert(e, first):
                for pos, kind, g in expert_chunks(first):
                    n, s, q = chunk_no(e, pos, first), slot_of(pos, first), pos % 6
                    if kind == "gu":
                        gate_up(n, s, e, g, q)
                    elif g == 0:
                        down(n, s, e - 1, GROUPS - 1, q - 4)
                    else:
                        down(n, s, e, g - 1, q - 4)

            expert(0, True)
            with sp.Fori(1, n_exp) as e:
                expert(e, False)
            for q in range(2):
                down(M1 - 2 + q, (M1 - 2 + q) % 6, n_exp - 1, GROUPS - 1, q)

            sp.wait_ge(extra_done, 1)
            many = sp.value_load(extra_i[0:1, EXTRA:EXTRA + 1], min_val=0, max_val=EXTRA)
            with sp.If(many > 0):
                with sp.Fori(0, many) as i:
                    e = sp.value_load(extra_i[0:1, bass.ds(i, 1)], min_val=0, max_val=n_exp - 1)
                    for pos in range(PER_EXPERT):
                        g, q = divmod(pos, 6)
                        n, s = M1 + PER_EXPERT * i + pos, (M1 + pos) % 6
                        if q < 4:
                            gate_up(n, s, e, g, q)
                        else:
                            down(n, s, e, g, q - 4)

        @block.gpsimd
        def _(pool):
            steps = [0]

            def link(ins):
                steps[0] += 1
                ins.then_inc(pool_step, 1)
                pool.wait_ge(pool_step, steps[0])

            link(pool.memset(ident[:, :], 0.0))
            link(pool.affine_select(out=ident[:, :], in_=ident[:, :], compare_op=ALU.not_equal, fill=1.0, base=0,
                                    pattern=[[-1, P]], channel_multiplier=1))
            pool.memset(ones[:, :], 1.0).then_inc(consts, 1)
            link(pool.iota(iota_i, pattern=[[1, P]], base=0, channel_multiplier=0))
            link(pool.tensor_copy(slot_no[:, :], iota_i))
            for g, w in enumerate(WINDOWS):
                link(pool.tensor_scalar(fix[:, g, :], slot_no[:, 0:HIST + 1], 1.0, float(w), ALU.add, ALU.min))
            pool.engine_nop().then_inc(consts, 1)
            pool.dma_start(router[:, :, :], a["router_w"][0].rearrange("(k p) e -> p k e", p=P)).then_inc(router_in, 16)

            for l in range(depth):
                pool.dma_start(o["pool_sample"][l, :, 0:HIST - 1, :], a["state_pool"][l, :, 1:HIST, :])\
                    .then_inc(shift_dma, 16)
            for l in range(depth):
                pool.wait_ge(act_took, count_of("in", l, 4 * GB - 1))
                pool.wait_ge(dve_took, count_of("in", l, 3 * GB - 1))
                pool.wait_ge(state_put, 2 * (l + 1))
                if l:
                    pool.wait_ge(tails_turned, l)
                pool.tensor_copy(last_rows[:, :, 0:HIST], zu[:, :, seq:seq + HIST]).then_inc(tails, 1)
                us = zu[:, :, SU:].rearrange("p b (s r) -> p b s r", r=HIST + 1)
                pool.tensor_copy(last_rows[:, :, HIST:HIST + dec], us[:, :, :, HIST]).then_inc(tails, 1)
                o1 = HIST + dec
                pool.tensor_copy(last_rows[:, :, o1:o1 + 2], zv[:, :, seq:seq + 2]).then_inc(tails, 1)
                vs = zv[:, :, SV:].rearrange("p b (s r) -> p b s r", r=3)
                pool.tensor_copy(last_rows[:, :, o1 + 2:o1 + 2 + 2 * dec].rearrange("p b (s r) -> p b s r", r=2),
                                 vs[:, :, :, 1:3]).then_inc(tails, 1)

            pool.wait_ge(tails_out, depth)
            pool.wait_ge(m_lo, 2 * depth)
            pool.wait_ge(out_dma, 64 * depth)
            link(pool.memset(tri, 0.0))
            link(pool.affine_select(out=tri, in_=tri, compare_op=ALU.is_ge, fill=1.0, base=0,
                                    pattern=[[-1, P]], channel_multiplier=1))
            link(pool.memset(earlier, 0.0))
            link(pool.affine_select(out=earlier, in_=earlier, compare_op=ALU.is_ge, fill=1.0, base=0,
                                    pattern=[[-1, E], [1, E]], channel_multiplier=0))
            link(pool.memset(real, 1.0))
            link(pool.affine_select(out=real[:, TT - 1:TT], in_=real[:, TT - 1:TT], compare_op=ALU.is_gt, fill=0.0,
                                    base=LAST, pattern=[[0, 1]], channel_multiplier=-1))
            link(pool.memset(logit, 0.0))
            pool.iota(code_e.bitcast(I32).rearrange("p (j e) -> p j e", e=E), pattern=[[0, TT - 1], [1, E]], base=0,
                      channel_multiplier=0).then_inc(pool_step, 1)
            pool.iota(code_s.bitcast(I32).rearrange("p (j e) -> p j e", e=E), pattern=[[P, TT - 1], [0, E]], base=P,
                      channel_multiplier=0).then_inc(pool_step, 1)
            steps[0] += 2
            pool.wait_ge(pool_step, steps[0])
            link(pool.tensor_copy(tmp_row, code_e.bitcast(I32)))
            link(pool.tensor_copy(code_e, tmp_row))
            link(pool.tensor_copy(tmp_row, code_s.bitcast(I32)))
            link(pool.tensor_copy(code_s, tmp_row))
            pool.wait_ge(sums, 4)
            link(pool.memset(tok_hi[:, TT - 1, :].bitcast(F32), 0.0))
            link(pool.memset(tok_lo[:, TT - 1, :].bitcast(F32), 0.0))
            pool.engine_nop().then_inc(tok_zero, 1)
            pool.memset(acc, 0.0).then_inc(acc_zero, 1)
            pool.wait_ge(shift_dma, 16 * depth)

        @block.scalar
        def _(act):
            steps = [0]

            def link(ins):
                steps[0] += 1
                ins.then_inc(act_step, 1)
                act.wait_ge(act_step, steps[0])

            act.dma_start(par_rows[0:depth * ADA_PARTS * KC, 0, :],
                          a["b_ada"].rearrange("l (j p) -> (l j) p", p=P)).then_inc(par_in, 16)
            small = [("g_mix", "l (j p) -> (l j) p"), ("g_ffn", "l (j p) -> (l j) p"), ("g_final", "(j p) -> j p"),
                     ("conv_w", "l k (j p) -> (l k j) p"), ("pool_scale", "l (j p) -> (l j) p"),
                     ("g_conv_out", "l (j p) -> (l j) p"), ("g_pool_out", "l (j p) -> (l j) p")]
            r = 0
            for name, pattern in small:
                v = a[name].rearrange(pattern, p=P)
                act.dma_start(par_rows[r:r + v.shape[0], 1, :], v).then_inc(par_in, 16)
                r += v.shape[0]
            assert r == PAR_ROWS

            def load_states(l):
                act.dma_start(pool_rows[0:dec * HIST, :], a["state_pool"][l].rearrange("b r c -> (b r) c"))\
                    .then_inc(states_in[l], 16)
                act.dma_start(conv_rows[0:dec * 2, :], a["state_conv"][l].rearrange("b r c -> (b r) c"))\
                    .then_inc(states_in[l], 16)

            load_states(0)
            act.wait_ge(c_in, 32)
            act.activation(c_rows[0:S, :], c_rows[0:S, :], ACT.Silu).then_inc(c_silu, 1)
            act.wait_ge(turned, 1)
            act.activation(silu_c[:, :, :], ps[:, 4, 0:KC * S].rearrange("p (k s) -> p k s", k=KC), ACT.Copy)\
                .then_inc(c_done, 1)

            def hi(m, slot, width=CHUNK):
                if not isinstance(m, int) or m >= SPLIT_SLOTS:
                    act.wait_ge(used, m - SPLIT_SLOTS + 1)
                act.activation(w_hi[:, slot % SPLIT_SLOTS, 0:width], raw[:, slot, 0:width], ACT.Copy)\
                    .then_inc(hi_done, 1)

            def landed(slot, turn):
                act.wait_ge(raw_in[slot], 16 * (turn + 1))

            def hi_of(ch):
                n, m, width = ch["n"], ch["m"], ch["nk"] * ch["width"]
                landed(n % RAW_SLOTS, n // RAW_SLOTS)
                if m >= SPLIT_SLOTS:
                    act.wait_ge(used, m - SPLIT_SLOTS + 1)
                act.activation(w_hi[:, m % SPLIT_SLOTS, 0:width], raw[:, n % RAW_SLOTS, 0:width], ACT.Copy)\
                    .then_inc(hi_done, 1)

            def ada_pairs(chunks):
                for k in sorted({ch["a"] // 2 for ch in chunks}):
                    act.wait_ge(ada_used, 2 * k + 2)
                    if k:
                        act.wait_ge(ada_turned, k)
                    act.activation(ada_rows[:, :], ps[0:S, 6 + k % 2, :], ACT.Copy).then_inc(ada_copied, 1)

            def square(c):
                act.activation(sq[:, c, :], xT[:, c, :], ACT.Square).then_inc(squares, 1)

            def root(k):
                act.wait_ge(inv_var, k + 1)
                act.activation(rstd, var, ACT.Sqrt).then_inc(rstd_done, 1)

            def norm_hi(k):
                for half in range(NORM_H):
                    c0, c1 = half * KC // NORM_H, (half + 1) * KC // NORM_H
                    act.wait_ge(normed, NORM_H * k + half + 1)
                    act.activation(h_hi[:, c0:c1, :], hn[:, c0:c1, :], ACT.Copy).then_inc(h_hi_done, 1)

            def mix_square(l, b, count):
                if count:
                    act.wait_ge(sq_used, count)
                src = y_pool[:, b - GB, :] if b >= GB else conv[:, b, :]
                act.activation(mix_squares[:, b % 2, :], src, ACT.Square).then_inc(mix_sq, 1)

            def take(ch):
                l, kind = ch["layer"], ch["kind"]
                act.wait_ge(used, ch["m"] + 1)
                for b in ch["blocks"]:
                    blk, col = blocks[b], blocks[b]["col"]
                    src = ps[:, b % 4, 0:T]
                    if kind in ("out", "down") and ch["last"]:
                        act.wait_ge(dve_took, blk["count"])
                        square(col)
                    elif blk["eng"] != "act":
                        continue
                    elif kind == "in" and col < 2 * GB:
                        act.activation(c_gate[:, col - GB, :], src, ACT.Copy).then_inc(act_took, 1)
                    elif kind == "in":
                        u = col - 3 * GB
                        us = zu[:, u, SU:].rearrange("p (s r) -> p s r", r=HIST + 1)
                        link(act.activation(us[:, :, HIST], src[:, seq:T], ACT.Copy))
                        act.activation(zu[:, u, HIST:SU], src[:, 0:seq], ACT.Copy).then_inc(act_took, 1)
                    elif kind == "gate":
                        if ch["j"] >= 2:
                            act.wait_ge(dve_took, count_of("up", l, col - 4))
                        act.activation(silu_g[:, 2 * (ch["j"] % 2) + col % 2, :], src, ACT.Silu)\
                            .then_inc(act_took, 1)
                    elif kind == "pool":
                        act.activation(y_pool[:, col, :], src, ACT.Copy, scale=pcol(PSC + GB * l + col))\
                            .then_inc(act_took, 1)
                if kind == "pool":
                    act.wait_ge(act_took, count_of("pool", l, GB - 1))
                    for b in range(GB):
                        mix_square(l, GB + b, 2 * GB * l + b - 1 if b >= 2 else 2 * GB * l)
                if kind == "up":
                    for b in range(2):
                        f = 2 * ch["j"] + b
                        act.wait_ge(dve_took, count_of("up", l, f))
                        act.activation(hid_hi[:, f, :], hid_f[:, b, :], ACT.Copy).then_inc(ffn_hi, 1)

            def diff_hi_of(l, g):
                act.wait_ge(diff_done, GB * l + g + 1)
                act.activation(diff[:, 0, g, :], scr[:, g % 2, 0:T], ACT.Copy).then_inc(diff_hi, 1)

            def mix_root(l, half):
                act.wait_ge(mix_inv, 2 * l + half + 1)
                act.activation(msq[:, half, :], msq[:, half, :], ACT.Sqrt).then_inc(mix_rstd, 1)

            def mix_hi(l, half):
                act.wait_ge(m_f, 2 * l + half + 1)
                for b in range(GB):
                    src, g = (conv, GCO) if half else (y_pool, GPO)
                    ins = act.activation(m_hi_t[:, (GB if half == 0 else 0) + b, :], src[:, b, :], ACT.Copy,
                                         scale=pcol(g + GB * l + b))
                ins.then_inc(m_hi, 1)

            def tails_scalar(l):
                act.wait_ge(tails_turned, l + 1)
                if l:
                    act.wait_ge(out_dma, 64 * l)
                act.activation(new_rows[0:ROWS, :], ps[0:ROWS, 5, :], ACT.Copy).then_inc(tails_out, 1)
                act.wait_ge(tails_out, l + 1)
                o1 = HIST + dec
                act.dma_start(o["pool_prompt"][l, 0], new_rows[0:HIST, :]).then_inc(out_dma, 16)
                act.dma_start(o["pool_sample"][l, :, HIST - 1, :], new_rows[HIST:o1, :]).then_inc(out_dma, 16)
                act.dma_start(o["conv_prompt"][l, 0], new_rows[o1:o1 + 2, :]).then_inc(out_dma, 16)
                act.dma_start(o["conv_sample"][l].rearrange("b r c -> (b r) c"), new_rows[o1 + 2:ROWS, :])\
                    .then_inc(out_dma, 16)

            def begin(phase, fill):
                ada_pairs(fill[:2])
                for ch in phase[:2]:
                    hi_of(ch)
                ada_pairs(fill[2:])
                hi_of(phase[2])

            def phase_in(l, phase):
                for i, ch in enumerate(phase):
                    if i >= SPLIT_SLOTS:
                        hi_of(ch)
                        take(phase[i - SPLIT_SLOTS])
                    if i == 5:
                        diff_hi_of(l, 0)
                        diff_hi_of(l, 1)
                    if i == 6:
                        diff_hi_of(l, 2)
                        diff_hi_of(l, 3)
                take(phase[6])
                mix_root(l, 0)
                mix_hi(l, 0)
                for b in range(GB):
                    act.wait_ge(dve_took, count_of("in", l, b))
                    mix_square(l, b, 2 * GB * l + GB + b - 1 if b >= 2 else 2 * GB * l + GB)
                mix_root(l, 1)
                mix_hi(l, 1)

            def phase_rest(phase):
                for i, ch in enumerate(phase):
                    if i >= SPLIT_SLOTS:
                        hi_of(ch)
                        take(phase[i - SPLIT_SLOTS])
                for ch in phase[-SPLIT_SLOTS:]:
                    take(ch)

            act.wait_ge(x_done, 1)
            for c in range(KC):
                square(c)
            act.wait_ge(turned, 3)
            act.activation(par[:, 0:96], ps[:, 5, 0:96], ACT.Copy).then_inc(par_done, 1)
            act.activation(par[:, 96:96 + PAR_ROWS], ps[:, 5, 96:96 + PAR_ROWS], ACT.Copy).then_inc(par_done, 1)
            root(0)
            ada_pairs(fillers[0])
            norm_hi(0)
            begin(phases[0], [])
            phase_in(0, phases[0])
            ada_pairs(fillers[1][:4])
            tails_scalar(0)
            begin(phases[1], fillers[1][4:])
            act.wait_ge(m_lo, 2)
            load_states(1)
            phase_rest(phases[1])
            root(1)
            ada_pairs(fillers[2][:4])
            norm_hi(1)
            begin(phases[2], fillers[2][4:])
            phase_rest(phases[2])
            root(2)
            ada_pairs(fillers[3][:8])
            norm_hi(2)
            begin(phases[3], fillers[3][8:])
            phase_in(1, phases[3])
            tails_scalar(1)
            begin(phases[4], fillers[4])
            phase_rest(phases[4])
            root(3)
            ada_pairs(fillers[5][:4])
            norm_hi(3)
            act.wait_ge(logits_ps, 1)
            act.activation(logitT, ps[0:E, 4, 0:T], ACT.Copy).then_inc(logits_row, 1)

            def landed_m(slot, turn):
                landed(slot, turn + N_ADA // RAW_SLOTS)

            def take_tokens(s0, s1):
                for s in range(s0, s1):
                    j, part_no, half = s // 4, s // 2 % 2, s % 2
                    rows = LAST if j == TT - 1 else P
                    act.wait_ge(tok_turned, s + 1)
                    dst = (tok_hi if part_no == 0 else tok_lo)[0:rows, j, half * BANK:(half + 1) * BANK]
                    act.activation(dst, ps[0:rows, s % 4, :], ACT.Copy).then_inc(tok_copied, 1)

            act.wait_ge(tok_zero, 1)
            take_tokens(0, 4 * TT)
            act.wait_ge(route_max, 1)
            act.wait_ge(chosen_done, 1)
            act.activation(rank, logit, ACT.Exp).then_inc(route_exp, 1)
            ada_pairs(fillers[5][4:])
            for k in range(SPLIT_SLOTS):
                landed_m((M0 + k) % 6, (M0 + k) // 6)
                hi(M0 + k, (M0 + k) % 6)

            def take_gather(e, width=2 * P):
                for s in range(8):
                    act.wait_ge(gather_ps, 8 * e + s + 1)
                    dst = (xs_hi if s < 4 else xs_lo)[:, 2 * (s % 4):2 * (s % 4) + 2, 0:width]
                    src = ps[:, 6 + s % 2, :].rearrange("p (c s) -> p c s", c=2)[:, :, 0:width]
                    act.activation(dst, src, ACT.Copy).then_inc(gathered, 1)

            def silu(q, bank, ready):
                act.wait_ge(used, ready)
                act.wait_ge(e_hid_done, q)
                act.activation(e_silu, ps[:, bank, :], ACT.Silu).then_inc(e_silu_done, 1)

            def split_hidden(q, bank):
                act.wait_ge(e_turned, q + 1)
                act.activation(eh_hi, ps[:, bank, :].rearrange("p (k s) -> p k s", k=GC), ACT.Copy)\
                    .then_inc(e_hi_done, 1)

            def scale_y(e, ready):
                act.wait_ge(used, ready)
                for half in range(HALVES):
                    act.activation(y_f[:, half * BANK:(half + 1) * BANK], ps[:, 4 + half, :], ACT.Copy,
                                   scale=gate_slot).then_inc(y_scaled, 1)
                act.wait_ge(y_scaled, HALVES * (e + 1))
                act.activation(y_hi, y_f.rearrange("p (c d) -> p c d", c=KC), ACT.Copy).then_inc(y_hi_done, 1)

            def take_selT(e, bank):
                act.wait_ge(selT_ps, e + 1)
                act.activation(selT, ps[:, bank, 0:T], ACT.Copy).then_inc(selT_done, 1)
                act.activation(gate_slot, ps[:, bank, T:T + 1], ACT.Copy).then_inc(selT_done, 1)

            plan = misc_plan()

            def expert(e, first, gather=None, split_before=0):
                for pos, kind, g in expert_chunks(first):
                    n, s = chunk_no(e, pos, first), slot_of(pos, first)
                    if not (first and pos < split_before):
                        landed_m(s, n // 6 if isinstance(n, int) else (M0 - 2 + pos) // 6 + GROUPS * e)
                        hi(n, s)
                    if pos % 6 == 0 and (pos or not first):
                        silu(GROUPS * e + g - 1, (g - 1) % GROUPS % 2 * 2, group_end(e, g - 1, first))
                    if pos == 0 and gather is not None:
                        take_gather(gather)
                    if pos % 6 == 3 and (pos > 3 or not first):
                        split_hidden(GROUPS * e + g - 1, plan["hid", (g - 1) % GROUPS])
                    if pos == 8 and not first:
                        scale_y(e - 1, expert_end(e - 1))
                    if pos == 13:
                        take_selT(e, plan["selT"])

            take_gather(0)
            expert(0, True, None, SPLIT_SLOTS)
            expert(1, False)
            with act.Fori(1, n_exp // 2) as pair:
                expert(2 * pair, False, pair)
                expert(2 * pair + 1, False)
            for q in range(2):
                n = M1 - 2 + q
                landed_m(n % 6, n // 6)
                hi(n, n % 6)
                if q == 0:
                    silu(n_exp * GROUPS - 1, (GROUPS - 1) % 2 * 2, group_end(n_exp, -1, False))
            split_hidden(n_exp * GROUPS - 1, plan["hid", GROUPS - 1])
            scale_y(n_exp - 1, M1)

            act.wait_ge(extra_done, 1)
            many = act.value_load(extra_i[0:1, EXTRA:EXTRA + 1], min_val=0, max_val=EXTRA)
            with act.If(many > 0):
                with act.Fori(0, many) as i:
                    take_selT(n_exp + i, 7)
                    take_gather(n_exp // 2 + i, P)
                    for pos in range(PER_EXPERT):
                        g, q = divmod(pos, 6)
                        landed_m((M1 + pos) % 6, (M1 + pos) // 6 + GROUPS * i)
                        hi(M1 + PER_EXPERT * i + pos, (M1 + pos) % 6)
                        if q == 5:
                            silu(GROUPS * (n_exp + i) + g, 0, M1 + PER_EXPERT * i + 6 * g + 4)
                            split_hidden(GROUPS * (n_exp + i) + g, 6)
                    scale_y(n_exp + i, M1 + PER_EXPERT * (i + 1))

            for c in range(KC):
                act.wait_ge(x_last, c + 1)
                square(c)
            root(n_norms - 1)
            act.wait_ge(out_dma, 64 * depth)
            for s in range(2 * TT):
                j, half = divmod(s, 2)
                rows = LAST if j == TT - 1 else P
                act.wait_ge(fin_ps, s + 1)
                act.activation(y_rows[0:rows, j, half * BANK:(half + 1) * BANK], ps[0:rows, s, :], ACT.Copy)\
                    .then_inc(fin_out, 1)
            for j in range(TT):
                act.wait_ge(fin_out, 2 * (j + 1))
                if j < TT - 1:
                    act.dma_start(o["y_prompt"][0, j * P:(j + 1) * P, :], y_rows[:, j, :]).then_inc(y_dma, 16)
                else:
                    act.dma_start(o["y_sample"].rearrange("b s d -> (b s) d"), y_rows[0:LAST, j, :])\
                        .then_inc(y_dma, 16)
            act.wait_ge(y_dma, 16 * TT)

        @block.vector
        def _(dve):
            steps = [0]

            def link(ins):
                steps[0] += 1
                ins.then_inc(dve_step, 1)
                dve.wait_ge(dve_step, steps[0])

            dve.wait_ge(consts, 2)
            link(dve.reciprocal(fix[:, :, :], fix[:, :, :]))
            for g, w in enumerate(WINDOWS):
                link(dve.tensor_scalar(fix[:, g, :], fix[:, g, :], float(w), None, ALU.mult))

            def lo(m, slot, width=CHUNK):
                dve.wait_ge(hi_done, m + 1)
                dve.tensor_tensor(w_lo[:, slot % SPLIT_SLOTS, 0:width], raw[:, slot, 0:width],
                                  w_hi[:, slot % SPLIT_SLOTS, 0:width].bitcast(F32), ALU.subtract)\
                    .then_inc(lo_done, 1)

            def lo_of(ch):
                m, raw_slot, width = ch["m"], ch["n"] % RAW_SLOTS, ch["nk"] * ch["width"]
                dve.wait_ge(hi_done, m + 1)
                dve.tensor_tensor(w_lo[:, m % SPLIT_SLOTS, 0:width], raw[:, raw_slot, 0:width],
                                  w_hi[:, m % SPLIT_SLOTS, 0:width].bitcast(F32), ALU.subtract)\
                    .then_inc(lo_done, 1)

            for c in range(KC):
                dve.wait_ge(turned, 4 + c)
                dve.tensor_copy(xT[:, c, :], ps[:, c % 4, 0:T]).then_inc(turned_out, 1)
            dve.wait_ge(turned_out, KC)
            dve.engine_nop().then_inc(x_done, 1)
            dve.wait_ge(par_done, 2)

            def mod(l, what):
                return modT[:, l, what * KC:(what + 1) * KC, :]

            def ada_pairs(chunks):
                for even in [ch for ch in chunks if ch["a"] % 2 == 0]:
                    k, l, b0 = even["a"] // 2, even["layer"], 2 * even["j"]
                    what = b0 // KC
                    dst = modT[:, l, b0:b0 + 4, :]
                    bias = pcol(BADA + ADA_PARTS * KC * l + b0, 4).unsqueeze(2).to_broadcast([P, 4, S])
                    dve.wait_ge(ada_turned, k + 1)
                    dve.tensor_tensor(dst, ps[:, 5, 0:4 * S].rearrange("p (b s) -> p b s", b=4), bias, ALU.add)\
                        .then_inc(ada_out, 1)
                    dve.wait_ge(ada_out, k + 1)
                    if what in (SC1, SC2):
                        g = pcol((G_MIX if what == SC1 else G_FFN) + KC * l + b0 % KC, 4)
                        link(dve.scalar_tensor_tensor(out=dst, in0=dst, scalar=1.0,
                                                      in1=g.unsqueeze(2).to_broadcast([P, 4, S]),
                                                      op0=ALU.add, op1=ALU.mult))

            def norm_start(k):
                dve.wait_ge(sums, k + 1)
                link(dve.tensor_scalar(var, ps[:, 4, 0:T], 1.0 / d_model, EPS, ALU.mult, ALU.add))
                dve.reciprocal(var, var).then_inc(inv_var, 1)
                dve.wait_ge(rstd_done, k + 1)
                rb = rstd.unsqueeze(1).to_broadcast([P, KC, T])
                link(dve.tensor_tensor(hn, xT[:, :, :], rb, ALU.mult))

            def norm_end(k):
                l, first = divmod(k, 2)
                sc, sh = (mod(l, SC1), mod(l, SH1)) if first == 0 else (mod(l, SC2), mod(l, SH2))
                hs = hn[:, :, seq:T]
                link(dve.tensor_tensor(hs, hs, sc[:, :, 1:S], ALU.mult))
                link(dve.tensor_tensor(hs, hs, sh[:, :, 1:S], ALU.add))
                for half in range(NORM_H):
                    for c in range(half * KC // NORM_H, (half + 1) * KC // NORM_H):
                        ins = dve.tensor_scalar(hn[:, c, 0:seq], hn[:, c, 0:seq], sc[:, c, 0:1], sh[:, c, 0:1],
                                                ALU.mult, ALU.add)
                        if c % (KC // NORM_H) != KC // NORM_H - 1:
                            ins.then_inc(dve_step, 1)
                            steps[0] += 1
                    dve.wait_ge(dve_step, steps[0])
                    ins.then_inc(normed, 1)
                for half in range(NORM_H):
                    c0, c1 = half * KC // NORM_H, (half + 1) * KC // NORM_H
                    dve.wait_ge(h_hi_done, NORM_H * k + half + 1)
                    dve.tensor_tensor(h_lo[:, c0:c1, :], hn[:, c0:c1, :], h_hi[:, c0:c1, :].bitcast(F32),
                                      ALU.subtract).then_inc(h_lo_done, 1)

            def add_gated(l, gt, c, src_p, src_s, done):
                link(dve.tensor_tensor(scr[:, 0, 0:dec], src_s, mod(l, gt)[:, c, 1:S], ALU.mult))
                link(dve.tensor_tensor(xT[:, c, seq:T], xT[:, c, seq:T], scr[:, 0, 0:dec], ALU.add))
                ins = dve.scalar_tensor_tensor(out=xT[:, c, 0:seq], in0=src_p, scalar=mod(l, gt)[:, c, 0:1],
                                               in1=xT[:, c, 0:seq], op0=ALU.mult, op1=ALU.add)
                if done is not None:
                    ins.then_inc(done, 1)
                return ins

            def take(ch):
                dve.wait_ge(used, ch["m"] + 1)
                l = ch["layer"]
                for b in ch["blocks"]:
                    blk, col = blocks[b], blocks[b]["col"]
                    src = ps[:, b % 4, 0:T]
                    if blk["eng"] != "dve":
                        continue
                    if ch["kind"] == "in" and col < GB:
                        dve.tensor_tensor(conv[:, col, :], src, conv[:, col, :], ALU.mult).then_inc(dve_took, 1)
                    elif ch["kind"] == "in":
                        v = col - 2 * GB
                        dve.wait_ge(act_took, count_of("in", l, GB + v))
                        vs = zv[:, v, SV:].rearrange("p (s r) -> p s r", r=3)
                        link(dve.tensor_tensor(vs[:, :, 2], src[:, seq:T], c_gate[:, v, seq:T], ALU.mult))
                        dve.tensor_tensor(zv[:, v, 2:SV], src[:, 0:seq], c_gate[:, v, 0:seq], ALU.mult)\
                            .then_inc(dve_took, 1)
                    elif ch["kind"] == "out":
                        add_gated(l, GT1, col, src[:, 0:seq], src[:, seq:T], dve_took)
                    elif ch["kind"] == "down" and ch["last"]:
                        add_gated(l, GT2, col, src[:, 0:seq], src[:, seq:T], dve_took)
                    elif ch["kind"] == "up":
                        f = col
                        dve.wait_ge(act_took, count_of("gate", l, f))
                        if f >= 2:
                            dve.wait_ge(ffn_lo, f - 1)
                        dve.tensor_tensor(hid_f[:, col % 2, :], src, silu_g[:, 2 * (ch["j"] % 2) + col % 2, :],
                                          ALU.mult).then_inc(dve_took, 1)
                if ch["kind"] == "up":
                    for b in range(2):
                        f = 2 * ch["j"] + b
                        dve.wait_ge(ffn_hi, f + 1)
                        dve.tensor_tensor(hid_lo[:, f, :], hid_f[:, b, :], hid_hi[:, f, :].bitcast(F32),
                                          ALU.subtract).then_inc(ffn_lo, 1)

            def put_states(l):
                link(dve.memset(zu[:, :, 0:HIST], 0.0))
                link(dve.memset(zv[:, :, 0:2], 0.0))
                dve.wait_ge(state_turned, 2 * (l + 1))
                us = zu[:, :, SU:].rearrange("p b (s r) -> p b s r", r=HIST + 1)
                ups = ps[:, 5, 0:GB * dec * HIST].rearrange("p (b s r) -> p b s r", b=GB, s=dec)
                vs = zv[:, :, SV:].rearrange("p b (s r) -> p b s r", r=3)
                vps = ps[:, 4, 0:GB * dec * 2].rearrange("p (b s r) -> p b s r", b=GB, s=dec)
                for b in range(GB):
                    link(dve.tensor_copy(us[:, b, :, 0:HIST], ups[:, b]))
                    link(dve.tensor_copy(vs[:, b, :, 0:2], vps[:, b]))
                dve.engine_nop().then_inc(state_put, 1)
                dve.engine_nop().then_inc(state_put, 1)

            wins = [sum_a[:, 0, :], sum_b[:, 0, :], sum_a[:, 2, :], sum_b[:, 2, :]]

            def window_sums(l):
                dve.wait_ge(act_took, count_of("in", l, 4 * GB - 1))
                if l:
                    dve.wait_ge(out_dma, 64 * l)
                n1 = ZU - 1
                link(dve.tensor_tensor(sum_a[:, :, 0:n1], zu[:, :, 0:n1], zu[:, :, 1:ZU], ALU.add))
                n2 = n1 - 2
                link(dve.tensor_tensor(sum_b[:, :, 0:n2], sum_a[:, 1:, 0:n2], sum_a[:, 1:, 2:n2 + 2], ALU.add))
                n3 = n2 - 4
                link(dve.tensor_tensor(sum_a[:, 2:, 0:n3], sum_b[:, 1:, 0:n3], sum_b[:, 1:, 4:n3 + 4], ALU.add))
                n4 = n3 - 8
                link(dve.tensor_tensor(sum_b[:, 2, 0:n4], sum_a[:, 3, 0:n4], sum_a[:, 3, 8:n4 + 8], ALU.add))

            def window_diff(l, g):
                w = WINDOWS[g]
                s0 = HIST + 1 - w
                head = wins[g][:, s0:s0 + HIST + 1]
                link(dve.tensor_tensor(head, head, fix[:, g, :], ALU.mult))
                if g >= 2:
                    dve.wait_ge(diff_hi, GB * l + g - 1)
                link(dve.scalar_tensor_tensor(out=scr[:, g % 2, 0:seq], in0=wins[g][:, s0:s0 + seq], scalar=1.0 / w,
                                              in1=zu[:, g, HIST:SU], op0=ALU.mult, op1=ALU.subtract))
                ends = zu[:, g, SU:].rearrange("p (s r) -> p s r", r=HIST + 1)[:, :, HIST]
                at_ = SU + HIST + 1 - w
                wv = wins[g][:, at_:at_ + (HIST + 1) * (dec - 1) + 1:HIST + 1]
                dve.scalar_tensor_tensor(out=scr[:, g % 2, seq:T], in0=wv, scalar=1.0 / w, in1=ends,
                                         op0=ALU.mult, op1=ALU.subtract).then_inc(diff_done, 1)

            def diff_low(l, g):
                dve.wait_ge(diff_hi, GB * l + g + 1)
                dve.tensor_tensor(diff[:, 1, g, :], scr[:, g % 2, 0:T], diff[:, 0, g, :].bitcast(F32), ALU.subtract)\
                    .then_inc(diff_lo, 1)

            def convolve(l, b):
                n = ZV - 2
                w = [pcol(CONV + (3 * l + k) * GB + b) for k in range(3)]
                link(dve.tensor_scalar(scr[:, 0, :], zv[:, b, 0:n], w[0], None, ALU.mult))
                link(dve.scalar_tensor_tensor(out=scr[:, 1, :], in0=zv[:, b, 1:n + 1], scalar=w[1],
                                              in1=scr[:, 0, :], op0=ALU.mult, op1=ALU.add))
                dve.scalar_tensor_tensor(out=conv[:, b, 0:seq], in0=zv[:, b, 2:seq + 2], scalar=w[2],
                                         in1=scr[:, 1, 0:seq], op0=ALU.mult, op1=ALU.add).then_inc(dve_step, 1)
                steps[0] += 1
                ends = slice(SV, SV + 3 * (dec - 1) + 1, 3)
                link(dve.scalar_tensor_tensor(out=conv[:, b, seq:T], in0=zv[:, b, SV + 2:SV + 3 * dec:3], scalar=w[2],
                                              in1=scr[:, 1, ends], op0=ALU.mult, op1=ALU.add))

            def mix_inverse(l, half):
                dve.wait_ge(sq_used, 2 * GB * l + GB * (half + 1))
                link(dve.tensor_scalar(msq[:, half, :], ps[:, 4, 0:T], 1.0 / (GB * P), EPS, ALU.mult, ALU.add))
                dve.reciprocal(msq[:, half, :], msq[:, half, :]).then_inc(mix_inv, 1)

            def mix_result(l, half):
                y = conv if half else y_pool
                g, k0 = (GCO, 0) if half else (GPO, GB)
                dve.wait_ge(mix_rstd, 2 * l + half + 1)
                rb = msq[:, half, :].unsqueeze(1).to_broadcast([P, GB, T])
                dve.tensor_tensor(y, y, rb, ALU.mult).then_inc(m_f, 1)
                dve.wait_ge(m_hi, 2 * l + half + 1)
                for b in range(GB):
                    ins = dve.scalar_tensor_tensor(out=m_lo_t[:, k0 + b, :], in0=y[:, b, :],
                                                   scalar=pcol(g + GB * l + b),
                                                   in1=m_hi_t[:, k0 + b, :].bitcast(F32),
                                                   op0=ALU.mult, op1=ALU.subtract)
                ins.then_inc(m_lo, 1)

            def begin(phase, fill):
                ada_pairs(fill[:2])
                for ch in phase[:2]:
                    lo_of(ch)
                ada_pairs(fill[2:])
                lo_of(phase[2])

            def phase_in(l, phase):
                for i, ch in enumerate(phase):
                    if i >= SPLIT_SLOTS:
                        lo_of(ch)
                        take(phase[i - SPLIT_SLOTS])
                    if i == 4:
                        window_sums(l)
                    if i in (5, 6):
                        g0 = 2 * (i - 5)
                        for g in (g0, g0 + 1):
                            window_diff(l, g)
                        for g in (g0, g0 + 1):
                            diff_low(l, g)
                    if i in (7, 8):
                        dve.wait_ge(dve_took, count_of("in", l, 2 * GB + 2 * (i - 7) + 1))
                        for b in (2 * (i - 7), 2 * (i - 7) + 1):
                            convolve(l, b)
                take(phase[7])
                dve.wait_ge(act_took, count_of("pool", l, GB - 1))
                mix_inverse(l, 0)
                mix_result(l, 0)
                take(phase[8])
                dve.wait_ge(dve_took, count_of("in", l, GB - 1))
                mix_inverse(l, 1)
                mix_result(l, 1)

            def phase_rest(phase):
                for i, ch in enumerate(phase):
                    if i >= SPLIT_SLOTS:
                        lo_of(ch)
                        take(phase[i - SPLIT_SLOTS])
                for ch in phase[-SPLIT_SLOTS:]:
                    take(ch)
                dve.wait_ge(dve_took, blocks[phase[-1]["blocks"][-1]]["count"])

            norm_start(0)
            ada_pairs(fillers[0])
            norm_end(0)
            begin(phases[0], [])
            put_states(0)
            phase_in(0, phases[0])
            ada_pairs(fillers[1][:4])
            begin(phases[1], fillers[1][4:])
            phase_rest(phases[1])
            norm_start(1)
            ada_pairs(fillers[2][:4])
            norm_end(1)
            begin(phases[2], fillers[2][4:])
            phase_rest(phases[2])
            norm_start(2)
            ada_pairs(fillers[3][:8])
            norm_end(2)
            begin(phases[3], fillers[3][8:])
            put_states(1)
            phase_in(1, phases[3])
            begin(phases[4], fillers[4])
            phase_rest(phases[4])
            norm_start(3)
            ada_pairs(fillers[5][:4])
            norm_end(3)

            dve.wait_ge(tok_zero, 1)
            dve.wait_ge(logits_turned, 1)
            for j in range(TT):
                rows = LAST if j == TT - 1 else P
                link(dve.tensor_copy(logit[0:rows, j, :], ps[0:rows, 5, E * j:E * (j + 1)]))
            shape = [P, TT, E, E]
            mine = logit.unsqueeze(3).to_broadcast(shape)
            other = logit.unsqueeze(2).to_broadcast(shape)
            link(dve.tensor_tensor(cmp1, other, mine, ALU.is_gt))
            link(dve.tensor_tensor(cmp2, other, mine, ALU.is_equal))
            link(dve.tensor_tensor(cmp2, cmp2, earlier.unsqueeze(1).to_broadcast(shape), ALU.mult))
            link(dve.tensor_tensor(cmp1, cmp1, cmp2, ALU.add))
            link(dve.tensor_reduce(rank, cmp1, axis=AX_X, op=ALU.add))
            link(dve.tensor_scalar(chosen, rank, 2.0, None, ALU.is_lt))
            dve.tensor_tensor(chosen, chosen, real.unsqueeze(2).to_broadcast([P, TT, E]), ALU.mult)\
                .then_inc(chosen_done, 1)
            link(dve.tensor_reduce(lmax, logit, axis=AX_X, op=ALU.max))
            dve.tensor_tensor(logit, logit, lmax.unsqueeze(2).to_broadcast([P, TT, E]), ALU.subtract)\
                .then_inc(route_max, 1)
            dve.wait_ge(chosen_done, 1)
            dve.wait_ge(cum_ps, 1)
            before = ps[:, 5, 0:TT * E].rearrange("p (j e) -> p j e", j=TT)
            place_j = place.rearrange("p e j -> p j e")
            link(dve.tensor_scalar(place_j, before, 1000.0, None, ALU.add))
            link(dve.tensor_tensor(place_j, place_j, chosen, ALU.mult))
            link(dve.tensor_scalar(place_j, place_j, -1000.0, None, ALU.add))

            def fill_sel(places, experts=2):
                dve.wait_ge(place_made, places)
                for h in range(experts):
                    for j in range(TT):
                        dve.tensor_scalar(sel[:, j, P * h:P * (h + 1)], slot_no[:, :], place_e[:, h, j:j + 1], None,
                                          ALU.is_equal).then_inc(sel_made, 1)

            dve.tensor_copy(place_e, place[:, 0:2, :]).then_inc(place_made, 1)
            fill_sel(1)
            dve.wait_ge(route_max, 1)
            dve.wait_ge(route_exp, 1)
            link(dve.tensor_tensor(logit, rank, chosen, ALU.mult))
            link(dve.tensor_reduce(lsum, logit, axis=AX_X, op=ALU.add))
            link(dve.tensor_scalar(lsum, lsum, 1e-30, None, ALU.max))
            link(dve.reciprocal(lsum, lsum))
            link(dve.tensor_tensor(gate.rearrange("p e j -> p j e"), logit,
                                   lsum.unsqueeze(2).to_broadcast([P, TT, E]), ALU.mult))
            dve.tensor_copy(gate_e, gate[:, 0:2, :]).then_inc(place_made, 1)
            count = ps[:, 5, TT * E:(TT + 1) * E]
            for j in range(TT - 1):
                link(dve.tensor_scalar(more[:, j, :], count, float(P * (j + 1)), None, ALU.is_gt))
            cur, nxt, d = more_row, more_no, 1
            link(dve.tensor_copy(tmp_row, more_row))
            cur = tmp_row
            while d < NX:
                link(dve.tensor_copy(nxt[:, 0:d], cur[:, 0:d]))
                link(dve.tensor_tensor(nxt[:, d:NX], cur[:, d:NX], cur[:, 0:NX - d], ALU.add))
                cur, nxt = nxt, cur
                d *= 2
            want = slot_no[:, 1:EXTRA + 1].unsqueeze(2).to_broadcast([P, EXTRA, NX])
            link(dve.tensor_tensor(hit, cur.unsqueeze(1).to_broadcast([P, EXTRA, NX]), want, ALU.is_equal))
            link(dve.tensor_tensor(hit, hit, more_row.unsqueeze(1).to_broadcast([P, EXTRA, NX]), ALU.mult))
            link(dve.tensor_tensor(hit2, hit, code_s.unsqueeze(1).to_broadcast([P, EXTRA, NX]), ALU.mult))
            link(dve.tensor_reduce(extra_shift, hit2, axis=AX_X, op=ALU.add))
            link(dve.tensor_tensor(hit2, hit, code_e.unsqueeze(1).to_broadcast([P, EXTRA, NX]), ALU.mult))
            link(dve.tensor_reduce(extra_f[:, 0:EXTRA], hit2, axis=AX_X, op=ALU.add))
            link(dve.tensor_copy(extra_f[:, EXTRA:EXTRA + 1], cur[:, NX - 1:NX]))
            dve.tensor_copy(extra_i[:, :], extra_f).then_inc(extra_done, 1)

            def make_sel(readers, gathers, first, n):
                dve.wait_ge(selT_done, readers)
                dve.wait_ge(gather_ps, gathers)
                dve.tensor_copy(place_e[:, 0:n, :], place[:, bass.ds(first, n), :]).then_inc(place_made, 1)
                dve.tensor_copy(gate_e[:, 0:n, :], gate[:, bass.ds(first, n), :]).then_inc(place_made, 1)

            def hidden(q, bank):
                dve.wait_ge(e_silu_done, q + 1)
                dve.wait_ge(e_turned, q)
                dve.tensor_tensor(e_hid, ps[:, bank + 1, :], e_silu, ALU.mult).then_inc(e_hid_done, 1)

            def split_hidden(q, bank):
                dve.wait_ge(e_hi_done, q + 1)
                dve.tensor_tensor(eh_lo, ps[:, bank, :].rearrange("p (k s) -> p k s", k=GC),
                                  eh_hi.bitcast(F32), ALU.subtract).then_inc(e_lo_done, 1)

            def split_y(e):
                dve.wait_ge(y_hi_done, e + 1)
                dve.tensor_tensor(y_lo, y_f.rearrange("p (c d) -> p c d", c=KC), y_hi.bitcast(F32), ALU.subtract)\
                    .then_inc(y_lo_done, 1)

            def combine(e, banks):
                for c in range(KC):
                    dve.wait_ge(comb_ps, KC * e + c + 1)
                    dve.tensor_tensor(acc[:, c, :], acc[:, c, :], ps[:, banks[c % 2], 0:T], ALU.add)\
                        .then_inc(combined, 1)
                dve.wait_ge(combined, KC * (e + 1))

            plan = misc_plan()

            def expert(e, first, sel_for=None):
                for pos, kind, g in expert_chunks(first):
                    n, s = chunk_no(e, pos, first), slot_of(pos, first)
                    if not (first and pos < SPLIT_SLOTS):
                        lo(n, s)
                    if pos % 6 == 0 and (pos or not first):
                        hidden(GROUPS * e + g - 1, (g - 1) % GROUPS % 2 * 2)
                    if pos % 6 == 3 and (pos > 3 or not first):
                        split_hidden(GROUPS * e + g - 1, plan["hid", (g - 1) % GROUPS])
                    if pos == 8 and not first:
                        split_y(e - 1)
                    if pos == 11 and not first:
                        combine(e - 1, plan["comb"])
                    if pos == 18 and sel_for is not None:
                        make_sel(4 * sel_for, 8 * sel_for, 2 * sel_for, 2)
                        fill_sel(2 * sel_for + 2)

            ada_pairs(fillers[5][4:])
            for k in range(SPLIT_SLOTS):
                lo(M0 + k, (M0 + k) % 6)
            dve.wait_ge(acc_zero, 1)
            expert(0, True)
            expert(1, False, 1)
            with dve.Fori(1, n_exp // 2 - 1) as pair:
                expert(2 * pair, False)
                expert(2 * pair + 1, False, pair + 1)
            expert(n_exp - 2, False)
            expert(n_exp - 1, False)
            for q in range(2):
                n = M1 - 2 + q
                lo(n, n % 6)
                if q == 0:
                    hidden(n_exp * GROUPS - 1, (GROUPS - 1) % 2 * 2)
            split_hidden(n_exp * GROUPS - 1, plan["hid", GROUPS - 1])
            split_y(n_exp - 1)
            combine(n_exp - 1, (6, 7))

            dve.wait_ge(extra_done, 1)
            many = dve.value_load(extra_i[0:1, EXTRA:EXTRA + 1], min_val=0, max_val=EXTRA)
            with dve.If(many > 0):
                with dve.Fori(0, many) as i:
                    e = dve.value_load(extra_i[0:1, bass.ds(i, 1)], min_val=0, max_val=n_exp - 1)
                    k = n_exp + i
                    make_sel(2 * k, 8 * (n_exp // 2 + i), e, 1)
                    dve.wait_ge(place_made, n_exp + 3 * i + 2)
                    dve.tensor_scalar(place_e[:, 0, :], place_e[:, 0, :], extra_shift[:, bass.ds(i, 1)], None,
                                      ALU.subtract).then_inc(place_made, 1)
                    fill_sel(n_exp + 3 * i + 3, 1)
                    for pos in range(PER_EXPERT):
                        g, q = divmod(pos, 6)
                        lo(M1 + PER_EXPERT * i + pos, (M1 + pos) % 6)
                        if q == 5:
                            hidden(GROUPS * k + g, 0)
                            split_hidden(GROUPS * k + g, 6)
                    split_y(k)
                    combine(k, (6, 7))

            dve.wait_ge(combined, KC * n_exp)
            for c in range(KC):
                add_gated(1, GT2, c, acc[:, c, 0:seq], acc[:, c, seq:T], x_last)
            dve.wait_ge(x_last, KC)
            norm_start(n_norms - 1)
            for c in range(KC):
                dve.tensor_scalar(hn[:, c, :], hn[:, c, :], pcol(G_FIN + c), None, ALU.mult).then_inc(fin_f, 1)

        @block.tensor
        def _(pe):
            pe.wait_ge(consts, 2)
            pe.wait_ge(c_silu, 1)
            for k in range(KC):
                ins = pe.transpose(ps[:, 4, k * S:(k + 1) * S], c_rows[0:S, k * P:(k + 1) * P], ident[0:S, 0:S])
            ins.then_inc(turned, 1)
            n0 = depth * ADA_PARTS * KC
            pe.wait_ge(par_in, 16 * 8)
            pe.transpose(ps[:, 5, 0:n0], par_rows[0:n0, 0, :], ident[0:n0, 0:n0]).then_inc(turned, 1)
            pe.transpose(ps[:, 5, n0:184], par_rows[0:184 - n0, 1, :], ident[0:184 - n0, 0:184 - n0])\
                .then_inc(turned, 1)
            pe.wait_ge(x_in, 32)
            for c in range(KC):
                if c >= 4:
                    pe.wait_ge(turned_out, c - 3)
                for j in range(TT):
                    rows = LAST if j == TT - 1 else P
                    ins = pe.transpose(ps[:, c % 4, j * P:j * P + rows], x_rows[0:rows, j, c * P:(c + 1) * P],
                                       ident[0:rows, 0:rows])
                ins.then_inc(turned, 1)
            def bank5(event=None, last=[(par_done, 2)]):
                pe.wait_ge(*last[0])
                last[0] = event

            def turn_states(l):
                pe.wait_ge(states_in[l], 32)
                bank5((state_put, 2 * (l + 1)))
                pe.wait_ge(inv_var, 2 * l + 1)
                for b in range(GB):
                    n = dec * HIST
                    ins = pe.transpose(ps[:, 5, b * n:(b + 1) * n], pool_rows[0:n, b * P:(b + 1) * P],
                                       ident[0:n, 0:n])
                ins.then_inc(state_turned, 1)
                for b in range(GB):
                    n = dec * 2
                    ins = pe.transpose(ps[:, 4, b * n:(b + 1) * n], conv_rows[0:n, b * P:(b + 1) * P],
                                       ident[0:n, 0:n])
                ins.then_inc(state_turned, 1)

            def ada_product(ch):
                a_no, n = ch["a"], ch["n"]
                pe.wait_ge(raw_in[n % RAW_SLOTS], 16 * (n // RAW_SLOTS + 1))
                if a_no // 2 >= 2:
                    pe.wait_ge(ada_copied, a_no // 2 - 1)
                out = ps[0:S, 6 + a_no // 2 % 2, 256 * (a_no % 2):256 * (a_no % 2 + 1)]
                for k in range(KC):
                    ins = pe.matmul(out, silu_c[:, k, :], raw[:, n % RAW_SLOTS, 256 * k:256 * (k + 1)],
                                    start=(k == 0), stop=(k == KC - 1))
                ins.then_inc(ada_used, 1)

            def ada_turn(k):
                pe.wait_ge(ada_copied, k + 1)
                bank5((ada_out, k + 1))
                for b in range(4):
                    ins = pe.transpose(ps[:, 5, S * b:S * (b + 1)], ada_rows[:, P * b:P * (b + 1)], ident[0:S, 0:S])
                ins.then_inc(ada_turned, 1)

            def fill(chunks, done=0):
                waiting = None
                for ch in chunks:
                    if done:
                        done -= 1
                    else:
                        ada_product(ch)
                    if waiting is not None:
                        ada_turn(waiting)
                        waiting = None
                    if ch["a"] % 2:
                        waiting = ch["a"] // 2
                ada_turn(waiting)

            def norm_sums(k):
                if k == 0:
                    pe.wait_ge(c_done, 1)
                elif k == n_norms - 1:
                    pe.wait_ge(logits_row, 1)
                elif k % 2:
                    pe.wait_ge(mix_inv, k + 1)
                else:
                    pe.wait_ge(inv_var, k)
                for c in range(KC):
                    pe.wait_ge(squares, KC * k + c + 1)
                    ins = pe.matmul(ps[:, 4, 0:T], ones[:, :], sq[:, c, :], start=(c == 0), stop=(c == KC - 1))
                ins.then_inc(sums, 1)

            def mix_sums(l, half):
                if half == 0:
                    pe.wait_ge(state_put, 2 * (l + 1))
                else:
                    pe.wait_ge(mix_inv, 2 * l + 1)
                for b in range(GB):
                    pe.wait_ge(mix_sq, 2 * GB * l + GB * half + b + 1)
                    pe.matmul(ps[:, 4, 0:T], ones[:, :], mix_squares[:, b % 2, :], start=(b == 0),
                              stop=(b == GB - 1)).then_inc(sq_used, 1)

            def turn_tails(l):
                pe.wait_ge(tails, 4 * (l + 1))
                bank5((tails_out, l + 1))
                for b in range(GB):
                    ins = pe.transpose(ps[0:ROWS, 5, b * P:(b + 1) * P], last_rows[:, b, :], ident[:, :])
                ins.then_inc(tails_turned, 1)

            def bank_free(b):
                if b >= 4:
                    old = blocks[b - 4]
                    pe.wait_ge(act_took if old["eng"] == "act" else dve_took, old["count"])
                else:
                    pe.wait_ge(turned_out, KC)

            def product(ch):
                s, l, kind = ch["m"] % SPLIT_SLOTS, ch["layer"], ch["kind"]
                x_hi, x_lo = {"down": (hid_hi, hid_lo), "out": (m_hi_t, m_lo_t)}.get(kind, (h_hi, h_lo))
                pe.wait_ge(lo_done, ch["m"] + 1)
                if kind == "in":
                    pe.wait_ge(h_lo_done, NORM_H * (2 * l + 1))
                if kind == "gate":
                    pe.wait_ge(h_lo_done, NORM_H * (2 * l + 2))
                if kind == "down":
                    pe.wait_ge(ffn_lo, min(FC, ch["k0"] + ch["nk"]))
                for b, blk in enumerate(ch["blocks"]):
                    if ch["first"]:
                        bank_free(blk)
                    out = ps[:, blk % 4, 0:T]
                    if kind == "pool":
                        w = slice(P * b, P * (b + 1))
                        pe.wait_ge(diff_lo, GB * l + b + 1)
                        pe.matmul(out, w_hi[:, s, w], diff[:, 0, b, :], start=True, stop=False)
                        pe.matmul(out, w_hi[:, s, w], diff[:, 1, b, :], start=False, stop=False)
                        ins = pe.matmul(out, w_lo[:, s, w], diff[:, 0, b, :], start=False, stop=True)
                        continue
                    order = [(k + GB) % KC for k in range(KC)] if kind == "out" else list(range(ch["nk"]))
                    for i, k in enumerate(order):
                        if kind == "out" and i % GB == 0:
                            pe.wait_ge(m_lo, 2 * l + 1 + i // GB)
                        w = slice(256 * k + P * b, 256 * k + P * (b + 1))
                        kk = ch["k0"] + k
                        pe.matmul(out, w_hi[:, s, w], x_hi[:, kk, :], start=ch["first"] and i == 0, stop=False)
                        pe.matmul(out, w_hi[:, s, w], x_lo[:, kk, :], start=False, stop=False)
                        ins = pe.matmul(out, w_lo[:, s, w], x_hi[:, kk, :], start=False,
                                        stop=ch["last"] and i == ch["nk"] - 1)
                ins.then_inc(used, 1)

            def phase_in(l, phase, next_fill):
                for i, ch in enumerate(phase):
                    product(ch)
                    if i == 7:
                        mix_sums(l, 0)
                ada_product(next_fill[0])
                mix_sums(l, 1)

            def phase_rest(phase):
                for ch in phase:
                    product(ch)

            norm_sums(0)
            fill(fillers[0])
            turn_states(0)
            phase_in(0, phases[0], fillers[1])
            fill(fillers[1][:4], 1)
            turn_tails(0)
            fill(fillers[1][4:])
            phase_rest(phases[1])
            norm_sums(1)
            fill(fillers[2])
            phase_rest(phases[2])
            norm_sums(2)
            fill(fillers[3])
            turn_states(1)
            phase_in(1, phases[3], fillers[4])
            turn_tails(1)
            fill(fillers[4], 1)
            phase_rest(phases[4])
            norm_sums(3)
            fill(fillers[5][:4])
            for ch in fillers[5][4:]:
                ada_product(ch)

            pe.wait_ge(router_in, 16)
            pe.wait_ge(h_lo_done, NORM_H * 4)
            pe.wait_ge(inv_var, 4)
            for k in range(KC):
                ins = pe.matmul(ps[0:E, 4, 0:T], router[:, k, :], hn[:, k, :], start=(k == 0), stop=(k == KC - 1))
            ins.then_inc(logits_ps, 1)
            pe.wait_ge(logits_row, 1)
            bank5((chosen_done, 1))
            for j in range(TT):
                rows = LAST if j == TT - 1 else P
                ins = pe.transpose(ps[0:rows, 5, E * j:E * (j + 1)], logitT[:, j * P:j * P + rows], ident[0:E, 0:E])
            ins.then_inc(logits_turned, 1)

            def turn_tokens(s0, s1):
                for s in range(s0, s1):
                    j, part_no, half = s // 4, s // 2 % 2, s % 2
                    rows = LAST if j == TT - 1 else P
                    if s >= 4:
                        pe.wait_ge(tok_copied, s - 3)
                    src = (h_hi if part_no == 0 else h_lo)
                    for c in range(4):
                        ins = pe.transpose(ps[0:rows, s % 4, c * P:(c + 1) * P],
                                           src[:, 4 * half + c, j * P:j * P + rows].bitcast(F32), ident[:, :])
                    ins.then_inc(tok_turned, 1)

            turn_tokens(0, 6)
            bank5((extra_done, 1))
            for j in range(TT + 1):
                out = ps[:, 5, E * j:E * (j + 1)]
                for i in range(min(j + 1, TT)):
                    ins = pe.matmul(out, tri[:, :] if i == j else ones[:, :], chosen[:, i, :], start=(i == 0),
                                    stop=(i == min(j, TT - 1)))
            ins.then_inc(cum_ps, 1)
            turn_tokens(6, 4 * TT)
            pe.wait_ge(tok_copied, 4 * TT)

            free = {6: None, 7: None}

            def bank(b):
                if free[b] is not None:
                    pe.wait_ge(*free[b])

            def gather(k, s0, s1, made, width=2 * P):
                pe.wait_ge(sel_made, made)
                for s in range(s0, s1):
                    b = 6 + s % 2
                    bank(b)
                    src = tok_hi if s < 4 else tok_lo
                    for c in range(2):
                        cc = 2 * (s % 4) + c
                        for j in range(TT):
                            ins = pe.matmul(ps[:, b, 2 * P * c:2 * P * c + width], src[:, j, cc * P:(cc + 1) * P],
                                            sel[:, j, 0:width], start=(j == 0), stop=(j == TT - 1))
                    ins.then_inc(gather_ps, 1)
                    free[b] = (gathered, 8 * k + s + 1)

            def turn_sel(k, b, h, made):
                bank(b)
                pe.wait_ge(place_made, made)
                cols = slice(P * h, P * (h + 1))
                for j in range(TT):
                    rows = LAST if j == TT - 1 else P
                    pe.transpose(ps[:, b, j * P:j * P + rows], sel[0:rows, j, cols].bitcast(F32),
                                 ident[0:rows, 0:rows])
                for j in range(TT):
                    ins = pe.matmul(ps[:, b, T:T + 1], sel[:, j, cols].bitcast(F32), gate_e[:, h, j:j + 1],
                                    start=(j == 0), stop=(j == TT - 1))
                ins.then_inc(selT_ps, 1)
                free[b] = (selT_done, 2 * (k + 1))

            def gate_up(n, s, c, b, groups_read, h):
                pe.wait_ge(lo_done, n + 1)
                if c == 0 and groups_read is not None:
                    pe.wait_ge(e_hid_done, groups_read)
                out = ps[:, b + c // 2, :]
                for k in range(4):
                    kk = 4 * (c % 2) + k
                    wv = slice(BANK * k, BANK * (k + 1))
                    pe.matmul(out, xs_hi[:, kk, P * h:P * (h + 1)], w_hi[:, s, wv], start=(kk == 0), stop=False)
                    pe.matmul(out, xs_hi[:, kk, P * h:P * (h + 1)], w_lo[:, s, wv], start=False, stop=False)
                    ins = pe.matmul(out, xs_lo[:, kk, P * h:P * (h + 1)], w_hi[:, s, wv], start=False, stop=(kk == KC - 1))
                ins.then_inc(used, 1)

            def turn_hidden(q, b):
                pe.wait_ge(e_hid_done, q + 1)
                bank(b)
                for k in range(GC):
                    ins = pe.transpose(ps[:, b, k * P:(k + 1) * P], e_hid[:, k * P:(k + 1) * P], ident[:, :])
                ins.then_inc(e_turned, 1)
                free[b] = (e_lo_done, q + 1)

            def down(n, s, q, e, g, c):
                pe.wait_ge(lo_done, n + 1)
                if c == 0:
                    pe.wait_ge(e_lo_done, q + 1)
                    if g == 0:
                        pe.wait_ge(y_scaled, HALVES * e)
                for k in range(2):
                    kk = 2 * c + k
                    first, last = g == 0 and kk == 0, g == GROUPS - 1 and kk == GC - 1
                    for half in range(HALVES):
                        out = ps[:, 4 + half, :]
                        wv = slice(d_model * k + half * BANK, d_model * k + (half + 1) * BANK)
                        pe.matmul(out, eh_hi[:, kk, :], w_hi[:, s, wv], start=first, stop=False)
                        pe.matmul(out, eh_hi[:, kk, :], w_lo[:, s, wv], start=False, stop=False)
                        ins = pe.matmul(out, eh_lo[:, kk, :], w_hi[:, s, wv], start=False, stop=last)
                ins.then_inc(used, 1)

            def combine(e, banks):
                pe.wait_ge(y_lo_done, e + 1)
                for c in range(KC):
                    b = banks[c % 2]
                    bank(b)
                    out = ps[:, b, 0:T]
                    pe.matmul(out, y_hi[:, c, :], selT, start=True, stop=False)
                    pe.matmul(out, y_lo[:, c, :], selT, start=False, stop=True).then_inc(comb_ps, 1)
                    free[b] = (combined, KC * e + c + 1)

            plan = misc_plan()

            def expert(e, first, pair, h, gather_next=False):
                for pos, kind, g in expert_chunks(first):
                    n, s = chunk_no(e, pos, first), slot_of(pos, first) % SPLIT_SLOTS
                    q = pos % 6
                    if q == 1 and (g or not first):
                        turn_hidden(GROUPS * e + g - 1, plan["hid", (g - 1) % GROUPS])
                    if kind == "gu":
                        if pos == 0 and h == 0:
                            pe.wait_ge(gathered, 8 * (pair + 1))
                        read = GROUPS * e + g - (1 if g else 0)
                        gate_up(n, s, q, g % 2 * 2, None if first and g < 2 else read, h)
                    elif g == 0:
                        down(n, s, GROUPS * e - 1, e - 1, GROUPS - 1, q - 4)
                    else:
                        down(n, s, GROUPS * e + g - 1, e, g - 1, q - 4)
                    if pos == 9:
                        if not first:
                            combine(e - 1, plan["comb"])
                        turn_sel(e, plan["selT"], h, 2 * (pair + 1))
                    if pos >= PER_EXPERT - 2 and gather_next:
                        s0 = 4 * (pos - PER_EXPERT + 2)
                        gather(pair + 1, s0, s0 + 4, 2 * TT * (pair + 2))

            def experts(pair, first=False, last=False):
                for b in (6, 7):
                    free[b] = (gathered, 8 * pair + b + 1)
                expert(2 * pair, first, pair, 0)
                expert(2 * pair + 1, False, pair, 1, not last)

            for k in (N_ADA // 2 - 2, N_ADA // 2 - 1):
                ada_turn(k)
            gather(0, 0, 8, 2 * TT)
            experts(0, first=True)
            with pe.Fori(1, n_exp // 2 - 1) as pair:
                experts(pair)
            experts(n_exp // 2 - 1, last=True)
            q = n_exp * GROUPS - 1
            turn_hidden(q, plan["hid", GROUPS - 1])
            for c in range(2):
                n = M1 - 2 + c
                down(n, n % SPLIT_SLOTS, q, n_exp - 1, GROUPS - 1, c)
            combine(n_exp - 1, (6, 7))

            many = pe.value_load(extra_i[0:1, EXTRA:EXTRA + 1], min_val=0, max_val=EXTRA)
            with pe.If(many > 0):
                with pe.Fori(0, many) as i:
                    k = n_exp + i
                    pe.wait_ge(combined, KC * k)
                    free[6] = free[7] = None
                    pe.wait_ge(sel_made, TT * (k + 1))
                    turn_sel(k, 7, 0, n_exp + 3 * i + 3)
                    gather(n_exp // 2 + i, 0, 8, TT * (k + 1), P)
                    pe.wait_ge(gathered, 8 * (n_exp // 2 + i + 1))
                    for g in range(GROUPS):
                        q = GROUPS * k + g
                        for c in range(4):
                            n = M1 + PER_EXPERT * i + 6 * g + c
                            gate_up(n, (M1 + 6 * g + c) % SPLIT_SLOTS, c, 0, q, 0)
                        free[6] = None
                        if g:
                            pe.wait_ge(e_lo_done, q)
                        turn_hidden(q, 6)
                        for c in range(2):
                            n = M1 + PER_EXPERT * i + 6 * g + 4 + c
                            down(n, (M1 + 6 * g + 4 + c) % SPLIT_SLOTS, q, k, g, c)
                    free[6] = free[7] = None
                    combine(k, (6, 7))

            norm_sums(n_norms - 1)
            pe.wait_ge(fin_f, KC)
            for s in range(2 * TT):
                j, half = divmod(s, 2)
                rows = LAST if j == TT - 1 else P
                for c in range(4):
                    ins = pe.transpose(ps[0:rows, s, c * P:(c + 1) * P], hn[:, 4 * half + c, j * P:j * P + rows],
                                       ident[:, :])
                ins.then_inc(fin_ps, 1)



_INS = ["x_prompt", "x_sample", "c_prompt", "c_sample", "state_conv", "state_pool", "w_ada", "b_ada", "g_mix",
        "g_ffn", "w_in", "conv_w", "pool_w", "pool_scale", "g_conv_out", "g_pool_out", "w_out", "dense_w_gate",
        "dense_w_up", "dense_w_down", "router_w", "moe_w_gate", "moe_w_up", "moe_w_down", "g_final"]


def kernel(**inputs):
    import numpy as _np
    import concourse.bacc as _bacc
    from concourse import mybir as _mybir
    from concourse.bass_utils import run_bass_kernel_spmd as _run

    nc = _bacc.Bacc("TRN2", target_bir_lowering=False, num_devices=1)
    arrays, a, o = {}, {}, {}
    for name in _INS:
        v = _np.ascontiguousarray(inputs[name])
        arrays[f"in_{name}_dram"] = v
        a[name] = nc.dram_tensor(f"in_{name}_dram", v.shape, _mybir.dt.from_np(v.dtype), kind="ExternalInput").ap()
    outs = {
        "y_prompt": inputs["x_prompt"].shape, "y_sample": inputs["x_sample"].shape,
        "conv_prompt": (inputs["state_conv"].shape[0], inputs["x_prompt"].shape[0]) + inputs["state_conv"].shape[2:],
        "pool_prompt": (inputs["state_pool"].shape[0], inputs["x_prompt"].shape[0]) + inputs["state_pool"].shape[2:],
        "conv_sample": inputs["state_conv"].shape, "pool_sample": inputs["state_pool"].shape,
    }
    for name, shape in outs.items():
        o[name] = nc.dram_tensor(f"out_{name}_dram", tuple(shape), _mybir.dt.float32, kind="ExternalOutput").ap()
    hybrid_trunk(nc, a, o)
    r = _run(nc, [arrays], core_ids=[0])
    return tuple(r.results[0][f"out_{name}_dram"] for name in outs)
```

```python
from contextlib import ExitStack

import concourse.bass as bass
from concourse import mybir

F32 = mybir.dt.float32
F32R = mybir.dt.float32r
I32 = mybir.dt.int32
ALU = mybir.AluOpType
ACT = mybir.ActivationFunctionType
AX_X = mybir.AxisListType.X

P = 128
EPS = 1e-6
RAW_SLOTS = 6
SPLIT_SLOTS = 3
CHUNK = 2048
BANK = 512
HIST = 15
WINDOWS = (2, 4, 8, 16)
ADA_PARTS = 6
SH1, SC1, GT1, SH2, SC2, GT2 = range(ADA_PARTS)


def hybrid_trunk(nc, a, o):
    depth, d_model, _ = a["w_ada"].shape
    seq = a["x_prompt"].shape[1]
    dec = a["x_sample"].shape[0]
    T = seq + dec
    S = dec + 1
    KC = d_model // P
    GB = a["pool_w"].shape[1]
    d_ff = a["dense_w_gate"].shape[2]
    FC = d_ff // P
    n_exp = a["moe_w_gate"].shape[1]
    d_ffe = a["moe_w_gate"].shape[3]
    GROUPS = d_ffe // BANK
    GC = BANK // P
    TT = -(-T // P)
    LAST = T - (TT - 1) * P
    HALVES = d_model // BANK
    ZU = HIST + seq + dec * (HIST + 1)
    ZV = 2 + seq + dec * 3
    SU = HIST + seq
    SV = 2 + seq
    EXTRA = 4
    assert depth == 2 and GB == 4 and KC == 8 and d_model == 2 * BANK and d_ffe % BANK == 0
    assert (TT - 1) * n_exp >= EXTRA and 2 * T < 5 * (P + 1)

    stream = []

    def cols_256(kind, l, w, rows, j, first=True, last=True, k0=0):
        src = w.rearrange("(k p) n -> p k n", p=P)[:, k0:k0 + rows, 256 * j:256 * j + 256]
        return dict(kind=kind, layer=l, nk=rows, k0=k0, j=j, src=src, first=first, last=last, width=256)

    ADA_Q = KC // 2

    def ada(l, *what):
        return [cols_256("ada", l, a["w_ada"][l], KC, ADA_Q * part + q) for part in what for q in range(ADA_Q)]

    def in_phase(l):
        half = GB // 2
        js = [3 * half + j for j in range(half)] + [half + j for j in range(2 * half)] + list(range(half))
        cs = [cols_256("in", l, a["w_in"][l], KC, j) for j in js]
        cs.insert(3 * half, dict(kind="pool", layer=l, nk=GB, k0=0, j=0, first=True, last=True, width=P,
                                 src=a["pool_w"][l].rearrange("g c d -> c g d")))
        return cs

    def out_phase(l):
        return [cols_256("out", l, a["w_out"][l], KC, j) for j in range(KC // 2)]

    def ffn_phase(l):
        cs = []
        for j in range(FC // 2):
            cs.append(cols_256("gate", l, a["dense_w_gate"][l // 2], KC, j))
            cs.append(cols_256("up", l, a["dense_w_up"][l // 2], KC, j))
        for j in range(KC // 2):
            for k0 in range(0, FC, KC):
                cs.append(cols_256("down", l, a["dense_w_down"][l // 2], min(KC, FC - k0), j,
                                   k0 == 0, k0 + KC >= FC, k0))
        return cs

    def mix_in(phase, more):
        assert len(more) < len(phase)
        return [c for i, ch in enumerate(phase) for c in [ch] + more[i:i + 1]]

    out0, shift, last_gate = out_phase(0), ada(0, SH2), ada(1, GT2)
    phases = [in_phase(0),
              out0[:1] + shift[:2] + out0[1:2] + shift[2:] + out0[2:],
              mix_in(ffn_phase(0), ada(0, GT2) + ada(1, SH1, SC1, GT1, SH2)),
              in_phase(1),
              out_phase(1)]
    fillers = [ada(0, SH1, SC1), ada(0, GT1), ada(0, SC2), ada(1, SC2), last_gate[:2], last_gate[2:]]
    for fill, phase in zip(fillers, phases + [[]]):
        stream += phase[:SPLIT_SLOTS] + fill + phase[SPLIT_SLOTS:]
    split = [ch for phase in phases for ch in phase]
    for n, ch in enumerate(stream):
        ch["n"] = n
    for m, ch in enumerate(split):
        ch["m"] = m
    in_order = [ch for fill, phase in zip(fillers, phases + [[]]) for ch in fill + phase if ch["kind"] == "ada"]
    for k, ch in enumerate(in_order):
        ch["a"] = k
    for k, ch in enumerate([ch for fill in fillers for ch in fill]):
        ch["u"] = k
    N_ADA = len(in_order)
    UNSPLIT = len(stream) - len(split)
    M0 = len(split)
    PER_EXPERT = 6 * GROUPS
    M1 = M0 + n_exp * PER_EXPERT
    assert UNSPLIT % RAW_SLOTS == 0

    blocks, taken = [], {"act": 0, "dve": 0}
    for i, ch in enumerate(split):
        if ch["kind"] == "down" and not ch["first"]:
            ch["blocks"] = split[i - 1]["blocks"]
            continue
        ch["blocks"] = []
        if ch["kind"] == "ada":
            continue
        for b in range(GB if ch["kind"] == "pool" else 2):
            col = b if ch["kind"] == "pool" else 2 * ch["j"] + b
            eng = "dve"
            if ch["kind"] in ("gate", "pool") or ch["kind"] == "in" and (col >= 3 * GB or GB <= col < 2 * GB):
                eng = "act"
            taken[eng] += 1
            ch["blocks"].append(len(blocks))
            blocks.append(dict(eng=eng, count=taken[eng], col=col))
    n_norms = 2 * depth + 1

    ctx = ExitStack()
    with ctx:
        def sb(name, shape, dt=F32):
            return ctx.enter_context(nc.sbuf_tensor(name, shape, dt))

        def sem(name):
            return ctx.enter_context(nc.semaphore(name))

        raw = sb("raw", [P, RAW_SLOTS, CHUNK])
        w_hi = sb("w_hi", [P, SPLIT_SLOTS, CHUNK], F32R)
        w_lo = sb("w_lo", [P, SPLIT_SLOTS, CHUNK], F32R)
        xT = sb("xT", [P, KC, T])
        h_hi = sb("h_hi", [P, KC, T], F32R)
        h_lo = sb("h_lo", [P, KC, T], F32R)
        parts = sb("parts", [P, 2 * FC * T], F32R)
        work = sb("work", [P, 8192])
        modT = sb("modT", [P, depth, ADA_PARTS * KC, S])
        par = sb("par", [P, 184])
        ident = sb("ident", [P, P])
        ones = sb("ones", [P, P])
        slot_no = sb("slot_no", [P, P])
        silu_c = sb("silu_c", [P, KC, S])
        last_rows = sb("last_rows", [P, GB, HIST + dec + 2 + 2 * dec])
        ROWS = HIST + dec + 2 + 2 * dec

        hid_hi = parts[:, 0:FC * T].rearrange("p (k t) -> p k t", t=T)
        hid_lo = parts[:, FC * T:2 * FC * T].rearrange("p (k t) -> p k t", t=T)

        at = 0

        def part(n):
            nonlocal at
            at += n
            assert at <= 2 * FC * T
            return parts[:, at - n:at]

        tok_hi = part(TT * d_model).rearrange("p (j d) -> p j d", j=TT)
        tok_lo = part(TT * d_model).rearrange("p (j d) -> p j d", j=TT)
        sel = part(TT * 2 * P).rearrange("p (j s) -> p j s", j=TT)
        selT = part(T)
        eh_hi = part(GC * P).rearrange("p (k s) -> p k s", k=GC)
        eh_lo = part(GC * P).rearrange("p (k s) -> p k s", k=GC)
        y_hi = part(d_model).rearrange("p (c d) -> p c d", c=KC)
        y_lo = part(d_model).rearrange("p (c d) -> p c d", c=KC)
        xs_hi = h_hi[:, :, 0:2 * P]
        xs_lo = h_lo[:, :, 0:2 * P]

        x_rows = work[:, 0:3 * d_model].rearrange("p (j d) -> p j d", j=3)
        c_rows = work[:, 3 * d_model:4 * d_model]
        par_rows = work[:, 4 * d_model + 2 * P:4 * d_model + 4 * P].rearrange("p (j d) -> p j d", j=2)
        zu = work[:, 0:GB * ZU].rearrange("p (b z) -> p b z", b=GB)
        at_v = GB * ZU
        zv = work[:, at_v:at_v + GB * ZV].rearrange("p (b z) -> p b z", b=GB)
        at_b = at_v + GB * ZV
        b_gate = work[:, at_b:at_b + GB * T].rearrange("p (b t) -> p b t", b=GB)
        at_c = at_b + GB * T
        c_gate = work[:, at_c:at_c + GB * T].rearrange("p (b t) -> p b t", b=GB)
        at_s = at_c + GB * T
        conv = b_gate
        diff = parts[:, 0:2 * GB * T].rearrange("p (h b t) -> p h b t", h=2, b=GB)
        sum_a = work[:, at_s:at_s + GB * ZU].rearrange("p (b z) -> p b z", b=GB)
        at_t = at_s + GB * ZU
        sum_b = work[:, at_t:at_t + 3 * ZU].rearrange("p (b z) -> p b z", b=3)
        at_w = at_t + 3 * ZU
        scr = work[:, at_w:at_w + 2 * (ZV - 2)].rearrange("p (b z) -> p b z", b=2)
        assert at_w + 2 * (ZV - 2) <= 8192
        y_pool = work[:, at_s:at_s + GB * T].rearrange("p (b t) -> p b t", b=GB)
        msq = work[:, at_t:at_t + 2 * T].rearrange("p (b t) -> p b t", b=2)
        mix_squares = work[:, at_t + 2 * T:at_t + 4 * T].rearrange("p (b t) -> p b t", b=2)
        assert at_t + 4 * T <= at_w
        pool_rows = work[:, at_s:at_s + BANK]
        conv_rows = work[:, at_t:at_t + BANK]
        new_rows = work[:, at_s + GB * T:at_s + GB * T + BANK]
        sq = work[:, 0:KC * T].rearrange("p (c t) -> p c t", c=KC)
        hn = work[:, KC * T:2 * KC * T].rearrange("p (c t) -> p c t", c=KC)
        rstd = work[:, at_w:at_w + T]
        var = work[:, at_w + T:at_w + 2 * T]
        silu_g = work[:, 0:2 * 2 * T].rearrange("p (b t) -> p b t", b=4)
        hid_f = work[:, 4 * T:4 * T + 2 * T].rearrange("p (b t) -> p b t", b=2)
        acc = work[:, 0:KC * T].rearrange("p (c t) -> p c t", c=KC)
        e_silu = work[:, 2112:2112 + BANK]
        e_hid = work[:, 2624:2624 + BANK]
        y_f = work[:, 3136:3136 + d_model]
        assert KC * T <= 2112
        r0 = 2 * KC * T
        E = n_exp
        logit = work[:, r0:r0 + TT * E].rearrange("p (j e) -> p j e", j=TT)
        r0 += TT * E
        cmp1 = work[:, r0:r0 + TT * E * E].rearrange("p (j e f) -> p j e f", j=TT, e=E)
        r0 += TT * E * E
        cmp2 = work[:, r0:r0 + TT * E * E].rearrange("p (j e f) -> p j e f", j=TT, e=E)
        r0 += TT * E * E
        rank = work[:, r0:r0 + TT * E].rearrange("p (j e) -> p j e", j=TT)
        r0 += TT * E
        chosen = work[:, r0:r0 + TT * E].rearrange("p (j e) -> p j e", j=TT)
        r0 += TT * E
        lmax = work[:, r0:r0 + TT]
        lsum = work[:, r0 + TT:r0 + 2 * TT]
        r0 += 2 * TT
        earlier = work[:, r0:r0 + E * E].rearrange("p (e f) -> p e f", e=E)
        r0 += E * E
        real = work[:, r0:r0 + TT]
        r0 += TT
        gate = work[:, r0:r0 + E * TT].rearrange("p (e j) -> p e j", e=E)
        r0 += TT * E
        place = work[:, r0:r0 + E * TT].rearrange("p (e j) -> p e j", e=E)
        r0 += TT * E
        place_e = work[:, r0:r0 + 2 * TT].rearrange("p (e j) -> p e j", e=2)
        gate_e = work[:, r0 + 2 * TT:r0 + 4 * TT].rearrange("p (e j) -> p e j", e=2)
        gate_slot = work[:, r0 + 4 * TT:r0 + 4 * TT + 1]
        r0 += 4 * TT + 1
        tri = work[:, 6800:6800 + P]
        logitT = work[0:E, 7000:7000 + T]
        assert r0 <= 6800 and 7000 + T <= at_w
        NX = (TT - 1) * E
        more = work[:, r0:r0 + NX].rearrange("p (j e) -> p j e", e=E)
        more_row = work[:, r0:r0 + NX]
        more_no = work[:, r0 + NX:r0 + 2 * NX]
        tmp_row = work[:, r0 + 2 * NX:r0 + 3 * NX]
        code_e = work[:, r0 + 3 * NX:r0 + 4 * NX]
        code_s = work[:, r0 + 4 * NX:r0 + 5 * NX]
        r0 += 5 * NX
        hit = work[:, r0:r0 + EXTRA * NX].rearrange("p (i k) -> p i k", i=EXTRA)
        hit2 = work[:, r0 + EXTRA * NX:r0 + 2 * EXTRA * NX].rearrange("p (i k) -> p i k", i=EXTRA)
        r0 += 2 * EXTRA * NX
        extra_shift = work[:, r0:r0 + EXTRA]
        extra_f = work[:, r0 + EXTRA:r0 + 2 * EXTRA + 1]
        r0 += 2 * EXTRA + 1
        assert r0 <= at_w, (r0, at_w)
        m_hi_t = parts[:, 2 * GB * T:2 * GB * T + KC * T].rearrange("p (k t) -> p k t", t=T)
        m_lo_t = parts[:, 2 * GB * T + KC * T:2 * GB * T + 2 * KC * T].rearrange("p (k t) -> p k t", t=T)
        fix = sb("fix", [P, GB, HIST + 1])
        extra_i = sb("extra_i", [P, EXTRA + 1], I32)
        twice = sb("twice", [2 * S, S])
        silu_parts = sb("silu_parts", [P, KC, 2 * S], F32R)
        ada_rows = sb("ada_rows", [2 * S, BANK])
        iota_i = work[:, 4 * d_model + 4 * P:4 * d_model + 5 * P].bitcast(I32)
        router = sb("router", [P, KC, E])
        y_rows = work[:, 2 * KC * T:2 * KC * T + TT * d_model].rearrange("p (j d) -> p j d", j=TT)

        ps = ctx.enter_context(nc.psum_tensor("ps", [P, 8, BANK], F32))

        PAR_ROWS = 88
        G_MIX, G_FFN, G_FIN, CONV, PSC, GCO, GPO, BADA = 96, 112, 128, 136, 160, 168, 176, 0

        def pcol(i, n=1):
            return par[:, i:i + n]

        raw_in = [sem(f"raw_in{i}") for i in range(RAW_SLOTS)]
        hi_done = sem("hi_done")
        lo_done = sem("lo_done")
        used = sem("used")
        c_in = sem("c_in")
        x_in = sem("x_in")
        par_in = sem("par_in")
        states_in = [sem(f"states_in{l}") for l in range(depth)]
        router_in = sem("router_in")
        consts = sem("consts")
        pool_step = sem("pool_step")
        dve_step = sem("dve_step")
        act_step = sem("act_step")
        c_silu = sem("c_silu")
        turned = sem("turned")
        c_done = sem("c_done")
        c_hi = sem("c_hi")
        c_lo = sem("c_lo")
        ada_used = sem("ada_used")
        ada_copied = sem("ada_copied")
        ada_turned = sem("ada_turned")
        ada_out = sem("ada_out")
        par_done = sem("par_done")
        x_done = sem("x_done")
        x_last = sem("x_last")
        turned_out = sem("turned_out")
        squares = sem("squares")
        sums = sem("sums")
        inv_var = sem("inv_var")
        rstd_done = sem("rstd_done")
        normed = sem("normed")
        h_hi_done = sem("h_hi_done")
        h_lo_done = sem("h_lo_done")
        act_took = sem("act_took")
        dve_took = sem("dve_took")
        ffn_hi = sem("ffn_hi")
        ffn_lo = sem("ffn_lo")
        state_turned = sem("state_turned")
        state_put = sem("state_put")
        diff_done = sem("diff_done")
        diff_hi = sem("diff_hi")
        diff_lo = sem("diff_lo")
        mix_sq = sem("mix_sq")
        mix_inv = sem("mix_inv")
        mix_rstd = sem("mix_rstd")
        m_f = sem("m_f")
        m_hi = sem("m_hi")
        m_lo = sem("m_lo")
        tails = sem("tails")
        tails_turned = sem("tails_turned")
        tails_out = sem("tails_out")
        out_dma = sem("out_dma")
        shift_dma = sem("shift_dma")
        sq_used = sem("sq_used")
        logits_ps = sem("logits_ps")
        logits_row = sem("logits_row")
        logits_turned = sem("logits_turned")
        chosen_done = sem("chosen_done")
        cum_ps = sem("cum_ps")
        route_exp = sem("route_exp")
        route_max = sem("route_max")
        extra_done = sem("extra_done")
        tok_turned = sem("tok_turned")
        tok_copied = sem("tok_copied")
        tok_zero = sem("tok_zero")
        acc_zero = sem("acc_zero")
        sel_made = sem("sel_made")
        place_made = sem("place_made")
        gather_ps = sem("gather_ps")
        gathered = sem("gathered")
        e_silu_done = sem("e_silu_done")
        e_hid_done = sem("e_hid_done")
        e_turned = sem("e_turned")
        e_hi_done = sem("e_hi_done")
        e_lo_done = sem("e_lo_done")
        y_scaled = sem("y_scaled")
        y_hi_done = sem("y_hi_done")
        y_lo_done = sem("y_lo_done")
        selT_ps = sem("selT_ps")
        selT_done = sem("selT_done")
        comb_ps = sem("comb_ps")
        combined = sem("combined")
        fin_f = sem("fin_f")
        fin_ps = sem("fin_ps")
        fin_out = sem("fin_out")
        y_dma = sem("y_dma")

        block = ctx.enter_context(nc.Block())

        def slot_reader(ch):
            return (ada_used, ch["u"] + 1) if "u" in ch else (lo_done, ch["m"] + 1)

        def count_of(kind, l, col):
            return next(blocks[b]["count"] for ch in split if ch["kind"] == kind and ch["layer"] == l
                        for b in ch["blocks"] if blocks[b]["col"] == col)

        def misc_plan():
            return {("hid", GROUPS - 1): 6, ("hid", 0): 7, "comb": (6, 7), "selT": 6,
                    **{("hid", g): 7 if g % 2 else 6 for g in range(1, GROUPS - 1)}}

        def group_end(e, g, first):
            return (M0 + 3 if first and g == 0 else M0 - 2 + PER_EXPERT * e + 6 * g + 3) + 1

        def expert_end(e):
            return M0 - 2 + PER_EXPERT * (e + 1) + 6

        def expert_chunks(first):
            for pos in range(PER_EXPERT):
                g, q = divmod(pos, 6)
                if q >= 4 and g == 0 and first:
                    continue
                yield pos, ("gu" if q < 4 else "down"), g

        def chunk_no(e, pos, first):
            if first and pos < 4:
                return M0 + pos
            return M0 - 2 + PER_EXPERT * e + pos

        def slot_of(pos, first):
            return (M0 + pos) % 6 if first and pos < 4 else (M0 - 2 + pos) % 6

        y_f_blocks = y_f.rearrange("p (c d) -> p c d", c=KC)

        def half_of(half):
            return slice(half * KC // HALVES, (half + 1) * KC // HALVES)

        NORM_H = 2

        @block.sync
        def _(sp):
            sp.dma_start(c_rows[0:1, :], a["c_prompt"]).then_inc(c_in, 16)
            sp.dma_start(c_rows[1:S, :], a["c_sample"]).then_inc(c_in, 16)
            sp.dma_start(x_rows[:, 0:seq // P, :], a["x_prompt"][0].rearrange("(j p) d -> p j d", p=P))\
                .then_inc(x_in, 16)
            sp.dma_start(x_rows[0:dec, seq // P, :], a["x_sample"].rearrange("b s d -> (b s) d")).then_inc(x_in, 16)

            def load(m, slot, dst, src):
                if isinstance(m, int) and m < M0 + RAW_SLOTS:
                    sp.wait_ge(*slot_reader(stream[len(stream) - RAW_SLOTS + m - M0]))
                else:
                    sp.wait_ge(lo_done, m - RAW_SLOTS + 1)
                sp.dma_start(dst, src).then_inc(raw_in[slot], 16)

            for n, ch in enumerate(stream):
                if n >= RAW_SLOTS:
                    sp.wait_ge(*slot_reader(stream[n - RAW_SLOTS]))
                w = ch["width"]
                sp.dma_start(raw[:, n % RAW_SLOTS, 0:ch["nk"] * w].rearrange("p (k m) -> p k m", m=w), ch["src"])\
                    .then_inc(raw_in[n % RAW_SLOTS], 16)

            wg = a["moe_w_gate"][0].rearrange("e (k p) n -> e p k n", p=P)
            wu = a["moe_w_up"][0].rearrange("e (k p) n -> e p k n", p=P)
            wd = a["moe_w_down"][0].rearrange("e (k p) n -> e p k n", p=P)

            def gate_up(n, slot, e, g, q):
                w = (wg if q < 2 else wu)[e, :, 4 * (q % 2):4 * (q % 2) + 4, BANK * g:BANK * (g + 1)]
                load(n, slot, raw[:, slot, :].rearrange("p (k m) -> p k m", k=4), w)

            def down(n, slot, e, g, q):
                w = wd[e, :, GC * g + 2 * q:GC * g + 2 * q + 2, :]
                load(n, slot, raw[:, slot, :].rearrange("p (k m) -> p k m", k=2), w)

            def expert(e, first):
                for pos, kind, g in expert_chunks(first):
                    n, s, q = chunk_no(e, pos, first), slot_of(pos, first), pos % 6
                    if kind == "gu":
                        gate_up(n, s, e, g, q)
                    elif g == 0:
                        down(n, s, e - 1, GROUPS - 1, q - 4)
                    else:
                        down(n, s, e, g - 1, q - 4)

            expert(0, True)
            with sp.Fori(1, n_exp) as e:
                expert(e, False)
            for q in range(2):
                down(M1 - 2 + q, (M1 - 2 + q) % 6, n_exp - 1, GROUPS - 1, q)

            sp.wait_ge(extra_done, 1)
            many = sp.value_load(extra_i[0:1, EXTRA:EXTRA + 1], min_val=0, max_val=EXTRA)
            with sp.If(many > 0):
                with sp.Fori(0, many) as i:
                    e = sp.value_load(extra_i[0:1, bass.ds(i, 1)], min_val=0, max_val=n_exp - 1)
                    for pos in range(PER_EXPERT):
                        g, q = divmod(pos, 6)
                        n, s = M1 + PER_EXPERT * i + pos, (M1 + pos) % 6
                        if q < 4:
                            gate_up(n, s, e, g, q)
                        else:
                            down(n, s, e, g, q - 4)

        @block.gpsimd
        def _(pool):
            steps = [0]

            def link(ins):
                steps[0] += 1
                ins.then_inc(pool_step, 1)
                pool.wait_ge(pool_step, steps[0])

            link(pool.memset(ident[:, :], 0.0))
            link(pool.affine_select(out=ident[:, :], in_=ident[:, :], compare_op=ALU.not_equal, fill=1.0, base=0,
                                    pattern=[[-1, P]], channel_multiplier=1))
            pool.memset(ones[:, :], 1.0).then_inc(consts, 1)
            link(pool.memset(twice[:, :], 0.0))
            for base in (0, -S):
                link(pool.affine_select(out=twice[:, :], in_=twice[:, :], compare_op=ALU.not_equal, fill=1.0,
                                        base=base, pattern=[[-1, S]], channel_multiplier=1))
            link(pool.iota(iota_i, pattern=[[1, P]], base=0, channel_multiplier=0))
            link(pool.tensor_copy(slot_no[:, :], iota_i))
            for g, w in enumerate(WINDOWS):
                link(pool.tensor_scalar(fix[:, g, :], slot_no[:, 0:HIST + 1], 1.0, float(w), ALU.add, ALU.min))
            pool.engine_nop().then_inc(consts, 1)
            pool.dma_start(router[:, :, :], a["router_w"][0].rearrange("(k p) e -> p k e", p=P)).then_inc(router_in, 16)

            for l in range(depth):
                pool.dma_start(o["pool_sample"][l, :, 0:HIST - 1, :], a["state_pool"][l, :, 1:HIST, :])\
                    .then_inc(shift_dma, 16)
            for l in range(depth):
                pool.wait_ge(act_took, count_of("in", l, 4 * GB - 1))
                pool.wait_ge(dve_took, count_of("in", l, 3 * GB - 1))
                pool.wait_ge(state_put, 2 * (l + 1))
                if l:
                    pool.wait_ge(tails_turned, l)
                pool.tensor_copy(last_rows[:, :, 0:HIST], zu[:, :, seq:seq + HIST]).then_inc(tails, 1)
                us = zu[:, :, SU:].rearrange("p b (s r) -> p b s r", r=HIST + 1)
                pool.tensor_copy(last_rows[:, :, HIST:HIST + dec], us[:, :, :, HIST]).then_inc(tails, 1)
                o1 = HIST + dec
                pool.tensor_copy(last_rows[:, :, o1:o1 + 2], zv[:, :, seq:seq + 2]).then_inc(tails, 1)
                vs = zv[:, :, SV:].rearrange("p b (s r) -> p b s r", r=3)
                pool.tensor_copy(last_rows[:, :, o1 + 2:o1 + 2 + 2 * dec].rearrange("p b (s r) -> p b s r", r=2),
                                 vs[:, :, :, 1:3]).then_inc(tails, 1)

            pool.wait_ge(tails_out, depth)
            pool.wait_ge(m_lo, 2 * depth)
            pool.wait_ge(out_dma, 64 * depth)
            link(pool.memset(tri, 0.0))
            link(pool.affine_select(out=tri, in_=tri, compare_op=ALU.is_ge, fill=1.0, base=0,
                                    pattern=[[-1, P]], channel_multiplier=1))
            link(pool.memset(earlier, 0.0))
            link(pool.affine_select(out=earlier, in_=earlier, compare_op=ALU.is_ge, fill=1.0, base=0,
                                    pattern=[[-1, E], [1, E]], channel_multiplier=0))
            link(pool.memset(real, 1.0))
            link(pool.affine_select(out=real[:, TT - 1:TT], in_=real[:, TT - 1:TT], compare_op=ALU.is_gt, fill=0.0,
                                    base=LAST, pattern=[[0, 1]], channel_multiplier=-1))
            link(pool.memset(logit, 0.0))
            pool.iota(code_e.bitcast(I32).rearrange("p (j e) -> p j e", e=E), pattern=[[0, TT - 1], [1, E]], base=0,
                      channel_multiplier=0).then_inc(pool_step, 1)
            pool.iota(code_s.bitcast(I32).rearrange("p (j e) -> p j e", e=E), pattern=[[P, TT - 1], [0, E]], base=P,
                      channel_multiplier=0).then_inc(pool_step, 1)
            steps[0] += 2
            pool.wait_ge(pool_step, steps[0])
            link(pool.tensor_copy(tmp_row, code_e.bitcast(I32)))
            link(pool.tensor_copy(code_e, tmp_row))
            link(pool.tensor_copy(tmp_row, code_s.bitcast(I32)))
            link(pool.tensor_copy(code_s, tmp_row))
            pool.wait_ge(sums, 4)
            link(pool.memset(tok_hi[:, TT - 1, :].bitcast(F32), 0.0))
            link(pool.memset(tok_lo[:, TT - 1, :].bitcast(F32), 0.0))
            pool.engine_nop().then_inc(tok_zero, 1)
            pool.memset(acc, 0.0).then_inc(acc_zero, 1)
            pool.wait_ge(shift_dma, 16 * depth)

        @block.scalar
        def _(act):
            steps = [0]

            def link(ins):
                steps[0] += 1
                ins.then_inc(act_step, 1)
                act.wait_ge(act_step, steps[0])

            act.dma_start(par_rows[0:depth * ADA_PARTS * KC, 0, :],
                          a["b_ada"].rearrange("l (j p) -> (l j) p", p=P)).then_inc(par_in, 16)
            small = [("g_mix", "l (j p) -> (l j) p"), ("g_ffn", "l (j p) -> (l j) p"), ("g_final", "(j p) -> j p"),
                     ("conv_w", "l k (j p) -> (l k j) p"), ("pool_scale", "l (j p) -> (l j) p"),
                     ("g_conv_out", "l (j p) -> (l j) p"), ("g_pool_out", "l (j p) -> (l j) p")]
            r = 0
            for name, pattern in small:
                v = a[name].rearrange(pattern, p=P)
                act.dma_start(par_rows[r:r + v.shape[0], 1, :], v).then_inc(par_in, 16)
                r += v.shape[0]
                if name == "g_ffn":
                    act.wait_ge(c_in, 32)
                    act.activation(c_rows[0:S, :], c_rows[0:S, :], ACT.Silu).then_inc(c_silu, 1)
            assert r == PAR_ROWS
            act.wait_ge(turned, 1)
            act.activation(silu_c[:, :, :], ps[:, 4, 0:KC * S].rearrange("p (k s) -> p k s", k=KC), ACT.Copy)\
                .then_inc(c_done, 1)
            act.wait_ge(c_done, 1)
            act.activation(silu_parts[:, :, 0:S], silu_c[:, :, :], ACT.Copy).then_inc(c_hi, 1)

            def load_states(l):
                act.dma_start(pool_rows[0:dec * HIST, :], a["state_pool"][l].rearrange("b r c -> (b r) c"))\
                    .then_inc(states_in[l], 16)
                act.dma_start(conv_rows[0:dec * 2, :], a["state_conv"][l].rearrange("b r c -> (b r) c"))\
                    .then_inc(states_in[l], 16)

            load_states(0)

            def hi(m, slot, width=CHUNK):
                if not isinstance(m, int) or m >= SPLIT_SLOTS:
                    act.wait_ge(used, m - SPLIT_SLOTS + 1)
                act.activation(w_hi[:, slot % SPLIT_SLOTS, 0:width], raw[:, slot, 0:width], ACT.Copy)\
                    .then_inc(hi_done, 1)

            def landed(slot, turn):
                act.wait_ge(raw_in[slot], 16 * (turn + 1))

            def hi_of(ch):
                n, m, width = ch["n"], ch["m"], ch["nk"] * ch["width"]
                landed(n % RAW_SLOTS, n // RAW_SLOTS)
                if m >= SPLIT_SLOTS:
                    act.wait_ge(used, m - SPLIT_SLOTS + 1)
                act.activation(w_hi[:, m % SPLIT_SLOTS, 0:width], raw[:, n % RAW_SLOTS, 0:width], ACT.Copy)\
                    .then_inc(hi_done, 1)

            def ada_pair(odd, rows=S):
                k = odd["a"] // 2
                if k:
                    act.wait_ge(ada_turned, k)
                act.activation(ada_rows[0:rows, :], ps[0:rows, 6 + k % 2, :], ACT.Copy).then_inc(ada_copied, 1)

            def ada_pairs(chunks):
                for odd in chunks[1::2]:
                    act.wait_ge(ada_used, odd["u"] + 1)
                    ada_pair(odd)

            def square(c):
                act.activation(sq[:, c, :], xT[:, c, :], ACT.Square).then_inc(squares, 1)

            def root(k):
                act.wait_ge(inv_var, k + 1)
                act.activation(rstd, var, ACT.Sqrt).then_inc(rstd_done, 1)

            def norm_hi(k, halves=range(NORM_H)):
                for half in halves:
                    c0, c1 = half * KC // NORM_H, (half + 1) * KC // NORM_H
                    act.wait_ge(normed, NORM_H * k + half + 1)
                    act.activation(h_hi[:, c0:c1, :], hn[:, c0:c1, :], ACT.Copy).then_inc(h_hi_done, 1)

            def mix_square(l, b, count):
                if count:
                    act.wait_ge(sq_used, count)
                src = y_pool[:, b - GB, :] if b >= GB else conv[:, b, :]
                act.activation(mix_squares[:, b % 2, :], src, ACT.Square).then_inc(mix_sq, 1)

            def take(ch):
                l, kind = ch["layer"], ch["kind"]
                act.wait_ge(used, ch["m"] + 1)
                if kind == "ada" and ch["a"] % 2:
                    ada_pair(ch, 2 * S)
                for b in ch["blocks"]:
                    blk, col = blocks[b], blocks[b]["col"]
                    src = ps[:, b % 4, 0:T]
                    if kind in ("out", "down") and ch["last"]:
                        act.wait_ge(dve_took, blk["count"])
                        square(col)
                    elif blk["eng"] != "act":
                        continue
                    elif kind == "in" and col < 2 * GB:
                        act.activation(c_gate[:, col - GB, :], src, ACT.Copy).then_inc(act_took, 1)
                    elif kind == "in":
                        u = col - 3 * GB
                        us = zu[:, u, SU:].rearrange("p (s r) -> p s r", r=HIST + 1)
                        link(act.activation(us[:, :, HIST], src[:, seq:T], ACT.Copy))
                        act.activation(zu[:, u, HIST:SU], src[:, 0:seq], ACT.Copy).then_inc(act_took, 1)
                    elif kind == "gate":
                        if ch["j"] >= 2:
                            act.wait_ge(dve_took, count_of("up", l, col - 4))
                        act.activation(silu_g[:, 2 * (ch["j"] % 2) + col % 2, :], src, ACT.Silu)\
                            .then_inc(act_took, 1)
                    elif kind == "pool":
                        act.activation(y_pool[:, col, :], src, ACT.Copy, scale=pcol(PSC + GB * l + col))\
                            .then_inc(act_took, 1)
                if kind == "pool":
                    act.wait_ge(act_took, count_of("pool", l, GB - 1))
                    for b in range(GB):
                        mix_square(l, GB + b, 2 * GB * l + b - 1 if b >= 2 else 2 * GB * l)
                if kind == "up":
                    for b in range(2):
                        f = 2 * ch["j"] + b
                        act.wait_ge(dve_took, count_of("up", l, f))
                        act.activation(hid_hi[:, f, :], hid_f[:, b, :], ACT.Copy).then_inc(ffn_hi, 1)

            def diff_hi_of(l, g):
                act.wait_ge(diff_done, GB * l + g + 1)
                act.activation(diff[:, 0, g, :], scr[:, g % 2, 0:T], ACT.Copy).then_inc(diff_hi, 1)

            def mix_root(l, half):
                act.wait_ge(mix_inv, 2 * l + half + 1)
                act.activation(msq[:, half, :], msq[:, half, :], ACT.Sqrt).then_inc(mix_rstd, 1)

            def mix_hi(l, half):
                act.wait_ge(m_f, 2 * l + half + 1)
                for b in range(GB):
                    src, g = (conv, GCO) if half else (y_pool, GPO)
                    ins = act.activation(m_hi_t[:, (GB if half == 0 else 0) + b, :], src[:, b, :], ACT.Copy,
                                         scale=pcol(g + GB * l + b))
                ins.then_inc(m_hi, 1)

            def tails_scalar(l):
                act.wait_ge(tails_turned, l + 1)
                if l:
                    act.wait_ge(out_dma, 64 * l)
                act.activation(new_rows[0:ROWS, :], ps[0:ROWS, 5, :], ACT.Copy).then_inc(tails_out, 1)
                act.wait_ge(tails_out, l + 1)
                o1 = HIST + dec
                act.dma_start(o["pool_prompt"][l, 0], new_rows[0:HIST, :]).then_inc(out_dma, 16)
                act.dma_start(o["pool_sample"][l, :, HIST - 1, :], new_rows[HIST:o1, :]).then_inc(out_dma, 16)
                act.dma_start(o["conv_prompt"][l, 0], new_rows[o1:o1 + 2, :]).then_inc(out_dma, 16)
                act.dma_start(o["conv_sample"][l].rearrange("b r c -> (b r) c"), new_rows[o1 + 2:ROWS, :])\
                    .then_inc(out_dma, 16)

            def phase_in(l, phase, following, late=()):
                for i, ch in enumerate(phase):
                    if i >= SPLIT_SLOTS:
                        hi_of(ch)
                        take(phase[i - SPLIT_SLOTS])
                    if i == SPLIT_SLOTS:
                        ada_pairs(late)
                    if i == 5:
                        diff_hi_of(l, 0)
                        diff_hi_of(l, 1)
                    if i == 6:
                        diff_hi_of(l, 2)
                        diff_hi_of(l, 3)
                take(phase[6])
                hi_of(following[0])
                mix_root(l, 0)
                for b in range(GB):
                    if b == 2:
                        mix_hi(l, 0)
                        hi_of(following[1])
                    act.wait_ge(dve_took, count_of("in", l, b))
                    mix_square(l, b, 2 * GB * l + GB + b - 1 if b >= 2 else 2 * GB * l + GB)
                hi_of(following[2])
                mix_root(l, 1)
                mix_hi(l, 1)

            def phase_rest(phase, following):
                for i, ch in enumerate(phase):
                    if i >= SPLIT_SLOTS:
                        hi_of(ch)
                        take(phase[i - SPLIT_SLOTS])
                if following:
                    hi_of(following[0])
                for ch in phase[-SPLIT_SLOTS:]:
                    take(ch)
                if following:
                    hi_of(following[1])

            hi_of(phases[0][0])
            act.wait_ge(x_done, 1)
            for c in range(KC):
                square(c)
            hi_of(phases[0][1])
            root(0)
            act.wait_ge(turned, 3 + KC)
            act.activation(par[:, 0:96], ps[:, 5, 0:96], ACT.Copy).then_inc(par_done, 1)
            act.activation(par[:, 96:96 + PAR_ROWS], ps[:, 5, 96:96 + PAR_ROWS], ACT.Copy).then_inc(par_done, 1)
            hi_of(phases[0][2])
            ada_pairs(fillers[0][:-2])
            norm_hi(0, [0])
            ada_pairs(fillers[0][-2:])
            norm_hi(0, [1])
            phase_in(0, phases[0], phases[1])
            ada_pairs(fillers[1])
            tails_scalar(0)
            act.wait_ge(m_lo, 2)
            load_states(1)
            phase_rest(phases[1], phases[2])
            root(1)
            hi_of(phases[2][2])
            ada_pairs(fillers[2][:2])
            norm_hi(1, [0])
            ada_pairs(fillers[2][2:])
            norm_hi(1, [1])
            phase_rest(phases[2], phases[3])
            root(2)
            hi_of(phases[3][2])
            ada_pairs(fillers[3][:2])
            norm_hi(2)
            phase_in(1, phases[3], phases[4], fillers[3][2:])
            tails_scalar(1)
            ada_pairs(fillers[4])
            phase_rest(phases[4], None)
            root(3)
            ada_pairs(fillers[5])
            norm_hi(3)
            def landed_m(slot, turn):
                landed(slot, turn + UNSPLIT // RAW_SLOTS)

            def take_tokens(s0, s1):
                for s in range(s0, s1):
                    j, part_no, half = s // 4, s // 2 % 2, s % 2
                    rows = LAST if j == TT - 1 else P
                    act.wait_ge(tok_turned, s + 1)
                    dst = (tok_hi if part_no == 0 else tok_lo)[0:rows, j, half * BANK:(half + 1) * BANK]
                    act.activation(dst, ps[0:rows, s % 4, :], ACT.Copy).then_inc(tok_copied, 1)

            for k in range(SPLIT_SLOTS):
                landed_m((M0 + k) % 6, (M0 + k) // 6)
                hi(M0 + k, (M0 + k) % 6)
            act.wait_ge(logits_ps, 1)
            act.activation(logitT, ps[0:E, 4, 0:T], ACT.Copy).then_inc(logits_row, 1)
            act.wait_ge(tok_zero, 1)
            take_tokens(0, 4 * TT)
            act.wait_ge(route_max, 1)
            act.wait_ge(chosen_done, 1)
            act.activation(rank, logit, ACT.Exp).then_inc(route_exp, 1)

            def take_gather(e, width=2 * P):
                for s in range(8):
                    act.wait_ge(gather_ps, 8 * e + s + 1)
                    dst = (xs_hi if s < 4 else xs_lo)[:, 2 * (s % 4):2 * (s % 4) + 2, 0:width]
                    src = ps[:, 6 + s % 2, :].rearrange("p (c s) -> p c s", c=2)[:, :, 0:width]
                    act.activation(dst, src, ACT.Copy).then_inc(gathered, 1)

            def silu(q, bank, ready):
                act.wait_ge(used, ready)
                act.wait_ge(e_hid_done, q)
                act.activation(e_silu, ps[:, bank, :], ACT.Silu).then_inc(e_silu_done, 1)

            def split_hidden(q, bank):
                act.wait_ge(e_turned, q + 1)
                act.activation(eh_hi, ps[:, bank, :].rearrange("p (k s) -> p k s", k=GC), ACT.Copy)\
                    .then_inc(e_hi_done, 1)

            def scale_y(e, ready):
                act.wait_ge(used, ready)
                for half in range(HALVES):
                    act.activation(y_f[:, half * BANK:(half + 1) * BANK], ps[:, 4 + half, :], ACT.Copy,
                                   scale=gate_slot).then_inc(y_scaled, 1)
                for half in range(HALVES):
                    act.wait_ge(y_scaled, HALVES * e + half + 1)
                    act.activation(y_hi[:, half_of(half), :], y_f_blocks[:, half_of(half), :], ACT.Copy)\
                        .then_inc(y_hi_done, 1)

            def take_selT(e, bank):
                act.wait_ge(selT_ps, e + 1)
                act.activation(selT, ps[:, bank, 0:T], ACT.Copy).then_inc(selT_done, 1)
                act.activation(gate_slot, ps[:, bank, T:T + 1], ACT.Copy).then_inc(selT_done, 1)

            plan = misc_plan()

            def expert(e, first, gather=None, split_before=0):
                for pos, kind, g in expert_chunks(first):
                    n, s = chunk_no(e, pos, first), slot_of(pos, first)
                    if pos == 0 and not first:
                        silu(GROUPS * e - 1, (GROUPS - 1) % 2 * 2, group_end(e, -1, first))
                    if not (first and pos < split_before):
                        landed_m(s, n // 6 if isinstance(n, int) else (M0 - 2 + pos) // 6 + GROUPS * e)
                        hi(n, s)
                    if pos % 6 == 0 and pos:
                        silu(GROUPS * e + g - 1, (g - 1) % GROUPS % 2 * 2, group_end(e, g - 1, first))
                    if pos == 0 and gather is not None:
                        take_gather(gather)
                    if pos % 6 == 3 and (pos > 3 or not first):
                        split_hidden(GROUPS * e + g - 1, plan["hid", (g - 1) % GROUPS])
                    if pos == 8 and not first:
                        scale_y(e - 1, expert_end(e - 1))
                    if pos == 13:
                        take_selT(e, plan["selT"])

            take_gather(0)
            expert(0, True, None, SPLIT_SLOTS)
            expert(1, False)
            with act.Fori(1, n_exp // 2) as pair:
                expert(2 * pair, False, pair)
                expert(2 * pair + 1, False)
            for q in range(2):
                n = M1 - 2 + q
                landed_m(n % 6, n // 6)
                hi(n, n % 6)
                if q == 0:
                    silu(n_exp * GROUPS - 1, (GROUPS - 1) % 2 * 2, group_end(n_exp, -1, False))
            split_hidden(n_exp * GROUPS - 1, plan["hid", GROUPS - 1])
            scale_y(n_exp - 1, M1)

            act.wait_ge(extra_done, 1)
            many = act.value_load(extra_i[0:1, EXTRA:EXTRA + 1], min_val=0, max_val=EXTRA)
            with act.If(many > 0):
                with act.Fori(0, many) as i:
                    take_selT(n_exp + i, 7)
                    take_gather(n_exp // 2 + i, P)
                    for pos in range(PER_EXPERT):
                        g, q = divmod(pos, 6)
                        landed_m((M1 + pos) % 6, (M1 + pos) // 6 + GROUPS * i)
                        hi(M1 + PER_EXPERT * i + pos, (M1 + pos) % 6)
                        if q == 5:
                            silu(GROUPS * (n_exp + i) + g, 0, M1 + PER_EXPERT * i + 6 * g + 4)
                            split_hidden(GROUPS * (n_exp + i) + g, 6)
                    scale_y(n_exp + i, M1 + PER_EXPERT * (i + 1))

            for c in range(KC):
                act.wait_ge(x_last, c + 1)
                square(c)
            root(n_norms - 1)
            act.wait_ge(out_dma, 64 * depth)
            for s in range(2 * TT):
                half, j = divmod(s, TT)
                rows = LAST if j == TT - 1 else P
                act.wait_ge(fin_ps, s + 1)
                act.activation(y_rows[0:rows, j, half * BANK:(half + 1) * BANK], ps[0:rows, s, :], ACT.Copy)\
                    .then_inc(fin_out, 1)
            for j in range(TT):
                act.wait_ge(fin_out, TT + j + 1)
                if j < TT - 1:
                    act.dma_start(o["y_prompt"][0, j * P:(j + 1) * P, :], y_rows[:, j, :]).then_inc(y_dma, 16)
                else:
                    act.dma_start(o["y_sample"].rearrange("b s d -> (b s) d"), y_rows[0:LAST, j, :])\
                        .then_inc(y_dma, 16)
            act.wait_ge(y_dma, 16 * TT)

        @block.vector
        def _(dve):
            steps = [0]

            def link(ins):
                steps[0] += 1
                ins.then_inc(dve_step, 1)
                dve.wait_ge(dve_step, steps[0])

            dve.wait_ge(consts, 2)
            link(dve.reciprocal(fix[:, :, :], fix[:, :, :]))
            for g, w in enumerate(WINDOWS):
                link(dve.tensor_scalar(fix[:, g, :], fix[:, g, :], float(w), None, ALU.mult))

            def lo(m, slot, width=CHUNK):
                dve.wait_ge(hi_done, m + 1)
                dve.tensor_tensor(w_lo[:, slot % SPLIT_SLOTS, 0:width], raw[:, slot, 0:width],
                                  w_hi[:, slot % SPLIT_SLOTS, 0:width].bitcast(F32), ALU.subtract)\
                    .then_inc(lo_done, 1)

            def lo_of(ch):
                m, raw_slot, width = ch["m"], ch["n"] % RAW_SLOTS, ch["nk"] * ch["width"]
                dve.wait_ge(hi_done, m + 1)
                dve.tensor_tensor(w_lo[:, m % SPLIT_SLOTS, 0:width], raw[:, raw_slot, 0:width],
                                  w_hi[:, m % SPLIT_SLOTS, 0:width].bitcast(F32), ALU.subtract)\
                    .then_inc(lo_done, 1)

            for c in range(KC):
                dve.wait_ge(turned, 2 + c)
                dve.tensor_copy(xT[:, c, :], ps[:, c % 4, 0:T]).then_inc(turned_out, 1)
            dve.wait_ge(turned_out, KC)
            dve.engine_nop().then_inc(x_done, 1)
            dve.wait_ge(c_hi, 1)
            dve.tensor_tensor(silu_parts[:, :, S:2 * S], silu_c[:, :, :], silu_parts[:, :, 0:S].bitcast(F32),
                              ALU.subtract).then_inc(c_lo, 1)

            def mod(l, what):
                return modT[:, l, what * KC:(what + 1) * KC, :]

            def ada_pairs(chunks):
                for odd in [ch for ch in chunks if ch["a"] % 2]:
                    k, l, b0 = odd["a"] // 2, odd["layer"], 2 * odd["j"] - 2
                    what = b0 // KC
                    dst = modT[:, l, b0:b0 + 4, :]
                    bias = pcol(BADA + ADA_PARTS * KC * l + b0, 4).unsqueeze(2).to_broadcast([P, 4, S])
                    dve.wait_ge(ada_turned, k + 1)
                    dve.tensor_tensor(dst, ps[:, 5, 0:4 * S].rearrange("p (b s) -> p b s", b=4), bias, ALU.add)\
                        .then_inc(ada_out, 1)
                    dve.wait_ge(ada_out, k + 1)
                    if what in (SC1, SC2):
                        g = pcol((G_MIX if what == SC1 else G_FFN) + KC * l + b0 % KC, 4)
                        link(dve.scalar_tensor_tensor(out=dst, in0=dst, scalar=1.0,
                                                      in1=g.unsqueeze(2).to_broadcast([P, 4, S]),
                                                      op0=ALU.add, op1=ALU.mult))

            def norm_start(k):
                dve.wait_ge(sums, k + 1)
                link(dve.tensor_scalar(var, ps[:, 4, 0:T], 1.0 / d_model, EPS, ALU.mult, ALU.add))
                dve.reciprocal(var, var).then_inc(inv_var, 1)
                dve.wait_ge(rstd_done, k + 1)
                rb = rstd.unsqueeze(1).to_broadcast([P, KC, T])
                link(dve.tensor_tensor(hn, xT[:, :, :], rb, ALU.mult))

            def norm_half(k, half):
                l, first = divmod(k, 2)
                sc, sh = (mod(l, SC1), mod(l, SH1)) if first == 0 else (mod(l, SC2), mod(l, SH2))
                c0, c1 = half * KC // NORM_H, (half + 1) * KC // NORM_H
                hs = hn[:, c0:c1, seq:T]
                link(dve.tensor_tensor(hs, hs, sc[:, c0:c1, 1:S], ALU.mult))
                link(dve.tensor_tensor(hs, hs, sh[:, c0:c1, 1:S], ALU.add))
                for c in range(c0, c1):
                    ins = dve.tensor_scalar(hn[:, c, 0:seq], hn[:, c, 0:seq], sc[:, c, 0:1], sh[:, c, 0:1],
                                            ALU.mult, ALU.add)
                    if c < c1 - 1:
                        ins.then_inc(dve_step, 1)
                        steps[0] += 1
                dve.wait_ge(dve_step, steps[0])
                ins.then_inc(normed, 1)

            def norm_low(k, half):
                c0, c1 = half * KC // NORM_H, (half + 1) * KC // NORM_H
                dve.wait_ge(h_hi_done, NORM_H * k + half + 1)
                dve.tensor_tensor(h_lo[:, c0:c1, :], hn[:, c0:c1, :], h_hi[:, c0:c1, :].bitcast(F32),
                                  ALU.subtract).then_inc(h_lo_done, 1)

            def norm_end(k):
                for half in range(NORM_H):
                    norm_half(k, half)
                for half in range(NORM_H):
                    norm_low(k, half)

            def add_gated(l, gt, c, src_p, src_s, done):
                link(dve.tensor_tensor(scr[:, 0, 0:dec], src_s, mod(l, gt)[:, c, 1:S], ALU.mult))
                link(dve.tensor_tensor(xT[:, c, seq:T], xT[:, c, seq:T], scr[:, 0, 0:dec], ALU.add))
                ins = dve.scalar_tensor_tensor(out=xT[:, c, 0:seq], in0=src_p, scalar=mod(l, gt)[:, c, 0:1],
                                               in1=xT[:, c, 0:seq], op0=ALU.mult, op1=ALU.add)
                if done is not None:
                    ins.then_inc(done, 1)
                return ins

            def take(ch):
                dve.wait_ge(used, ch["m"] + 1)
                l = ch["layer"]
                if ch["kind"] == "ada":
                    ada_pairs([ch])
                for b in ch["blocks"]:
                    blk, col = blocks[b], blocks[b]["col"]
                    src = ps[:, b % 4, 0:T]
                    if blk["eng"] != "dve":
                        continue
                    if ch["kind"] == "in" and col < GB:
                        dve.tensor_tensor(conv[:, col, :], src, conv[:, col, :], ALU.mult).then_inc(dve_took, 1)
                    elif ch["kind"] == "in":
                        v = col - 2 * GB
                        dve.wait_ge(act_took, count_of("in", l, GB + v))
                        vs = zv[:, v, SV:].rearrange("p (s r) -> p s r", r=3)
                        link(dve.tensor_tensor(vs[:, :, 2], src[:, seq:T], c_gate[:, v, seq:T], ALU.mult))
                        dve.tensor_tensor(zv[:, v, 2:SV], src[:, 0:seq], c_gate[:, v, 0:seq], ALU.mult)\
                            .then_inc(dve_took, 1)
                    elif ch["kind"] == "out":
                        add_gated(l, GT1, col, src[:, 0:seq], src[:, seq:T], dve_took)
                    elif ch["kind"] == "down" and ch["last"]:
                        add_gated(l, GT2, col, src[:, 0:seq], src[:, seq:T], dve_took)
                    elif ch["kind"] == "up":
                        f = col
                        dve.wait_ge(act_took, count_of("gate", l, f))
                        if f >= 2:
                            dve.wait_ge(ffn_lo, f - 1)
                        dve.tensor_tensor(hid_f[:, col % 2, :], src, silu_g[:, 2 * (ch["j"] % 2) + col % 2, :],
                                          ALU.mult).then_inc(dve_took, 1)
                if ch["kind"] == "up":
                    for b in range(2):
                        f = 2 * ch["j"] + b
                        dve.wait_ge(ffn_hi, f + 1)
                        dve.tensor_tensor(hid_lo[:, f, :], hid_f[:, b, :], hid_hi[:, f, :].bitcast(F32),
                                          ALU.subtract).then_inc(ffn_lo, 1)

            def put_states(l):
                link(dve.memset(zu[:, :, 0:HIST], 0.0))
                link(dve.memset(zv[:, :, 0:2], 0.0))
                dve.wait_ge(state_turned, 2 * (l + 1))
                us = zu[:, :, SU:].rearrange("p b (s r) -> p b s r", r=HIST + 1)
                ups = ps[:, 5, 0:GB * dec * HIST].rearrange("p (b s r) -> p b s r", b=GB, s=dec)
                vs = zv[:, :, SV:].rearrange("p b (s r) -> p b s r", r=3)
                vps = ps[:, 4, 0:GB * dec * 2].rearrange("p (b s r) -> p b s r", b=GB, s=dec)
                for b in range(GB):
                    link(dve.tensor_copy(us[:, b, :, 0:HIST], ups[:, b]))
                    link(dve.tensor_copy(vs[:, b, :, 0:2], vps[:, b]))
                dve.engine_nop().then_inc(state_put, 1)
                dve.engine_nop().then_inc(state_put, 1)

            wins = [sum_a[:, 0, :], sum_b[:, 0, :], sum_a[:, 2, :], sum_b[:, 2, :]]

            def window_sums(l):
                dve.wait_ge(act_took, count_of("in", l, 4 * GB - 1))
                if l:
                    dve.wait_ge(out_dma, 64 * l)
                n1 = ZU - 1
                link(dve.tensor_tensor(sum_a[:, :, 0:n1], zu[:, :, 0:n1], zu[:, :, 1:ZU], ALU.add))
                n2 = n1 - 2
                link(dve.tensor_tensor(sum_b[:, :, 0:n2], sum_a[:, 1:, 0:n2], sum_a[:, 1:, 2:n2 + 2], ALU.add))
                n3 = n2 - 4
                link(dve.tensor_tensor(sum_a[:, 2:, 0:n3], sum_b[:, 1:, 0:n3], sum_b[:, 1:, 4:n3 + 4], ALU.add))
                n4 = n3 - 8
                link(dve.tensor_tensor(sum_b[:, 2, 0:n4], sum_a[:, 3, 0:n4], sum_a[:, 3, 8:n4 + 8], ALU.add))

            def window_diff(l, g):
                w = WINDOWS[g]
                s0 = HIST + 1 - w
                head = wins[g][:, s0:s0 + HIST + 1]
                link(dve.tensor_tensor(head, head, fix[:, g, :], ALU.mult))
                if g >= 2:
                    dve.wait_ge(diff_hi, GB * l + g - 1)
                link(dve.scalar_tensor_tensor(out=scr[:, g % 2, 0:seq], in0=wins[g][:, s0:s0 + seq], scalar=1.0 / w,
                                              in1=zu[:, g, HIST:SU], op0=ALU.mult, op1=ALU.subtract))
                ends = zu[:, g, SU:].rearrange("p (s r) -> p s r", r=HIST + 1)[:, :, HIST]
                at_ = SU + HIST + 1 - w
                wv = wins[g][:, at_:at_ + (HIST + 1) * (dec - 1) + 1:HIST + 1]
                dve.scalar_tensor_tensor(out=scr[:, g % 2, seq:T], in0=wv, scalar=1.0 / w, in1=ends,
                                         op0=ALU.mult, op1=ALU.subtract).then_inc(diff_done, 1)

            def diff_low(l, g):
                dve.wait_ge(diff_hi, GB * l + g + 1)
                dve.tensor_tensor(diff[:, 1, g, :], scr[:, g % 2, 0:T], diff[:, 0, g, :].bitcast(F32), ALU.subtract)\
                    .then_inc(diff_lo, 1)

            def convolve(l, b):
                n = ZV - 2
                w = [pcol(CONV + (3 * l + k) * GB + b) for k in range(3)]
                link(dve.tensor_scalar(scr[:, 0, :], zv[:, b, 0:n], w[0], None, ALU.mult))
                link(dve.scalar_tensor_tensor(out=scr[:, 1, :], in0=zv[:, b, 1:n + 1], scalar=w[1],
                                              in1=scr[:, 0, :], op0=ALU.mult, op1=ALU.add))
                dve.scalar_tensor_tensor(out=conv[:, b, 0:seq], in0=zv[:, b, 2:seq + 2], scalar=w[2],
                                         in1=scr[:, 1, 0:seq], op0=ALU.mult, op1=ALU.add).then_inc(dve_step, 1)
                steps[0] += 1
                ends = slice(SV, SV + 3 * (dec - 1) + 1, 3)
                link(dve.scalar_tensor_tensor(out=conv[:, b, seq:T], in0=zv[:, b, SV + 2:SV + 3 * dec:3], scalar=w[2],
                                              in1=scr[:, 1, ends], op0=ALU.mult, op1=ALU.add))

            def mix_inverse(l, half):
                dve.wait_ge(sq_used, 2 * GB * l + GB * (half + 1))
                link(dve.tensor_scalar(msq[:, half, :], ps[:, 4, 0:T], 1.0 / (GB * P), EPS, ALU.mult, ALU.add))
                dve.reciprocal(msq[:, half, :], msq[:, half, :]).then_inc(mix_inv, 1)

            def mix_scale(l, half):
                y = conv if half else y_pool
                dve.wait_ge(mix_rstd, 2 * l + half + 1)
                rb = msq[:, half, :].unsqueeze(1).to_broadcast([P, GB, T])
                dve.tensor_tensor(y, y, rb, ALU.mult).then_inc(m_f, 1)

            def mix_low(l, half):
                y = conv if half else y_pool
                g, k0 = (GCO, 0) if half else (GPO, GB)
                dve.wait_ge(m_hi, 2 * l + half + 1)
                for b in range(GB):
                    ins = dve.scalar_tensor_tensor(out=m_lo_t[:, k0 + b, :], in0=y[:, b, :],
                                                   scalar=pcol(g + GB * l + b),
                                                   in1=m_hi_t[:, k0 + b, :].bitcast(F32),
                                                   op0=ALU.mult, op1=ALU.subtract)
                ins.then_inc(m_lo, 1)

            def phase_in(l, phase, following, late=()):
                for i, ch in enumerate(phase):
                    if SPLIT_SLOTS <= i < 7:
                        lo_of(ch)
                    if i == SPLIT_SLOTS + 1:
                        ada_pairs(late)
                    if i >= SPLIT_SLOTS:
                        take(phase[i - SPLIT_SLOTS])
                    if i >= 7:
                        lo_of(ch)
                    if i == 4:
                        window_sums(l)
                    if i in (5, 6):
                        g0 = 2 * (i - 5)
                        for g in (g0, g0 + 1):
                            window_diff(l, g)
                        for g in (g0, g0 + 1):
                            diff_low(l, g)
                    if i in (7, 8):
                        dve.wait_ge(dve_took, count_of("in", l, 2 * GB + 2 * (i - 7) + 1))
                        for b in ([0] if i == 7 else range(1, GB)):
                            convolve(l, b)
                take(phase[7])
                lo_of(following[0])
                dve.wait_ge(act_took, count_of("pool", l, GB - 1))
                mix_inverse(l, 0)
                mix_scale(l, 0)
                take(phase[8])
                mix_low(l, 0)
                lo_of(following[1])
                dve.wait_ge(dve_took, count_of("in", l, GB - 1))
                mix_inverse(l, 1)
                mix_scale(l, 1)
                lo_of(following[2])
                mix_low(l, 1)

            def phase_rest(phase, following, late=()):
                for i, ch in enumerate(phase):
                    if i >= SPLIT_SLOTS:
                        lo_of(ch)
                        take(phase[i - SPLIT_SLOTS])
                    if i == SPLIT_SLOTS:
                        ada_pairs(late)
                if following:
                    lo_of(following[0])
                for ch in phase[-SPLIT_SLOTS:]:
                    take(ch)
                if following:
                    lo_of(following[1])
                dve.wait_ge(dve_took, blocks[phase[-1]["blocks"][-1]]["count"])

            lo_of(phases[0][0])
            norm_start(0)
            lo_of(phases[0][1])
            lo_of(phases[0][2])
            dve.wait_ge(par_done, 2)
            ada_pairs(fillers[0][:-2])
            norm_half(0, 0)
            norm_low(0, 0)
            ada_pairs(fillers[0][-2:])
            norm_half(0, 1)
            norm_low(0, 1)
            put_states(0)
            phase_in(0, phases[0], phases[1])
            ada_pairs(fillers[1])
            phase_rest(phases[1], phases[2])
            norm_start(1)
            lo_of(phases[2][2])
            ada_pairs(fillers[2][:2])
            norm_half(1, 0)
            norm_low(1, 0)
            ada_pairs(fillers[2][2:])
            norm_half(1, 1)
            norm_low(1, 1)
            phase_rest(phases[2], phases[3])
            norm_start(2)
            norm_end(2)
            ada_pairs(fillers[3][:2])
            put_states(1)
            lo_of(phases[3][2])
            phase_in(1, phases[3], phases[4], fillers[3][2:])
            phase_rest(phases[4], None, fillers[4])
            norm_start(3)
            norm_end(3)

            for k in range(SPLIT_SLOTS):
                lo(M0 + k, (M0 + k) % 6)

            dve.wait_ge(tok_zero, 1)
            dve.wait_ge(logits_turned, 1)
            for j in range(TT):
                rows = LAST if j == TT - 1 else P
                link(dve.tensor_copy(logit[0:rows, j, :], ps[0:rows, 5, E * j:E * (j + 1)]))
            shape = [P, TT, E, E]
            mine = logit.unsqueeze(3).to_broadcast(shape)
            other = logit.unsqueeze(2).to_broadcast(shape)
            link(dve.tensor_tensor(cmp1, other, mine, ALU.is_gt))
            link(dve.tensor_tensor(cmp2, other, mine, ALU.is_equal))
            link(dve.tensor_tensor(cmp2, cmp2, earlier.unsqueeze(1).to_broadcast(shape), ALU.mult))
            link(dve.tensor_tensor(cmp1, cmp1, cmp2, ALU.add))
            link(dve.tensor_reduce(rank, cmp1, axis=AX_X, op=ALU.add))
            link(dve.tensor_scalar(chosen, rank, 2.0, None, ALU.is_lt))
            dve.tensor_tensor(chosen, chosen, real.unsqueeze(2).to_broadcast([P, TT, E]), ALU.mult)\
                .then_inc(chosen_done, 1)
            link(dve.tensor_reduce(lmax, logit, axis=AX_X, op=ALU.max))
            dve.tensor_tensor(logit, logit, lmax.unsqueeze(2).to_broadcast([P, TT, E]), ALU.subtract)\
                .then_inc(route_max, 1)
            dve.wait_ge(chosen_done, 1)
            dve.wait_ge(cum_ps, 1)
            before = ps[:, 5, 0:TT * E].rearrange("p (j e) -> p j e", j=TT)
            place_j = place.rearrange("p e j -> p j e")
            link(dve.tensor_scalar(place_j, before, 1000.0, None, ALU.add))
            link(dve.tensor_tensor(place_j, place_j, chosen, ALU.mult))
            link(dve.tensor_scalar(place_j, place_j, -1000.0, None, ALU.add))

            def fill_sel(places, experts=2):
                dve.wait_ge(place_made, places)
                for h in range(experts):
                    for j in range(TT):
                        dve.tensor_scalar(sel[:, j, P * h:P * (h + 1)], slot_no[:, :], place_e[:, h, j:j + 1], None,
                                          ALU.is_equal).then_inc(sel_made, 1)

            dve.tensor_copy(place_e, place[:, 0:2, :]).then_inc(place_made, 1)
            fill_sel(1)
            dve.wait_ge(route_max, 1)
            dve.wait_ge(route_exp, 1)
            link(dve.tensor_tensor(logit, rank, chosen, ALU.mult))
            link(dve.tensor_reduce(lsum, logit, axis=AX_X, op=ALU.add))
            link(dve.tensor_scalar(lsum, lsum, 1e-30, None, ALU.max))
            link(dve.reciprocal(lsum, lsum))
            link(dve.tensor_tensor(gate.rearrange("p e j -> p j e"), logit,
                                   lsum.unsqueeze(2).to_broadcast([P, TT, E]), ALU.mult))
            dve.tensor_copy(gate_e, gate[:, 0:2, :]).then_inc(place_made, 1)
            count = ps[:, 5, TT * E:(TT + 1) * E]
            for j in range(TT - 1):
                link(dve.tensor_scalar(more[:, j, :], count, float(P * (j + 1)), None, ALU.is_gt))
            cur, nxt, d = more_row, more_no, 1
            link(dve.tensor_copy(tmp_row, more_row))
            cur = tmp_row
            while d < NX:
                link(dve.tensor_copy(nxt[:, 0:d], cur[:, 0:d]))
                link(dve.tensor_tensor(nxt[:, d:NX], cur[:, d:NX], cur[:, 0:NX - d], ALU.add))
                cur, nxt = nxt, cur
                d *= 2
            want = slot_no[:, 1:EXTRA + 1].unsqueeze(2).to_broadcast([P, EXTRA, NX])
            link(dve.tensor_tensor(hit, cur.unsqueeze(1).to_broadcast([P, EXTRA, NX]), want, ALU.is_equal))
            link(dve.tensor_tensor(hit, hit, more_row.unsqueeze(1).to_broadcast([P, EXTRA, NX]), ALU.mult))
            link(dve.tensor_tensor(hit2, hit, code_s.unsqueeze(1).to_broadcast([P, EXTRA, NX]), ALU.mult))
            link(dve.tensor_reduce(extra_shift, hit2, axis=AX_X, op=ALU.add))
            link(dve.tensor_tensor(hit2, hit, code_e.unsqueeze(1).to_broadcast([P, EXTRA, NX]), ALU.mult))
            link(dve.tensor_reduce(extra_f[:, 0:EXTRA], hit2, axis=AX_X, op=ALU.add))
            link(dve.tensor_copy(extra_f[:, EXTRA:EXTRA + 1], cur[:, NX - 1:NX]))
            dve.tensor_copy(extra_i[:, :], extra_f).then_inc(extra_done, 1)

            def make_sel(readers, gathers, first, n):
                dve.wait_ge(selT_done, readers)
                dve.wait_ge(gather_ps, gathers)
                dve.tensor_copy(place_e[:, 0:n, :], place[:, bass.ds(first, n), :]).then_inc(place_made, 1)
                dve.tensor_copy(gate_e[:, 0:n, :], gate[:, bass.ds(first, n), :]).then_inc(place_made, 1)

            def hidden(q, bank):
                dve.wait_ge(e_silu_done, q + 1)
                dve.wait_ge(e_turned, q)
                dve.tensor_tensor(e_hid, ps[:, bank + 1, :], e_silu, ALU.mult).then_inc(e_hid_done, 1)

            def split_hidden(q, bank):
                dve.wait_ge(e_hi_done, q + 1)
                dve.tensor_tensor(eh_lo, ps[:, bank, :].rearrange("p (k s) -> p k s", k=GC),
                                  eh_hi.bitcast(F32), ALU.subtract).then_inc(e_lo_done, 1)

            def split_y(e):
                for half in range(HALVES):
                    cs = half_of(half)
                    dve.wait_ge(y_hi_done, HALVES * e + half + 1)
                    dve.tensor_tensor(y_lo[:, cs, :], y_f_blocks[:, cs, :], y_hi[:, cs, :].bitcast(F32),
                                      ALU.subtract).then_inc(y_lo_done, 1)

            def combine(e, banks):
                for c in range(KC):
                    dve.wait_ge(comb_ps, KC * e + c + 1)
                    dve.tensor_tensor(acc[:, c, :], acc[:, c, :], ps[:, banks[c % 2], 0:T], ALU.add)\
                        .then_inc(combined, 1)
                dve.wait_ge(combined, KC * (e + 1))

            plan = misc_plan()

            def expert(e, first, sel_for=None):
                for pos, kind, g in expert_chunks(first):
                    n, s = chunk_no(e, pos, first), slot_of(pos, first)
                    if pos == 0 and not first:
                        hidden(GROUPS * e - 1, (GROUPS - 1) % 2 * 2)
                    if not (first and pos < SPLIT_SLOTS):
                        lo(n, s)
                    if pos % 6 == 0 and pos:
                        hidden(GROUPS * e + g - 1, (g - 1) % GROUPS % 2 * 2)
                    if pos % 6 == 3 and (pos > 3 or not first):
                        split_hidden(GROUPS * e + g - 1, plan["hid", (g - 1) % GROUPS])
                    if pos == 8 and not first:
                        split_y(e - 1)
                    if pos == 10 and not first:
                        combine(e - 1, plan["comb"])
                    if pos == 18 and sel_for is not None:
                        make_sel(4 * sel_for, 8 * sel_for, 2 * sel_for, 2)
                        fill_sel(2 * sel_for + 2)

            ada_pairs(fillers[5])
            dve.wait_ge(acc_zero, 1)
            expert(0, True)
            expert(1, False, 1)
            with dve.Fori(1, n_exp // 2 - 1) as pair:
                expert(2 * pair, False)
                expert(2 * pair + 1, False, pair + 1)
            expert(n_exp - 2, False)
            expert(n_exp - 1, False)
            for q in range(2):
                n = M1 - 2 + q
                lo(n, n % 6)
                if q == 0:
                    hidden(n_exp * GROUPS - 1, (GROUPS - 1) % 2 * 2)
            split_hidden(n_exp * GROUPS - 1, plan["hid", GROUPS - 1])
            split_y(n_exp - 1)
            combine(n_exp - 1, (6, 7))

            dve.wait_ge(extra_done, 1)
            many = dve.value_load(extra_i[0:1, EXTRA:EXTRA + 1], min_val=0, max_val=EXTRA)
            with dve.If(many > 0):
                with dve.Fori(0, many) as i:
                    e = dve.value_load(extra_i[0:1, bass.ds(i, 1)], min_val=0, max_val=n_exp - 1)
                    k = n_exp + i
                    make_sel(2 * k, 8 * (n_exp // 2 + i), e, 1)
                    dve.wait_ge(place_made, n_exp + 3 * i + 2)
                    dve.tensor_scalar(place_e[:, 0, :], place_e[:, 0, :], extra_shift[:, bass.ds(i, 1)], None,
                                      ALU.subtract).then_inc(place_made, 1)
                    fill_sel(n_exp + 3 * i + 3, 1)
                    for pos in range(PER_EXPERT):
                        g, q = divmod(pos, 6)
                        lo(M1 + PER_EXPERT * i + pos, (M1 + pos) % 6)
                        if q == 5:
                            hidden(GROUPS * k + g, 0)
                            split_hidden(GROUPS * k + g, 6)
                    split_y(k)
                    combine(k, (6, 7))

            dve.wait_ge(combined, KC * n_exp)
            gate_2 = mod(depth - 1, GT2)
            link(dve.tensor_tensor(acc[:, :, seq:T], acc[:, :, seq:T], gate_2[:, :, 1:S], ALU.mult))
            link(dve.tensor_tensor(xT[:, :, seq:T], xT[:, :, seq:T], acc[:, :, seq:T], ALU.add))
            for c in range(KC):
                dve.scalar_tensor_tensor(out=xT[:, c, 0:seq], in0=acc[:, c, 0:seq], scalar=gate_2[:, c, 0:1],
                                         in1=xT[:, c, 0:seq], op0=ALU.mult, op1=ALU.add).then_inc(x_last, 1)
            dve.wait_ge(x_last, KC)
            dve.wait_ge(sums, n_norms)
            link(dve.tensor_scalar(var, ps[:, 4, 0:T], 1.0 / d_model, EPS, ALU.mult, ALU.add))
            dve.reciprocal(var, var).then_inc(inv_var, 1)
            dve.wait_ge(rstd_done, n_norms)
            for c in range(KC):
                dve.scalar_tensor_tensor(out=hn[:, c, :], in0=xT[:, c, :], scalar=pcol(G_FIN + c), in1=rstd,
                                         op0=ALU.mult, op1=ALU.mult).then_inc(fin_f, 1)

        @block.tensor
        def _(pe):
            pe.wait_ge(consts, 2)
            pe.wait_ge(c_silu, 1)
            for k in range(KC):
                ins = pe.transpose(ps[:, 4, k * S:(k + 1) * S], c_rows[0:S, k * P:(k + 1) * P], ident[0:S, 0:S])
            ins.then_inc(turned, 1)
            pe.wait_ge(x_in, 32)
            for c in range(KC):
                if c >= 4:
                    pe.wait_ge(turned_out, c - 3)
                for j in range(TT):
                    rows = LAST if j == TT - 1 else P
                    ins = pe.transpose(ps[:, c % 4, j * P:j * P + rows], x_rows[0:rows, j, c * P:(c + 1) * P],
                                       ident[0:rows, 0:rows])
                ins.then_inc(turned, 1)
            bank5_read = (par_done, 2)

            def bank5(event):
                nonlocal bank5_read
                pe.wait_ge(*bank5_read)
                bank5_read = event

            def turn_states(l):
                pe.wait_ge(states_in[l], 32)
                bank5((state_put, 2 * (l + 1)))
                pe.wait_ge(inv_var, 2 * l + 1)
                for b in range(GB):
                    n = dec * HIST
                    ins = pe.transpose(ps[:, 5, b * n:(b + 1) * n], pool_rows[0:n, b * P:(b + 1) * P],
                                       ident[0:n, 0:n])
                ins.then_inc(state_turned, 1)
                for b in range(GB):
                    n = dec * 2
                    ins = pe.transpose(ps[:, 4, b * n:(b + 1) * n], conv_rows[0:n, b * P:(b + 1) * P],
                                       ident[0:n, 0:n])
                ins.then_inc(state_turned, 1)

            def ada_bank(ch):
                k = ch["a"] // 2
                if k >= 2:
                    pe.wait_ge(ada_copied, k - 1)
                return ps[:, 6 + k % 2, 256 * (ch["a"] % 2):256 * (ch["a"] % 2 + 1)]

            def ada_product(ch):
                n = ch["n"]
                pe.wait_ge(raw_in[n % RAW_SLOTS], 16 * (n // RAW_SLOTS + 1))
                out = ada_bank(ch)[0:S, :]
                for k in range(KC):
                    ins = pe.matmul(out, silu_c[:, k, :], raw[:, n % RAW_SLOTS, 256 * k:256 * (k + 1)],
                                    start=(k == 0), stop=(k == KC - 1))
                ins.then_inc(ada_used, 1)

            def ada_split_product(ch):
                s = ch["m"] % SPLIT_SLOTS
                pe.wait_ge(c_lo, 1)
                out = ada_bank(ch)[0:2 * S, :]
                for k in range(KC):
                    w = slice(256 * k, 256 * (k + 1))
                    pe.matmul(out, silu_parts[:, k, :], w_hi[:, s, w], start=(k == 0), stop=False)
                    ins = pe.matmul(out, silu_parts[:, k, :], w_lo[:, s, w], start=False, stop=(k == KC - 1))
                ins.then_inc(used, 1)

            def ada_turn(odd):
                k = odd["a"] // 2
                pe.wait_ge(ada_copied, k + 1)
                bank5((ada_out, k + 1))
                for b in range(4):
                    out, cols = ps[:, 5, S * b:S * (b + 1)], slice(P * b, P * (b + 1))
                    if "u" in odd:
                        ins = pe.transpose(out, ada_rows[0:S, cols], ident[0:S, 0:S])
                    else:
                        ins = pe.matmul(out, ada_rows[:, cols], twice[:, :], start=True, stop=True)
                ins.then_inc(ada_turned, 1)

            def fill(chunks, done=0):
                waiting = None
                for i, ch in enumerate(chunks):
                    if i >= done:
                        ada_product(ch)
                    if waiting is not None:
                        ada_turn(waiting)
                    waiting = ch if ch["a"] % 2 else None
                ada_turn(waiting)

            def norm_sums(k):
                if k == 0:
                    pe.wait_ge(c_done, 1)
                elif k == n_norms - 1:
                    pe.wait_ge(logits_row, 1)
                elif k % 2:
                    pe.wait_ge(mix_inv, k + 1)
                else:
                    pe.wait_ge(inv_var, k)
                for c in range(KC):
                    pe.wait_ge(squares, KC * k + c + 1)
                    ins = pe.matmul(ps[:, 4, 0:T], ones[:, :], sq[:, c, :], start=(c == 0), stop=(c == KC - 1))
                ins.then_inc(sums, 1)

            def mix_sums(l, half):
                if half == 0:
                    pe.wait_ge(state_put, 2 * (l + 1))
                else:
                    pe.wait_ge(mix_inv, 2 * l + 1)
                for b in range(GB):
                    pe.wait_ge(mix_sq, 2 * GB * l + GB * half + b + 1)
                    pe.matmul(ps[:, 4, 0:T], ones[:, :], mix_squares[:, b % 2, :], start=(b == 0),
                              stop=(b == GB - 1)).then_inc(sq_used, 1)

            def turn_tails(l):
                pe.wait_ge(tails, 4 * (l + 1))
                bank5((tails_out, l + 1))
                for b in range(GB):
                    ins = pe.transpose(ps[0:ROWS, 5, b * P:(b + 1) * P], last_rows[:, b, :], ident[:, :])
                ins.then_inc(tails_turned, 1)

            def bank_free(b):
                if b >= 4:
                    old = blocks[b - 4]
                    pe.wait_ge(act_took if old["eng"] == "act" else dve_took, old["count"])
                else:
                    pe.wait_ge(turned_out, KC)

            def product(ch):
                s, l, kind = ch["m"] % SPLIT_SLOTS, ch["layer"], ch["kind"]
                x_hi, x_lo = {"down": (hid_hi, hid_lo), "out": (m_hi_t, m_lo_t)}.get(kind, (h_hi, h_lo))
                pe.wait_ge(lo_done, ch["m"] + 1)
                if kind == "ada":
                    ada_split_product(ch)
                    return
                if kind == "down":
                    pe.wait_ge(ffn_lo, min(FC, ch["k0"] + ch["nk"]))
                for b, blk in enumerate(ch["blocks"]):
                    if ch["first"]:
                        bank_free(blk)
                    out = ps[:, blk % 4, 0:T]
                    if kind == "pool":
                        w = slice(P * b, P * (b + 1))
                        pe.wait_ge(diff_lo, GB * l + b + 1)
                        pe.matmul(out, w_hi[:, s, w], diff[:, 0, b, :], start=True, stop=False)
                        pe.matmul(out, w_hi[:, s, w], diff[:, 1, b, :], start=False, stop=False)
                        ins = pe.matmul(out, w_lo[:, s, w], diff[:, 0, b, :], start=False, stop=True)
                        continue
                    order = [(k + GB) % KC for k in range(KC)] if kind == "out" else list(range(ch["nk"]))
                    for i, k in enumerate(order):
                        if i % GB == 0 and kind == "out":
                            pe.wait_ge(m_lo, 2 * l + 1 + i // GB)
                        if i % GB == 0 and kind in ("in", "gate", "up"):
                            pe.wait_ge(h_lo_done, NORM_H * (2 * l + (kind != "in")) + 1 + i // GB)
                        w = slice(256 * k + P * b, 256 * k + P * (b + 1))
                        kk = ch["k0"] + k
                        pe.matmul(out, w_hi[:, s, w], x_hi[:, kk, :], start=ch["first"] and i == 0, stop=False)
                        pe.matmul(out, w_hi[:, s, w], x_lo[:, kk, :], start=False, stop=False)
                        ins = pe.matmul(out, w_lo[:, s, w], x_hi[:, kk, :], start=False,
                                        stop=ch["last"] and i == ch["nk"] - 1)
                ins.then_inc(used, 1)

            def phase_in(l, phase, next_fill, late=()):
                for i, ch in enumerate(phase):
                    product(ch)
                    if i == 1:
                        for odd in late[1::2]:
                            ada_turn(odd)
                    if i == 7:
                        mix_sums(l, 0)
                ada_product(next_fill[0])
                mix_sums(l, 1)

            def phase_rest(phase, late=None):
                waiting = [late, None]
                for ch in phase:
                    product(ch)
                    odd = waiting.pop(0)
                    if odd is not None:
                        ada_turn(odd)
                    waiting.append(ch if ch["kind"] == "ada" and ch["a"] % 2 else None)
                assert waiting == [None, None]

            norm_sums(0)
            n0 = depth * ADA_PARTS * KC
            pe.wait_ge(par_in, 16 * 8)
            pe.transpose(ps[:, 5, 0:n0], par_rows[0:n0, 0, :], ident[0:n0, 0:n0]).then_inc(turned, 1)
            pe.transpose(ps[:, 5, n0:184], par_rows[0:184 - n0, 1, :], ident[0:184 - n0, 0:184 - n0])\
                .then_inc(turned, 1)
            fill(fillers[0])
            turn_states(0)
            phase_in(0, phases[0], fillers[1])
            fill(fillers[1], 1)
            turn_tails(0)
            phase_rest(phases[1])
            norm_sums(1)
            fill(fillers[2])
            phase_rest(phases[2])
            norm_sums(2)
            for ch in fillers[3]:
                ada_product(ch)
            ada_turn(fillers[3][1])
            turn_states(1)
            phase_in(1, phases[3], fillers[4], fillers[3][2:])
            turn_tails(1)
            ada_product(fillers[4][1])
            phase_rest(phases[4], fillers[4][1])
            norm_sums(3)
            for ch in fillers[5]:
                ada_product(ch)

            pe.wait_ge(router_in, 16)
            pe.wait_ge(normed, NORM_H * 4)
            pe.wait_ge(inv_var, 4)
            for k in range(KC):
                ins = pe.matmul(ps[0:E, 4, 0:T], router[:, k, :], hn[:, k, :], start=(k == 0), stop=(k == KC - 1))
            ins.then_inc(logits_ps, 1)
            pe.wait_ge(logits_row, 1)
            bank5((chosen_done, 1))
            for j in range(TT):
                rows = LAST if j == TT - 1 else P
                ins = pe.transpose(ps[0:rows, 5, E * j:E * (j + 1)], logitT[:, j * P:j * P + rows], ident[0:E, 0:E])
            ins.then_inc(logits_turned, 1)

            def turn_tokens(s0, s1):
                for s in range(s0, s1):
                    j, part_no, half = s // 4, s // 2 % 2, s % 2
                    rows = LAST if j == TT - 1 else P
                    if s >= 4:
                        pe.wait_ge(tok_copied, s - 3)
                    src = (h_hi if part_no == 0 else h_lo)
                    for c in range(4):
                        ins = pe.transpose(ps[0:rows, s % 4, c * P:(c + 1) * P],
                                           src[:, 4 * half + c, j * P:j * P + rows].bitcast(F32), ident[:, :])
                    ins.then_inc(tok_turned, 1)

            pe.wait_ge(h_lo_done, NORM_H * 4)
            turn_tokens(0, 6)
            bank5((extra_done, 1))
            for j in range(TT + 1):
                out = ps[:, 5, E * j:E * (j + 1)]
                for i in range(min(j + 1, TT)):
                    ins = pe.matmul(out, tri[:, :] if i == j else ones[:, :], chosen[:, i, :], start=(i == 0),
                                    stop=(i == min(j, TT - 1)))
            ins.then_inc(cum_ps, 1)
            turn_tokens(6, 4 * TT)
            pe.wait_ge(tok_copied, 4 * TT)

            free = {6: None, 7: None}

            def bank(b):
                if free[b] is not None:
                    pe.wait_ge(*free[b])

            def gather(k, s0, s1, made, width=2 * P):
                pe.wait_ge(sel_made, made)
                for s in range(s0, s1):
                    b = 6 + s % 2
                    bank(b)
                    src = tok_hi if s < 4 else tok_lo
                    for c in range(2):
                        cc = 2 * (s % 4) + c
                        for j in range(TT):
                            ins = pe.matmul(ps[:, b, 2 * P * c:2 * P * c + width], src[:, j, cc * P:(cc + 1) * P],
                                            sel[:, j, 0:width], start=(j == 0), stop=(j == TT - 1))
                    ins.then_inc(gather_ps, 1)
                    free[b] = (gathered, 8 * k + s + 1)

            def turn_sel(k, b, h, made):
                bank(b)
                pe.wait_ge(place_made, made)
                cols = slice(P * h, P * (h + 1))
                for j in range(TT):
                    rows = LAST if j == TT - 1 else P
                    pe.transpose(ps[:, b, j * P:j * P + rows], sel[0:rows, j, cols].bitcast(F32),
                                 ident[0:rows, 0:rows])
                for j in range(TT):
                    ins = pe.matmul(ps[:, b, T:T + 1], sel[:, j, cols].bitcast(F32), gate_e[:, h, j:j + 1],
                                    start=(j == 0), stop=(j == TT - 1))
                ins.then_inc(selT_ps, 1)
                free[b] = (selT_done, 2 * (k + 1))

            def gate_up(n, s, c, b, groups_read, h):
                pe.wait_ge(lo_done, n + 1)
                if c == 0 and groups_read is not None:
                    pe.wait_ge(e_hid_done, groups_read)
                out = ps[:, b + c // 2, :]
                for k in range(4):
                    kk = 4 * (c % 2) + k
                    wv = slice(BANK * k, BANK * (k + 1))
                    pe.matmul(out, xs_hi[:, kk, P * h:P * (h + 1)], w_hi[:, s, wv], start=(kk == 0), stop=False)
                    pe.matmul(out, xs_hi[:, kk, P * h:P * (h + 1)], w_lo[:, s, wv], start=False, stop=False)
                    ins = pe.matmul(out, xs_lo[:, kk, P * h:P * (h + 1)], w_hi[:, s, wv], start=False, stop=(kk == KC - 1))
                ins.then_inc(used, 1)

            def turn_hidden(q, b):
                pe.wait_ge(e_hid_done, q + 1)
                bank(b)
                for k in range(GC):
                    ins = pe.transpose(ps[:, b, k * P:(k + 1) * P], e_hid[:, k * P:(k + 1) * P], ident[:, :])
                ins.then_inc(e_turned, 1)
                free[b] = (e_lo_done, q + 1)

            def down(n, s, q, e, g, c):
                pe.wait_ge(lo_done, n + 1)
                if c == 0:
                    pe.wait_ge(e_lo_done, q + 1)
                    if g == 0:
                        pe.wait_ge(y_scaled, HALVES * e)
                for k in range(2):
                    kk = 2 * c + k
                    first, last = g == 0 and kk == 0, g == GROUPS - 1 and kk == GC - 1
                    for half in range(HALVES):
                        out = ps[:, 4 + half, :]
                        wv = slice(d_model * k + half * BANK, d_model * k + (half + 1) * BANK)
                        pe.matmul(out, eh_hi[:, kk, :], w_hi[:, s, wv], start=first, stop=False)
                        pe.matmul(out, eh_hi[:, kk, :], w_lo[:, s, wv], start=False, stop=False)
                        ins = pe.matmul(out, eh_lo[:, kk, :], w_hi[:, s, wv], start=False, stop=last)
                ins.then_inc(used, 1)

            def combine(e, banks):
                for c in range(KC):
                    if c % (KC // HALVES) == 0:
                        pe.wait_ge(y_lo_done, HALVES * e + c // (KC // HALVES) + 1)
                    b = banks[c % 2]
                    bank(b)
                    out = ps[:, b, 0:T]
                    pe.matmul(out, y_hi[:, c, :], selT, start=True, stop=False)
                    pe.matmul(out, y_lo[:, c, :], selT, start=False, stop=True).then_inc(comb_ps, 1)
                    free[b] = (combined, KC * e + c + 1)

            plan = misc_plan()

            def expert(e, first, pair, h, gather_next=False):
                for pos, kind, g in expert_chunks(first):
                    n, s = chunk_no(e, pos, first), slot_of(pos, first) % SPLIT_SLOTS
                    q = pos % 6
                    if q == 1 and (g or not first):
                        turn_hidden(GROUPS * e + g - 1, plan["hid", (g - 1) % GROUPS])
                    if kind == "gu":
                        if pos == 0 and h == 0:
                            pe.wait_ge(gathered, 8 * (pair + 1))
                        read = GROUPS * e + g - (1 if g else 0)
                        gate_up(n, s, q, g % 2 * 2, None if first and g < 2 else read, h)
                    elif g == 0:
                        down(n, s, GROUPS * e - 1, e - 1, GROUPS - 1, q - 4)
                    else:
                        down(n, s, GROUPS * e + g - 1, e, g - 1, q - 4)
                    if pos == 9:
                        if not first:
                            combine(e - 1, plan["comb"])
                        turn_sel(e, plan["selT"], h, 2 * (pair + 1))
                    if pos >= PER_EXPERT - 2 and gather_next:
                        s0 = 4 * (pos - PER_EXPERT + 2)
                        gather(pair + 1, s0, s0 + 4, 2 * TT * (pair + 2))

            def experts(pair, first=False, last=False):
                for b in (6, 7):
                    free[b] = (gathered, 8 * pair + b + 1)
                expert(2 * pair, first, pair, 0)
                expert(2 * pair + 1, False, pair, 1, not last)

            pe.wait_ge(ada_copied, N_ADA // 2)
            gather(0, 0, 8, 2 * TT)
            ada_turn(fillers[5][1])
            experts(0, first=True)
            with pe.Fori(1, n_exp // 2 - 1) as pair:
                experts(pair)
            experts(n_exp // 2 - 1, last=True)
            q = n_exp * GROUPS - 1
            turn_hidden(q, plan["hid", GROUPS - 1])
            for c in range(2):
                n = M1 - 2 + c
                down(n, n % SPLIT_SLOTS, q, n_exp - 1, GROUPS - 1, c)
            combine(n_exp - 1, (6, 7))

            many = pe.value_load(extra_i[0:1, EXTRA:EXTRA + 1], min_val=0, max_val=EXTRA)
            with pe.If(many > 0):
                with pe.Fori(0, many) as i:
                    k = n_exp + i
                    pe.wait_ge(combined, KC * k)
                    free[6] = free[7] = None
                    pe.wait_ge(sel_made, TT * (k + 1))
                    turn_sel(k, 7, 0, n_exp + 3 * i + 3)
                    gather(n_exp // 2 + i, 0, 8, TT * (k + 1), P)
                    pe.wait_ge(gathered, 8 * (n_exp // 2 + i + 1))
                    for g in range(GROUPS):
                        q = GROUPS * k + g
                        for c in range(4):
                            n = M1 + PER_EXPERT * i + 6 * g + c
                            gate_up(n, (M1 + 6 * g + c) % SPLIT_SLOTS, c, 0, q, 0)
                        free[6] = None
                        if g:
                            pe.wait_ge(e_lo_done, q)
                        turn_hidden(q, 6)
                        for c in range(2):
                            n = M1 + PER_EXPERT * i + 6 * g + 4 + c
                            down(n, (M1 + 6 * g + 4 + c) % SPLIT_SLOTS, q, k, g, c)
                    free[6] = free[7] = None
                    combine(k, (6, 7))

            norm_sums(n_norms - 1)
            for s in range(2 * TT):
                half, j = divmod(s, TT)
                pe.wait_ge(fin_f, 4 * (half + 1))
                rows = LAST if j == TT - 1 else P
                for c in range(4):
                    ins = pe.transpose(ps[0:rows, s, c * P:(c + 1) * P], hn[:, 4 * half + c, j * P:j * P + rows],
                                       ident[:, :])
                ins.then_inc(fin_ps, 1)



_INS = ["x_prompt", "x_sample", "c_prompt", "c_sample", "state_conv", "state_pool", "w_ada", "b_ada", "g_mix",
        "g_ffn", "w_in", "conv_w", "pool_w", "pool_scale", "g_conv_out", "g_pool_out", "w_out", "dense_w_gate",
        "dense_w_up", "dense_w_down", "router_w", "moe_w_gate", "moe_w_up", "moe_w_down", "g_final"]


def kernel(**inputs):
    import numpy as _np
    import concourse.bacc as _bacc
    from concourse import mybir as _mybir
    from concourse.bass_utils import run_bass_kernel_spmd as _run

    nc = _bacc.Bacc("TRN2", target_bir_lowering=False, num_devices=1)
    arrays, a, o = {}, {}, {}
    for name in _INS:
        v = _np.ascontiguousarray(inputs[name])
        arrays[f"in_{name}_dram"] = v
        a[name] = nc.dram_tensor(f"in_{name}_dram", v.shape, _mybir.dt.from_np(v.dtype), kind="ExternalInput").ap()
    outs = {
        "y_prompt": inputs["x_prompt"].shape, "y_sample": inputs["x_sample"].shape,
        "conv_prompt": (inputs["state_conv"].shape[0], inputs["x_prompt"].shape[0]) + inputs["state_conv"].shape[2:],
        "pool_prompt": (inputs["state_pool"].shape[0], inputs["x_prompt"].shape[0]) + inputs["state_pool"].shape[2:],
        "conv_sample": inputs["state_conv"].shape, "pool_sample": inputs["state_pool"].shape,
    }
    for name, shape in outs.items():
        o[name] = nc.dram_tensor(f"out_{name}_dram", tuple(shape), _mybir.dt.float32, kind="ExternalOutput").ap()
    hybrid_trunk(nc, a, o)
    r = _run(nc, [arrays], core_ids=[0])
    return tuple(r.results[0][f"out_{name}_dram"] for name in outs)
```
